# Optimizing a Trainium2 kernel written in Bass

```python
import math
import jax, jax.numpy as jnp
from jax import lax
import numpy as np

D_MODEL = 1024
BATCH = 1
SEQ = 1024
DEPTH = 2

N_A = max(1, DEPTH // 2)
N_B = DEPTH - N_A
D_CONV = D_MODEL
CONV_K = 3
N_HEADS = 16
HEAD_DIM = D_MODEL // N_HEADS
D_ATTN = N_HEADS * HEAD_DIM
Q_BLOCK = 128
EPS = 1e-6


def rmsnorm(x, g):
    xf = x.astype(jnp.float32)
    y = xf * lax.rsqrt(jnp.mean(xf * xf, axis=-1, keepdims=True) + EPS)
    return (y * g.astype(jnp.float32)).astype(x.dtype)

def modulation(c, w, b, n):
    m = jax.nn.silu(c) @ w + b
    return jnp.split(m, n, axis=-1)

def modulated_norm(x, g, shift, scale):
    return rmsnorm(x, g) * (1.0 + scale[:, None, :]) + shift[:, None, :]

def causal_dwconv(u, w):
    return lax.conv_general_dilated(
        u, w[:, None, :].astype(u.dtype), window_strides=(1,),
        padding=[(CONV_K - 1, 0)], dimension_numbers=("NWC", "WIO", "NWC"),
        feature_group_count=u.shape[-1])

def short_conv_layer(x, c, mod_w, mod_b, norm_g, w_in, conv_w, w_out):
    shift, scale, gate = modulation(c, mod_w, mod_b, 3)
    h = modulated_norm(x, norm_g, shift, scale)
    proj = h @ w_in
    b_gate, c_gate, u, z = jnp.split(proj, 4, axis=-1)
    y = b_gate * causal_dwconv(c_gate * u, conv_w)
    y = y * jax.nn.silu(z)
    return x + gate[:, None, :] * (y @ w_out)

def stick_breaking_attention(q, k, v):
    seq = q.shape[2]
    inv_sqrt_d = 1.0 / math.sqrt(q.shape[-1])
    outs = []
    for i in range(seq // Q_BLOCK):
        q0 = i * Q_BLOCK
        kend = q0 + Q_BLOCK
        qb = q[:, :, q0:kend].astype(jnp.float32)
        kb = k[:, :, :kend].astype(jnp.float32)
        vb = v[:, :, :kend]
        z = jnp.einsum('bhqd,bhkd->bhqk', qb, kb) * inv_sqrt_d
        qpos = q0 + jnp.arange(Q_BLOCK)[:, None]
        kpos = jnp.arange(kend)[None, :]
        mask = kpos < qpos
        log_beta = jax.nn.log_sigmoid(z)
        log_1m_beta = jnp.where(mask, log_beta - z, 0.0)
        suffix = lax.cumsum(log_1m_beta, axis=3, reverse=True) - log_1m_beta
        a = jnp.where(mask, jnp.exp(log_beta + suffix), 0.0)
        outs.append(jnp.einsum('bhqk,bhkd->bhqd', a.astype(vb.dtype), vb))
    return jnp.concatenate(outs, axis=2)

def split_heads(t):
    b, s, _ = t.shape
    return t.reshape(b, s, N_HEADS, HEAD_DIM).transpose(0, 2, 1, 3)

def stick_breaking_layer(x, c, k, v, mod_w, mod_b, norm_g, w_qz, w_out):
    shift, scale, gate = modulation(c, mod_w, mod_b, 3)
    h = modulated_norm(x, norm_g, shift, scale)
    proj = h @ w_qz
    q, z = jnp.split(proj, 2, axis=-1)
    o = stick_breaking_attention(split_heads(q), k, v)
    b, _, s, _ = o.shape
    o = o.transpose(0, 2, 1, 3).reshape(b, s, D_ATTN)
    o = o * jax.nn.silu(z)
    return x + gate[:, None, :] * (o @ w_out)

def first_inputs(seed: int = 0) -> dict:
    key = jax.random.key(seed)
    ks = jax.random.split(key, 20)
    D = D_MODEL
    nrm = lambda k, shape, s: jax.random.normal(k, shape, jnp.float32) * s
    return {
        "x": nrm(ks[0], (BATCH, SEQ, D), 1.0),
        "c": nrm(ks[1], (BATCH, D), 1.0),
        "a_mod_w": nrm(ks[2], (N_A, D, 3 * D), 0.02),
        "a_mod_b": nrm(ks[3], (N_A, 3 * D), 0.01),
        "a_norm_g": 1.0 + nrm(ks[4], (N_A, D), 0.02),
        "a_w_in": nrm(ks[5], (N_A, D, 4 * D_CONV), D ** -0.5),
        "a_conv_w": nrm(ks[6], (N_A, CONV_K, D_CONV), CONV_K ** -0.5),
        "a_w_out": nrm(ks[7], (N_A, D_CONV, D), D_CONV ** -0.5),
        "kv_mod_w": nrm(ks[8], (D, 2 * D), 0.02),
        "kv_mod_b": nrm(ks[9], (2 * D,), 0.01),
        "kv_norm_g": 1.0 + nrm(ks[10], (D,), 0.02),
        "w_kv": nrm(ks[11], (D, 2 * D_ATTN), D ** -0.5),
        "b_mod_w": nrm(ks[12], (N_B, D, 3 * D), 0.02),
        "b_mod_b": nrm(ks[13], (N_B, 3 * D), 0.01),
        "b_norm_g": 1.0 + nrm(ks[14], (N_B, D), 0.02),
        "b_w_qz": nrm(ks[15], (N_B, D, 2 * D_ATTN), D ** -0.5),
        "b_w_out": nrm(ks[16], (N_B, D_ATTN, D), D_ATTN ** -0.5),
        "final_norm_g": 1.0 + nrm(ks[17], (D,), 0.02),
    }

def first_block(x, c, a_mod_w, a_mod_b, a_norm_g, a_w_in, a_conv_w, a_w_out,
              kv_mod_w, kv_mod_b, kv_norm_g, w_kv,
              b_mod_w, b_mod_b, b_norm_g, b_w_qz, b_w_out, final_norm_g):
    k = v = None
    for layer in range(DEPTH):
        if layer < N_A:
            x = short_conv_layer(x, c, a_mod_w[layer], a_mod_b[layer], a_norm_g[layer],
                                 a_w_in[layer], a_conv_w[layer], a_w_out[layer])
        else:
            if layer == N_A:
                kv_shift, kv_scale = modulation(c, kv_mod_w, kv_mod_b, 2)
                hkv = modulated_norm(x, kv_norm_g, kv_shift, kv_scale)
                k_flat, v_flat = jnp.split(hkv @ w_kv, 2, axis=-1)
                k, v = split_heads(k_flat), split_heads(v_flat)
            j = layer - N_A
            x = stick_breaking_layer(x, c, k, v, b_mod_w[j], b_mod_b[j], b_norm_g[j],
                                     b_w_qz[j], b_w_out[j])
    return rmsnorm(x, final_norm_g)


DEPTH_2 = 1

HEAD_DIM_2 = 64
SWA_HEADS = 8
SWA_KV_HEADS = 2
SWA_GROUP = SWA_HEADS // SWA_KV_HEADS
WINDOW = 128
DIFF_HEADS = 4
DIFF_VDIM = 2 * HEAD_DIM_2
BLOCK = 128
D_FF = 2816
CONV_WIDTH = 3
RMS_EPS = 1e-6
NEG_INF = -1e30

SWA_Q = SWA_HEADS * HEAD_DIM_2
SWA_KV = SWA_KV_HEADS * HEAD_DIM_2
DIFF_QK = DIFF_HEADS * 2 * HEAD_DIM_2
DIFF_V = DIFF_HEADS * DIFF_VDIM
IN_COLS = SWA_Q + 2 * SWA_KV + 2 * DIFF_QK + DIFF_V + 2 * D_MODEL


def _rmsnorm(x, g):
    xf = x.astype(jnp.float32)
    y = xf * lax.rsqrt(jnp.mean(xf * xf, axis=-1, keepdims=True) + RMS_EPS)
    return (y * g.astype(jnp.float32)).astype(x.dtype)

def _alibi_slopes(n):
    return jnp.array([2.0 ** (-8.0 * (i + 1) / n) for i in range(n)], dtype=jnp.float32)

def _sliding_window_attention(q, k, v, sinks, slopes):
    b, s, _, d = q.shape
    nb = s // BLOCK
    qb = q.reshape(b, nb, BLOCK, SWA_KV_HEADS, SWA_GROUP, d)

    def with_prev(t):
        tb = t.reshape(b, nb, BLOCK, SWA_KV_HEADS, d)
        prev = jnp.concatenate([jnp.zeros_like(tb[:, :1]), tb[:, :-1]], axis=1)
        return jnp.concatenate([prev, tb], axis=2)

    kb, vb = with_prev(k), with_prev(v)
    scores = jnp.einsum('bnqkgd,bnskd->bnkgqs', qb, kb).astype(jnp.float32) * (d ** -0.5)
    qi = jnp.arange(BLOCK)[:, None]
    kj = jnp.arange(2 * BLOCK)[None, :]
    delta = qi + BLOCK - kj
    key_pos = jnp.arange(nb)[:, None, None] * BLOCK - BLOCK + kj[None]
    valid = (delta >= 0) & (delta < WINDOW) & (key_pos >= 0)
    bias = -slopes[:, :, None, None] * delta.astype(jnp.float32)
    scores = jnp.where(valid[None, :, None, None], scores + bias, NEG_INF)
    sink = jnp.broadcast_to(sinks.astype(jnp.float32).reshape(SWA_KV_HEADS, SWA_GROUP, 1, 1),
                            scores.shape[:-1] + (1,))
    probs = jax.nn.softmax(jnp.concatenate([scores, sink], axis=-1), axis=-1)[..., :-1]
    out = jnp.einsum('bnkgqs,bnskd->bnqkgd', probs.astype(v.dtype), vb)
    return out.reshape(b, s, SWA_HEADS * d)

def _diff_attention(q, k, v, lam, lam_init, subln_g, slopes):
    b, s = q.shape[:2]
    nb = s // BLOCK
    qb = jnp.moveaxis(q.reshape(b, nb, BLOCK, DIFF_HEADS, 2, HEAD_DIM_2), 1, 0)
    key_pos = jnp.arange(s)
    scale = HEAD_DIM_2 ** -0.5

    def block_fn(args):
        qblk, n = args
        scores = jnp.einsum('bqhmd,bshmd->bhmqs', qblk, k).astype(jnp.float32) * scale
        q_pos = n * BLOCK + jnp.arange(BLOCK)
        delta = q_pos[:, None] - key_pos[None, :]
        scores = scores - slopes[:, None, None, None] * delta.astype(jnp.float32)
        scores = jnp.where(delta >= 0, scores, NEG_INF)
        p = jax.nn.softmax(scores, axis=-1)
        a = p[:, :, 0] - lam * p[:, :, 1]
        return jnp.einsum('bhqs,bshe->bqhe', a.astype(v.dtype), v)

    out = lax.map(block_fn, (qb, jnp.arange(nb)))
    out = jnp.moveaxis(out, 0, 1).reshape(b, s, DIFF_HEADS, DIFF_VDIM)
    out = _rmsnorm(out, subln_g) * (1.0 - lam_init)
    return out.reshape(b, s, DIFF_V)

def _conv_ffn(h, w_up, conv_w, conv_b, w_down):
    u = h @ w_up
    a, g = jnp.split(u, 2, axis=-1)
    s = a.shape[1]
    ap = jnp.pad(a, ((0, 0), (CONV_WIDTH - 1, 0), (0, 0)))
    a = ap[:, 0:s] * conv_w[0] + ap[:, 1:s + 1] * conv_w[1] + ap[:, 2:s + 2] * conv_w[2] + conv_b
    return (jax.nn.gelu(a, approximate=False) * g) @ w_down

def second_inputs(seed: int = 0) -> dict:
    key = jax.random.key(seed)
    ks = jax.random.split(key, 20)
    nrm = lambda k, shape, s: jax.random.normal(k, shape, jnp.float32) * s
    D = D_MODEL
    return {
        "x": nrm(ks[0], (BATCH, SEQ, D), 1.0),
        "c": nrm(ks[1], (BATCH, D), 1.0),
        "w_ada": nrm(ks[2], (DEPTH_2, D, 6 * D), 0.5 * D ** -0.5),
        "b_ada": nrm(ks[3], (DEPTH_2, 6 * D), 0.02),
        "norm1_g": 1.0 + nrm(ks[4], (DEPTH_2, D), 0.02),
        "w_in": nrm(ks[5], (DEPTH_2, D, IN_COLS), D ** -0.5),
        "swa_sinks": nrm(ks[6], (DEPTH_2, SWA_HEADS), 1.0),
        "diff_lambda": nrm(ks[7], (DEPTH_2, 4, HEAD_DIM_2), 0.1),
        "diff_subln_g": 1.0 + nrm(ks[8], (DEPTH_2, DIFF_VDIM), 0.02),
        "w_branch_swa": nrm(ks[9], (DEPTH_2, SWA_Q, D), SWA_Q ** -0.5),
        "w_branch_diff": nrm(ks[10], (DEPTH_2, DIFF_V, D), DIFF_V ** -0.5),
        "w_out": nrm(ks[11], (DEPTH_2, D, D), D ** -0.5),
        "norm2_g": 1.0 + nrm(ks[12], (DEPTH_2, D), 0.02),
        "w_up": nrm(ks[13], (DEPTH_2, D, 2 * D_FF), D ** -0.5),
        "conv_w": nrm(ks[14], (DEPTH_2, CONV_WIDTH, D_FF), CONV_WIDTH ** -0.5),
        "conv_b": nrm(ks[15], (DEPTH_2, D_FF), 0.02),
        "w_down": nrm(ks[16], (DEPTH_2, D_FF, D), D_FF ** -0.5),
        "final_g": 1.0 + nrm(ks[17], (D,), 0.02),
    }

def second_block(x, c, w_ada, b_ada, norm1_g, w_in, swa_sinks, diff_lambda, diff_subln_g,
              w_branch_swa, w_branch_diff, w_out, norm2_g, w_up, conv_w, conv_b, w_down, final_g):
    b, s, _ = x.shape
    sizes = [SWA_Q, SWA_KV, SWA_KV, DIFF_QK, DIFF_QK, DIFF_V, D_MODEL, D_MODEL]
    points = [int(p) for p in np.cumsum(sizes)[:-1]]
    slopes_swa = _alibi_slopes(SWA_HEADS).reshape(SWA_KV_HEADS, SWA_GROUP)
    slopes_diff = _alibi_slopes(DIFF_HEADS)
    cs = jax.nn.silu(c)
    for l in range(DEPTH_2):
        mod = cs @ w_ada[l] + b_ada[l]
        shift1, scale1, gate1, shift2, scale2, gate2 = [m[:, None, :] for m in jnp.split(mod, 6, axis=-1)]

        h = _rmsnorm(x, norm1_g[l]) * (1.0 + scale1) + shift1
        proj = h @ w_in[l]
        qa, ka, va, qd, kd, vd, ga, gd = jnp.split(proj, points, axis=-1)
        out_a = _sliding_window_attention(
            qa.reshape(b, s, SWA_HEADS, HEAD_DIM_2),
            ka.reshape(b, s, SWA_KV_HEADS, HEAD_DIM_2),
            va.reshape(b, s, SWA_KV_HEADS, HEAD_DIM_2),
            swa_sinks[l], slopes_swa)
        lam_init = 0.8 - 0.6 * math.exp(-0.3 * l)
        lp = diff_lambda[l].astype(jnp.float32)
        lam = jnp.exp(jnp.sum(lp[0] * lp[1])) - jnp.exp(jnp.sum(lp[2] * lp[3])) + lam_init
        out_d = _diff_attention(
            qd.reshape(b, s, DIFF_HEADS, 2, HEAD_DIM_2),
            kd.reshape(b, s, DIFF_HEADS, 2, HEAD_DIM_2),
            vd.reshape(b, s, DIFF_HEADS, DIFF_VDIM),
            lam, lam_init, diff_subln_g[l], slopes_diff)
        merged = (jax.nn.sigmoid(ga) * (out_a @ w_branch_swa[l])
                  + jax.nn.sigmoid(gd) * (out_d @ w_branch_diff[l]))
        x = x + gate1 * (merged @ w_out[l])

        h2 = _rmsnorm(x, norm2_g[l]) * (1.0 + scale2) + shift2
        x = x + gate2 * _conv_ffn(h2, w_up[l], conv_w[l], conv_b[l], w_down[l])
    return _rmsnorm(x, final_g)


def setup_inputs(seed=0):
    out = dict(first_inputs(seed))
    for name, value in second_inputs(seed + 1).items():
        if name != "x":
            out[name + "_2"] = value
    return out


def reference(
    x, c, a_mod_w, a_mod_b, a_norm_g, a_w_in, a_conv_w, a_w_out, kv_mod_w, kv_mod_b, kv_norm_g,
    w_kv, b_mod_w, b_mod_b, b_norm_g, b_w_qz, b_w_out, final_norm_g, c_2, w_ada_2, b_ada_2,
    norm1_g_2, w_in_2, swa_sinks_2, diff_lambda_2, diff_subln_g_2, w_branch_swa_2,
    w_branch_diff_2, w_out_2, norm2_g_2, w_up_2, conv_w_2, conv_b_2, w_down_2, final_g_2,
):
    x = first_block(
        x, c, a_mod_w, a_mod_b, a_norm_g, a_w_in, a_conv_w, a_w_out, kv_mod_w, kv_mod_b,
        kv_norm_g, w_kv, b_mod_w, b_mod_b, b_norm_g, b_w_qz, b_w_out, final_norm_g,
    )
    return second_block(
        x, c_2, w_ada_2, b_ada_2, norm1_g_2, w_in_2, swa_sinks_2, diff_lambda_2, diff_subln_g_2,
        w_branch_swa_2, w_branch_diff_2, w_out_2, norm2_g_2, w_up_2, conv_w_2, conv_b_2,
        w_down_2, final_g_2,
    )


_drawn_inputs = setup_inputs


def setup_inputs(seed=0):
    import zlib

    import numpy as np

    out = dict(_drawn_inputs(seed))
    spreads = {}
    factors = {'a_mod_b': 3.803,
     'a_norm_g': 3.612,
     'kv_mod_b': 8.0,
     'kv_norm_g': 8.0,
     'b_mod_b': 8.0,
     'b_norm_g': 8.0,
     'final_norm_g': 2.803,
     'norm1_g_2': 8.0,
     'swa_sinks_2': 200.0,
     'diff_subln_g_2': 45.981,
     'norm2_g_2': 8.0,
     'conv_b_2': 25.121,
     'final_g_2': 22.742}
    for name, (base, spread) in spreads.items():
        noise = np.random.default_rng([zlib.crc32(name.encode()), seed]).standard_normal(out[name].shape)
        drawn = base * np.exp(spread * noise) if base else spread * noise
        out[name] = __import__('jax').numpy.asarray(drawn.astype(out[name].dtype))
    for name, factor in factors.items():
        out[name] = (out[name] * factor).astype(out[name].dtype)
    return out
```

```python
from contextlib import ExitStack

import numpy as np

import concourse.bass as bass
from concourse import mybir

F32 = mybir.dt.float32
F32R = mybir.dt.float32r
ALU = mybir.AluOpType
ACT = mybir.ActivationFunctionType
AX_X = mybir.AxisListType.X

P = 128
T = 1024
D = 1024
KC = D // P
HALF = T // 2
NQ = HALF // P
NT = T // P
DH = 64
HEADS = 16
EPS = 1e-6
MASKED = -1e30
CLAMP = 30.0
SWA_HEADS = 8
DIFF_HEADS = 4
LAM_INIT = 0.8 - 0.6
D_FF = 2816
FC = D_FF // P
FGROUPS = [(0, 8), (8, 8), (16, 6)]
SWA_COL, KA_COL, VA_COL, QD_COL, KD_COL, VD_COL, GA_COL, GD_COL = 0, 512, 640, 768, 1280, 1792, 2304, 3328
QSCALE = DH ** -0.5

ROWS0 = [("c", 8), ("c_2", 8), ("a_mod_b", 24), ("a_norm_g", 8), ("a_conv_w", 24), ("kv_mod_b", 16),
         ("b_mod_b", 24), ("kv_norm_g", 8), ("b_norm_g", 8)]
ROWS1 = [("b_ada_2", 48), ("final_norm_g", 8), ("norm1_g_2", 8), ("norm2_g_2", 8), ("final_g_2", 8),
         ("conv_b_2", 22), ("diff_subln_g_2", 1)]
ROWS2 = [("conv_w_2", 66)]
MODS = [("a_mod_w", 0, 0), ("a_mod_w", 1, 0), ("a_mod_w", 2, 0), ("kv_mod_w", 0, 0), ("kv_mod_w", 1, 0),
        ("b_mod_w", 0, 0), ("b_mod_w", 1, 0), ("b_mod_w", 2, 0)] + [("w_ada_2", g, 1) for g in range(6)]
MOD_BIAS = {"a_mod_w": "a_mod_b", "kv_mod_w": "kv_mod_b", "b_mod_w": "b_mod_b", "w_ada_2": "b_ada_2"}
A_SHIFT, A_SCALE, A_GATE, KV_SHIFT, KV_SCALE, B_SHIFT, B_SCALE, B_GATE = range(8)
SHIFT1, SCALE1, GATE1, SHIFT2, SCALE2, GATE2 = range(8, 14)
MODS_AT = {0: [2, 3], 1: [4, 5], 2: [6, 7], 3: [8, 9], 4: [10], 5: [11], 6: [12], 7: [13]}


def unit_list():
    units = []
    for j in range(KC):
        for part in (1, 2, 0, 3):
            units.append(("a_w_in", part * D + j * P, 0, KC))
    units += [("a_w_out", n * P, 0, KC) for n in range(KC)]
    units += [("w_kv", n * P, 0, KC) for n in range(2 * KC)]
    units += [("b_w_qz", n * P, 0, KC) for n in range(2 * KC)]
    units += [("b_w_out", n * P, 0, KC) for n in range(KC)]
    cols = ([SWA_COL + n * P for n in range(4)] + [QD_COL + n * P for n in range(4)] + [KA_COL]
            + [KD_COL + n * P for n in range(4)] + [VA_COL] + [VD_COL + n * P for n in range(4)]
            + [GA_COL + n * P for n in range(8)] + [GD_COL + n * P for n in range(8)])
    units += [("w_in_2", col, 0, KC) for col in cols]
    units += [("branch", n * P, 0, KC) for n in range(KC)]
    units += [("w_out_2", n * P, 0, KC) for n in range(KC)]
    for first, many in FGROUPS:
        for f in range(first, first + many):
            units += [("w_up_2", f * P, 0, KC), ("w_up_2", D_FF + f * P, 0, KC)]
        units += [("w_down_2", n * P, first * P, many) for n in range(KC)]
    return units


UNITS = unit_list()
U_AIN = 0
U_AOUT = U_AIN + 4 * KC
U_KV = U_AOUT + KC
U_QZ = U_KV + 2 * KC
U_BOUT = U_QZ + 2 * KC
U_IN2 = U_BOUT + KC
U_BRANCH = U_IN2 + 34
U_OUT2 = U_BRANCH + KC
U_FFN = U_OUT2 + KC

FIRST_V = (U_KV + KC, U_IN2 + 13)

STICK = [(0, kb) for kb in range(NQ - 1, -1, -1)] + [(1, kb) for kb in range(NT - 1, -1, -1)]


def program(nc, a, out, known):
    names = {}
    ctx = ExitStack()
    with ctx:
        def sem(name):
            return ctx.enter_context(nc.semaphore(name))

        base = -(-nc.sbuf_base // 64) * 64
        KIB = 1024
        AT_X, AT_A, AT_B = base, base + 32 * KIB, base + 96 * KIB
        AT_W = base + 160 * KIB
        AT_M = AT_W + 24 * KIB
        AT_C = AT_M + 20 * KIB

        def at(name, offset, shape, dt=F32):
            return nc.alloc_sbuf_tensor_at(name, [P] + shape, dt, offset=offset)

        X = at("X", AT_X, [KC, T])
        opA = at("opA", AT_A, [2, KC, T], F32R)
        opB = at("opB", AT_B, [2, KC, T], F32R)
        w_raw = at("w_raw", AT_W, [2, KC, P])
        w_hi = at("w_hi", AT_W + 8 * KIB, [2, KC, P], F32R)
        w_lo = at("w_lo", AT_W + 16 * KIB, [2, KC, P], F32R)
        M = [at(f"M{i}", AT_M + 4 * KIB * i, [T]) for i in range(5)]
        ident = at("ident", AT_C, [P])
        ones = at("ones", AT_C + 512, [P])
        cols = at("cols", AT_C + 1024, [3 * P])
        small = at("small", AT_C + 2560, [100])
        mod = at("mod", AT_C + 2560 + 416, [14, KC])
        x_rows = at("x_rows", AT_B, [NT, D])
        vec_rows = at("vec_rows", AT_A, [3, P])
        mod_acc = M[3]
        mod_raw = at("mod_raw", AT_M + 16 * KIB, [2, HALF])
        cs = at("cs", AT_M + 4 * KIB, [2, HALF])
        yt = at("yt", AT_M + 8 * KIB, [2, HALF])
        hn = at("hn", AT_M + 8 * KIB, [2, HALF])
        xn = at("xn", AT_M, [2, HALF])
        stage = at("stage", AT_B + 32 * KIB, [2, 2, T], F32R)
        vstage = at("vstage", AT_B + 48 * KIB, [2, 2, T], F32R)
        vt = at("vt", AT_M + 8 * KIB, [T])
        sz = at("sz", AT_B, [KC, T])
        hin = at("hin", AT_B + 32 * KIB, [2, 4, T], F32R)
        s_t = at("s_t", AT_X, [2, HALF])
        s_sp = at("s_sp", AT_X + 4 * KIB, [2, HALF])
        s_p = at("s_p", AT_X + 8 * KIB, [2, HALF])
        s_a = at("s_a", AT_X + 12 * KIB, [2, HALF])
        s_ah = at("s_ah", AT_X + 16 * KIB, [2, HALF], F32R)
        s_al = at("s_al", AT_X + 20 * KIB, [2, HALF], F32R)
        s_o = at("s_o", AT_X + 24 * KIB, [2, HALF])
        s_tmp = at("s_tmp", AT_X + 28 * KIB, [HALF])
        tri = at("tri", AT_X + 30 * KIB, [P])
        nones = at("nones", AT_X + 30 * KIB + 512, [P])
        ident_r = at("ident_r", AT_X + 31 * KIB, [P], F32R)
        mask_r = at("mask_r", AT_X + 31 * KIB + 512, [P], F32R)
        masks = at("masks", AT_M, [P])
        qkv = at("qkv", AT_X, [6, T], F32R)
        bias = at("bias", AT_X + 24 * KIB, [2, T])
        prob = at("prob", AT_M, [2, T])
        aT = at("aT", AT_M + 8 * KIB, [2, T], F32R)
        d_o = at("d_o", AT_M + 16 * KIB, [2, HALF])
        gates = at("gates", AT_B, [2 * KC, T])

        PS = ctx.enter_context(nc.psum_tensor("PS", [P, 8, HALF], F32))

        def scratch(name, shape, dt=F32):
            return nc.dram_tensor(name, shape, dt).ap()

        x_dram = scratch("x_dram", [P, KC * T], F32)
        k_dram = scratch("k_dram", [2, D, T])
        q_dram = scratch("q_dram", [2, D, T])
        v_dram = scratch("v_dram", [KC, P, 2, T])
        q2_dram = scratch("q2_dram", [2, D, T])
        k2_dram = scratch("k2_dram", [2, D, T])
        va_dram = scratch("va_dram", [P, 2, T])
        vd_dram = scratch("vd_dram", [DIFF_HEADS, P, 2, T])

        def banks(b):
            return PS[:, b:b + 2, :].rearrange("p b t -> p (b t)")

        pe_done, act_done, dve_done, pool_done = sem("pe_done"), sem("act_done"), sem("dve_done"), sem("pool_done")
        vec_in = sem("vec_in")
        x_in = [sem(f"x_in{tb}") for tb in range(NT)]
        w_in = [sem(f"w_in{s}") for s in range(2)]
        mod_in = [sem(f"mod_in{s}") for s in range(2)]
        x_moved = sem("x_moved")
        stored = [sem(f"stored{s}") for s in range(2)]
        v_stored = [sem(f"v_stored{s}") for s in range(2)]
        head_in = [sem(f"head_in{s}") for s in range(2)]
        qk_in, v_in = sem("qk_in"), sem("v_in")
        row_gone = [sem(f"row_gone{s}") for s in range(4)]
        total = {}

        def now(s):
            return total.get(id(s), 0)

        def step(s, *name, by=1):
            total[id(s)] = now(s) + by
            if name:
                names[name] = now(s)

        def at(*name):
            return known.get(name, 0)

        def reader(u):
            if u < U_AOUT:
                return act_done if u % 4 in (0, 3) else dve_done
            if u >= U_FFN:
                first = [f for f, many in FGROUPS if U_FFN + 2 * f + KC * FGROUPS.index((f, many)) <= u][-1]
                gi = [f for f, _ in FGROUPS].index(first)
                n = u - (U_FFN + 2 * first + KC * gi)
                return act_done if n < 2 * FGROUPS[gi][1] and n % 2 == 0 else dve_done
            on_act = (range(U_KV + KC, U_QZ), range(U_QZ + KC, U_BOUT), range(U_IN2 + 13, U_BRANCH))
            return act_done if any(u in r for r in on_act) else dve_done

        def col(rows, name):
            at0 = 0
            for t, rs in enumerate((ROWS0, ROWS1, ROWS2)):
                at0 = t * P
                for n, many in rs:
                    if n == name:
                        return at0
                    at0 += many
            raise KeyError(name)

        C = {n: col(None, n) for rs in (ROWS0, ROWS1, ROWS2) for n, _ in rs}
        EPS_COL, SILU_C, GS, SINK, LAM = 0, 1, 17, 25, 33
        MX, RS, RI, LAMS, SUBG = 41, 49, 57, 65, 69

        block = ctx.enter_context(nc.Block())

        MISC_FREE = {"kv": "a", "n1": "fin1", "fin2": "n2"}

        def source(u):
            name, col0, row0, chunks = UNITS[u]
            if name == "branch":
                return [(a["w_branch_swa_2"][0], col0, 0, 4, 0), (a["w_branch_diff_2"][0], col0, 0, 4, 4)]
            w = a[name]
            if len(w.shape) == 3:
                w = w[0]
            return [(w, col0, row0, chunks, 0)]

        def second_loads(sp):
            sp.wait_ge(stored[(U_IN2 + 11) % 2], at("stored", U_IN2 + 11))
            sp.wait_ge(stored[(U_IN2 + 12) % 2], at("stored", U_IN2 + 12))
            sp.wait_ge(v_stored[(U_IN2 + 16) % 2], at("v_stored", U_IN2 + 16))
            sp.wait_ge(v_stored[(U_IN2 + 17) % 2], at("v_stored", U_IN2 + 17))
            for n in range(0, SWA_HEADS, 2):
                if n == 0:
                    sp.wait_ge(x_moved, at("x_out", 1))
                else:
                    sp.wait_ge(pe_done, at("swa_S", n - 1, 1))
                for part in range(2):
                    sp.dma_start(qkv[:, part, :].bitcast(F32), q2_dram[part, n // 2 * P:(n // 2 + 1) * P, :]).then_inc(qk_in, 16)
                    step(qk_in, "qk_in", n, by=16)
                if n % 4 == 0:
                    kv = n // 4
                    for part in range(2):
                        for place in range(2):
                            sp.dma_start(qkv[place * DH:(place + 1) * DH, 2 + part, :].bitcast(F32),
                                         k2_dram[part, kv * DH:(kv + 1) * DH, :]).then_inc(qk_in, 16)
                            step(qk_in, "qk_in", n, by=16)
                    if n:
                        sp.wait_ge(pe_done, at("swa_pv", n - 1, 1))
                    src = va_dram[:, kv, :].rearrange("p (b s d) -> p b s d", b=NT, s=2)
                    for order in range(2):
                        dst = qkv[:, 4 + order, :].bitcast(F32).rearrange("p (b s d) -> p b s d", b=NT, s=2)
                        for s in range(2):
                            sp.dma_start(dst[:, :, s if order == 0 else 1 - s, :], src[:, :, s, :]).then_inc(v_in, 16)
                            step(v_in, "v_in", n, by=16)
            for j in range(DIFF_HEADS):
                if j == 0:
                    sp.wait_ge(pe_done, at("swa_S", SWA_HEADS - 1, 1))
                else:
                    sp.wait_ge(pe_done, at("diff_S", j - 1, NT - 1, 1))
                if j:
                    sp.wait_ge(pe_done, at("diff_S", j - 1, NT - 1, 0))
                for part in range(2):
                    sp.dma_start(qkv[:, part, :].bitcast(F32), q2_dram[part, (4 + j) * P:(5 + j) * P, :]).then_inc(qk_in, 16)
                    step(qk_in, "qk_in", SWA_HEADS + j, by=16)
                    sp.dma_start(qkv[:, 2 + part, :].bitcast(F32), k2_dram[part, (1 + j) * P:(2 + j) * P, :]).then_inc(qk_in, 16)
                    step(qk_in, "qk_in", SWA_HEADS + j, by=16)
                if j == 0:
                    sp.wait_ge(pe_done, at("swa_pv", SWA_HEADS - 1, 1))
                else:
                    sp.wait_ge(pe_done, at("diff_pv", j - 1, NT - 1))
                sp.dma_start(qkv[:, 4:6, :].bitcast(F32), vd_dram[j]).then_inc(v_in, 16)
                step(v_in, "v_in", SWA_HEADS + j, by=16)

        def turn_v(pe, u):
            pe.wait_ge(act_done, at("vt", u))
            if not (u in FIRST_V):
                pe.wait_ge(dve_done, at("v_split", u - 1))
            for kb in range(NT):
                ins = pe.transpose(PS[:, 4 + kb // 4, (kb % 4) * P:(kb % 4 + 1) * P], vt[:, kb * P:(kb + 1) * P], ident[:])
            ins.then_inc(pe_done, 1)
            step(pe_done, "v_T", u)

        def stick_pe(pe):
            n = HEADS * len(STICK)

            def where(g):
                h, i = divmod(g, len(STICK))
                hf, kb = STICK[i]
                return h, i, hf, kb, max(0, (kb - NQ * hf) * P)

            def scores(g):
                h, i, hf, kb, qs = where(g)
                s, bank = h % 2, g % 4
                pe.wait_ge(head_in[h % 2], at("head_in", h))
                pe.wait_ge(pool_done, at("stick_consts"))
                if g >= 4:
                    pe.wait_ge(act_done, at("stick_a", g - 4))
                pe.wait_ge(reader(U_BOUT - 1), at("free", U_BOUT - 1))
                pe.wait_ge(reader(U_BOUT - 2), at("free", U_BOUT - 2))
                q = slice(hf * HALF + qs, (hf + 1) * HALF)
                k = hin[:, s, 0, kb * P:(kb + 1) * P]
                pe.matmul(PS[:, bank, qs:], k, hin[:, s, 1, q], start=True, stop=False)
                diag = kb >= NQ * hf
                ins = pe.matmul(PS[:, bank, qs:], k, hin[:, s, 2, q], start=False, stop=True)
                if diag:
                    ins = pe.matmul(PS[:, bank, qs:qs + P], ident_r[:], mask_r[:], start=False, stop=True,
                                    skip_group_check=True)
                ins.then_inc(pe_done, 1)
                step(pe_done, "stick_s", g)

            def sums(g):
                h, i, hf, kb, qs = where(g)
                pe.wait_ge(dve_done, at("stick_sp", g))
                top = kb == NQ * hf + NQ - 1
                ins = pe.matmul(PS[:, g % 4, qs:], tri[:], s_sp[:, g % 2, qs:], start=False, stop=True,
                                skip_group_check=True)
                if not top:
                    qp = max(0, (kb + 1 - NQ * hf) * P)
                    pe.wait_ge(pool_done, at("stick_p", g - 1))
                    ins = pe.matmul(PS[:, g % 4, qp:], nones[:], s_p[:, (g - 1) % 2, qp:], start=False, stop=True,
                                    skip_group_check=True)
                ins.then_inc(pe_done, 1)
                step(pe_done, "stick_b", g)

            def values(g):
                h, i, hf, kb, qs = where(g)
                s, o = h % 2, 4 + (2 * h + hf) % 2
                top = kb == NQ * hf + NQ - 1
                pe.wait_ge(dve_done, at("stick_al", g))
                if h:
                    pe.wait_ge(dve_done, at("stick_o", h - 1, hf))
                v = hin[:, s, 3, kb * P:(kb + 1) * P]
                pe.matmul(PS[:, o, qs:], v, s_ah[:, g % 2, qs:], start=top, stop=False, skip_group_check=True)
                ins = pe.matmul(PS[:, o, qs:], v, s_al[:, g % 2, qs:], start=False, stop=(kb == 0),
                                skip_group_check=True)
                ins.then_inc(pe_done, 1)
                step(pe_done, "stick_c", g)
                if i == len(STICK) - 1:
                    names[("stick_free", h)] = names[("stick_c", g)]

            for g in range(n + 3):
                if g < n:
                    scores(g)
                if 0 <= g - 2 < n:
                    sums(g - 2)
                if 0 <= g - 3 < n:
                    values(g - 3)

        def second_pe(pe):
            def swa_scores(n, hf):
                g = 2 * n + hf
                pe.wait_ge(qk_in, at("qk_in", n - n % 2))
                if g >= 2:
                    pe.wait_ge(dve_done, at("swa_s", (g - 2) // 2, g % 2))
                pe.wait_ge(reader(U_BRANCH - 1), at("free", U_BRANCH - 1))
                pe.wait_ge(reader(U_BRANCH - 2), at("free", U_BRANCH - 2))
                pe.wait_ge(dve_done, at("v_split", U_IN2 + 17))
                for b in range(NQ):
                    i = NQ * hf + b
                    pieces = [(0, (i - 1) * P, 2 * P)] if i else [(0, 0, P), (P, 0, P)]
                    for at0, k0, width in pieces:
                        dst = PS[:, 2 * (g % 2) + b // 2, (b % 2) * 2 * P + at0:(b % 2) * 2 * P + at0 + width]
                        for x, (pq, pk) in enumerate(((0, 0), (1, 0), (0, 1))):
                            ins = pe.matmul(dst, swa_q(n, pq, i), swa_k(n, pk, k0, width), start=(x == 0), stop=(x == 2))
                ins.then_inc(pe_done, 1)
                step(pe_done, "swa_S", n, hf)

            def swa_q(n, part, i):
                r = DH * (n % 2)
                return qkv[r:r + DH, part, i * P:(i + 1) * P]

            def swa_k(n, part, k0, width):
                r = DH * (n % 2)
                return qkv[r:r + DH, 2 + part, k0:k0 + width]

            def swa_turn(n, hf):
                pe.wait_ge(dve_done, at("swa_p", n, hf))
                if n or hf:
                    pe.wait_ge(dve_done, at("swa_lo", (2 * n + hf - 1) // 2, (hf + 1) % 2))
                for x in range(8):
                    ins = pe.transpose(PS[:, 4 + x // 4, (x % 4) * P:(x % 4 + 1) * P],
                                       prob[:, hf, x * P:(x + 1) * P], ident[:])
                ins.then_inc(pe_done, 1)
                step(pe_done, "swa_T", n, hf)

            def swa_values(n, hf):
                g = 2 * n + hf
                pe.wait_ge(v_in, at("v_in", n - n % 4))
                pe.wait_ge(dve_done, at("swa_lo", n, hf))
                if g >= 2:
                    pe.wait_ge(dve_done, at("swa_o", (g - 2) // 2, hf))
                for b in range(NQ):
                    i = NQ * hf + b
                    steps = [(w, part) for w in range(2) if i or w for part in range(2)]
                    for x, (w, part) in enumerate(steps):
                        kb = i - 1 + w
                        ins = pe.matmul(PS[:, 6 + hf, b * P:(b + 1) * P], qkv[:, 4 + n % 2, kb * P:(kb + 1) * P],
                                        aT[:, part, (2 * b + w) * P:(2 * b + w + 1) * P],
                                        start=(x == 0), stop=(x == len(steps) - 1))
                ins.then_inc(pe_done, 1)
                step(pe_done, "swa_pv", n, hf)

            steps = [(n, hf) for n in range(SWA_HEADS) for hf in range(2)]
            for x in range(len(steps) + 1):
                if x < len(steps):
                    swa_scores(*steps[x])
                if x:
                    swa_turn(*steps[x - 1])
                    swa_values(*steps[x - 1])

            def diff_scores(j, i):
                pe.wait_ge(qk_in, at("qk_in", SWA_HEADS + j))
                pe.wait_ge(dve_done, at("swa_s", SWA_HEADS - 1, 1))
                for m in range(2):
                    if i or j:
                        pe.wait_ge(dve_done, at("diff_s", (8 * j + i - 1) // 8, (i - 1) % 8, m))
                    r = slice(DH * m, DH * (m + 1))
                    for k0 in range(0, (i + 1) * P, HALF):
                        width = min(HALF, (i + 1) * P - k0)
                        for x, (pq, pk) in enumerate(((0, 0), (1, 0), (0, 1))):
                            ins = pe.matmul(PS[:, 2 * m + k0 // HALF, 0:width], qkv[r, pq, i * P:(i + 1) * P],
                                            qkv[r, 2 + pk, k0:k0 + width], start=(x == 0), stop=(x == 2))
                    ins.then_inc(pe_done, 1)
                    step(pe_done, "diff_S", j, i, m)

            def diff_turn(j, i):
                pe.wait_ge(dve_done, at("diff_a", j, i))
                if i or j:
                    pe.wait_ge(dve_done, at("diff_lo", (8 * j + i - 1) // 8, (i - 1) % 8))
                for kb in range(i + 1):
                    ins = pe.transpose(PS[:, 4 + kb // 4, (kb % 4) * P:(kb % 4 + 1) * P],
                                       prob[:, 0, kb * P:(kb + 1) * P], ident[:])
                ins.then_inc(pe_done, 1)
                step(pe_done, "diff_T", j, i)

            def diff_values(j, i):
                pe.wait_ge(v_in, at("v_in", SWA_HEADS + j))
                pe.wait_ge(dve_done, at("diff_lo", j, i))
                if i % NQ == 0:
                    if i or j:
                        pe.wait_ge(dve_done, at("diff_o", (2 * j + i // NQ - 1) // 2, (i // NQ + 1) % 2))
                    pe.wait_ge(dve_done, at("swa_o", SWA_HEADS - 1, 1))
                    pe.wait_ge(dve_done, at("swa_o", SWA_HEADS - 1, 0))
                for kb in range(i + 1):
                    for x, (pv, pa) in enumerate(((0, 0), (1, 0), (0, 1))):
                        ins = pe.matmul(PS[:, 6, (i % NQ) * P:(i % NQ + 1) * P],
                                        qkv[:, 4 + pv, kb * P:(kb + 1) * P], aT[:, pa, kb * P:(kb + 1) * P],
                                        start=(kb == 0 and x == 0), stop=(kb == i and x == 2))
                ins.then_inc(pe_done, 1)
                step(pe_done, "diff_pv", j, i)
                if i % NQ == NQ - 1:
                    hf = i // NQ
                    pe.wait_ge(act_done, at("diff_sq", j, hf))
                    pe.matmul(PS[:, 7, :], ones[:], d_o[:, 0, :], start=True, stop=True).then_inc(pe_done, 1)
                    step(pe_done, "diff_ss", j, hf)

            steps = [(j, i) for j in range(DIFF_HEADS) for i in range(NT)]
            for x in range(len(steps) + 1):
                if x < len(steps):
                    diff_scores(*steps[x])
                if x:
                    diff_turn(*steps[x - 1])
                    diff_values(*steps[x - 1])

        def stick_act(act):
            n = HEADS * len(STICK)

            def cut(g):
                h, i = divmod(g, len(STICK))
                hf, kb = STICK[i]
                return h, hf, kb, max(0, (kb - NQ * hf) * P)

            for g in range(n + 2):
                if g < n:
                    h, hf, kb, qs = cut(g)
                    t = s_t[:, g % 2, qs:]
                    act.wait_ge(dve_done, at("stick_t", g))
                    act.wait_ge(act_done, now(act_done))
                    act.activation(t, t, ACT.Exp).then_inc(act_done, 1)
                    step(act_done)
                    act.wait_ge(act_done, now(act_done))
                    act.activation(t, t, ACT.Ln, bias=1.0).then_inc(act_done, 1)
                    step(act_done, "stick_l", g)
                if g >= 2:
                    e = g - 2
                    h, hf, kb, qs = cut(e)
                    act.wait_ge(pe_done, at("stick_b", e))
                    if e >= 2:
                        act.wait_ge(dve_done, at("stick_al", e - 2))
                    act.wait_ge(act_done, now(act_done))
                    act.activation(s_a[:, e % 2, qs:], PS[:, e % 4, qs:], ACT.Exp).then_inc(act_done, 1)
                    step(act_done, "stick_a", e)
                if g >= 4 and (g - 4) % len(STICK) in (NQ - 1, len(STICK) - 1):
                    h, hf, kb, qs = cut(g - 4)
                    other = slice(DH * (1 - h % 2), DH * (1 - h % 2) + DH)
                    main = slice(DH * (h % 2), DH * (h % 2) + DH)
                    act.wait_ge(pe_done, at("stick_c", g - 4))
                    if h or hf:
                        act.wait_ge(dve_done, at("stick_o", (2 * h + hf - 1) // 2, (hf + 1) % 2))
                    act.wait_ge(act_done, now(act_done))
                    act.activation(s_tmp[main, :], PS[other, 4 + hf, :], ACT.Copy).then_inc(act_done, 1)
                    step(act_done, "stick_tmp", h, hf)
            for x in (2,):
                h, hf, kb, qs = cut(n - 1)
                other = slice(0, DH)
                main = slice(DH, P)
                act.wait_ge(pe_done, at("stick_c", n - 1))
                act.wait_ge(dve_done, at("stick_o", h, 0))
                act.wait_ge(act_done, now(act_done))
                act.activation(s_tmp[main, :], PS[other, 4 + hf, :], ACT.Copy).then_inc(act_done, 1)
                step(act_done, "stick_tmp", h, hf)

        def second_act(act):
            def exps(n, hf):
                for b in range(NQ):
                    c = hf * 4 + b
                    p = prob[:, hf, b * 2 * P:(b + 1) * 2 * P]
                    act.wait_ge(dve_done, at("swa_mx", n, hf))
                    act.wait_ge(act_done, now(act_done))
                    act.activation(p, p, ACT.Exp, bias=small[:, MX + c:MX + c + 1],
                                   accum_out=small[:, RS + c:RS + c + 1]).then_inc(act_done, 1)
                    step(act_done, "swa_e", n, hf)
                act.wait_ge(act_done, now(act_done))
                act.activation(small[:, RI + 4 * hf:RI + 4 * hf + 4], small[:, MX + 4 * hf:MX + 4 * hf + 4],
                               ACT.Exp, bias=small[:, SINK + n:SINK + n + 1]).then_inc(act_done, 1)
                step(act_done, "swa_se", n, hf)

            def outputs(n, hf):
                act.wait_ge(pe_done, at("swa_T", n, hf))
                if n or hf:
                    act.wait_ge(pe_done, at("swa_pv", (2 * n + hf - 1) // 2, (hf + 1) % 2))
                act.wait_ge(act_done, now(act_done))
                act.activation(aT[:, 0, :], banks(4), ACT.Copy).then_inc(act_done, 1)
                step(act_done, "swa_hi", n, hf)
                other = slice(DH * (1 - n % 2), DH * (1 - n % 2) + DH)
                main = slice(DH * (n % 2), DH * (n % 2) + DH)
                act.wait_ge(pe_done, at("swa_pv", n, hf))
                if n >= 2:
                    act.wait_ge(dve_done, at("swa_out", n // 2 - 1, hf))
                act.wait_ge(act_done, now(act_done))
                act.activation(d_o[main, hf, :], PS[other, 6 + hf, :], ACT.Copy).then_inc(act_done, 1)
                step(act_done, "swa_tmp", n, hf)

            steps = [(n, hf) for n in range(SWA_HEADS) for hf in range(2)]
            for x in range(len(steps) + 1):
                if x < len(steps):
                    exps(*steps[x])
                if x:
                    outputs(*steps[x - 1])

            def rows_exp(j, i):
                w = (i + 1) * P
                for m in (1, 0):
                    act.wait_ge(dve_done, at("diff_mx", j, i, m))
                    act.wait_ge(act_done, now(act_done))
                    act.activation(prob[:, m, 0:w], prob[:, m, 0:w], ACT.Exp, bias=small[:, MX + m:MX + m + 1],
                                   accum_out=small[:, RS + m:RS + m + 1]).then_inc(act_done, 1)
                    step(act_done, "diff_e", j, i, m)

            def turned_hi(j, i):
                w = (i + 1) * P
                act.wait_ge(pe_done, at("diff_T", j, i))
                if i or j:
                    act.wait_ge(pe_done, at("diff_pv", (8 * j + i - 1) // 8, (i - 1) % 8))
                else:
                    act.wait_ge(pe_done, at("swa_pv", SWA_HEADS - 1, 1))
                act.wait_ge(act_done, now(act_done))
                act.activation(aT[:, 0, 0:w], banks(4)[:, 0:w], ACT.Copy).then_inc(act_done, 1)
                step(act_done, "diff_hi", j, i)

            def head_rms(j, hf):
                act.wait_ge(pe_done, at("diff_pv", j, NQ * hf + NQ - 1))
                act.wait_ge(dve_done, at("swa_out", 3, 1))
                act.wait_ge(dve_done, at("swa_out", 3, 0))
                if j or hf:
                    act.wait_ge(dve_done, at("diff_o", (2 * j + hf - 1) // 2, (hf + 1) % 2))
                act.wait_ge(act_done, now(act_done))
                act.activation(d_o[:, 0, :], PS[:, 6, :], ACT.Square).then_inc(act_done, 1)
                step(act_done, "diff_sq", j, hf)
                act.wait_ge(pe_done, at("diff_ss", j, hf))
                act.wait_ge(act_done, now(act_done))
                act.activation(d_o[:, 0, :], PS[:, 7, :], ACT.Ln, bias=small[:, EPS_COL:EPS_COL + 1],
                               scale=1.0 / P).then_inc(act_done, 1)
                step(act_done)
                act.wait_ge(act_done, now(act_done))
                act.activation(d_o[:, 0, :], d_o[:, 0, :], ACT.Exp, scale=-0.5).then_inc(act_done, 1)
                step(act_done, "diff_r", j, hf)

            def out_hi(j, hf):
                act.wait_ge(dve_done, at("diff_o", j, hf))
                act.wait_ge(act_done, now(act_done))
                act.activation(opA[:, 0, 4 + j, hf * HALF:(hf + 1) * HALF], d_o[:, 1, :], ACT.Copy).then_inc(act_done, 1)
                step(act_done, "diff_ohi", j, hf)

            steps = [(j, i) for j in range(DIFF_HEADS) for i in range(NT)]
            for x in range(len(steps) + 2):
                if 1 <= x <= len(steps):
                    turned_hi(*steps[x - 1])
                if x < len(steps):
                    rows_exp(*steps[x])
                if x >= 2 and x - 2 < len(steps) and (x - 2) % NQ == NQ - 1:
                    out_hi(steps[x - 2][0], steps[x - 2][1] // NQ)
                if 1 <= x <= len(steps) and (x - 1) % NQ == NQ - 1:
                    head_rms(steps[x - 1][0], steps[x - 1][1] // NQ)

        def stick_dve(dve):
            n = HEADS * len(STICK)

            def cut(g):
                h, i = divmod(g, len(STICK))
                hf, kb = STICK[i]
                return h, hf, kb, max(0, (kb - NQ * hf) * P)

            def finish(h, hf):
                main = slice(DH * (h % 2), DH * (h % 2) + DH)
                j = h // 2
                t = slice(hf * HALF, (hf + 1) * HALF)
                dve.wait_ge(act_done, at("stick_tmp", h, hf))
                dve.wait_ge(dve_done, now(dve_done))
                dve.tensor_tensor(s_o[main, hf, :], PS[main, 4 + hf, :], s_tmp[main, :], ALU.add).then_inc(dve_done, 1)
                step(dve_done, "stick_o", h, hf)
                if h % 2:
                    dve.wait_ge(reader(U_BOUT - 1), at("free", U_BOUT - 1))
                    dve.wait_ge(dve_done, now(dve_done))
                    dve.tensor_tensor(s_o[:, hf, :], s_o[:, hf, :], sz[:, j, t], ALU.mult).then_inc(dve_done, 1)
                    step(dve_done)
                    dve.wait_ge(pe_done, at("unit", U_BOUT - 1, 1))
                    dve.wait_ge(dve_done, now(dve_done))
                    dve.tensor_copy(opA[:, 0, j, t], s_o[:, hf, :]).then_inc(dve_done, 1)
                    step(dve_done)
                    dve.wait_ge(dve_done, now(dve_done))
                    dve.tensor_tensor(opA[:, 1, j, t], s_o[:, hf, :], opA[:, 0, j, t].bitcast(F32),
                                      ALU.subtract).then_inc(dve_done, 1)
                    step(dve_done, "stick_out", j, hf)

            for g in range(n + 5):
                if g < n:
                    h, hf, kb, qs = cut(g)
                    dve.wait_ge(pe_done, at("stick_s", g))
                    dve.wait_ge(x_moved, at("x_out", 0))
                    dve.wait_ge(dve_done, now(dve_done))
                    dve.tensor_scalar(s_t[:, g % 2, qs:], PS[:, g % 4, qs:], CLAMP, None, ALU.min).then_inc(dve_done, 1)
                    step(dve_done, "stick_t", g)
                if 1 <= g <= n:
                    e = g - 1
                    h, hf, kb, qs = cut(e)
                    dve.wait_ge(act_done, at("stick_l", e))
                    if e >= 2:
                        dve.wait_ge(pe_done, at("stick_b", e - 2))
                    if e >= 2 and cut(e - 2)[2] > 0:
                        dve.wait_ge(pool_done, at("stick_p", e - 2))
                    dve.wait_ge(dve_done, now(dve_done))
                    dve.tensor_tensor(s_sp[:, e % 2, qs:], s_t[:, e % 2, qs:], PS[:, e % 4, qs:], ALU.max).then_inc(dve_done, 1)
                    step(dve_done, "stick_sp", e)
                if 3 <= g < n + 3:
                    e = g - 3
                    h, hf, kb, qs = cut(e)
                    dve.wait_ge(act_done, at("stick_a", e))
                    if e >= 2:
                        dve.wait_ge(pe_done, at("stick_c", e - 2))
                    dve.wait_ge(dve_done, now(dve_done))
                    dve.tensor_copy(s_ah[:, e % 2, qs:], s_a[:, e % 2, qs:]).then_inc(dve_done, 1)
                    step(dve_done)
                    dve.wait_ge(dve_done, now(dve_done))
                    dve.tensor_tensor(s_al[:, e % 2, qs:], s_a[:, e % 2, qs:],
                                      s_ah[:, e % 2, qs:].bitcast(F32), ALU.subtract).then_inc(dve_done, 1)
                    step(dve_done, "stick_al", e)
                if g >= 5 and (g - 5) % len(STICK) in (NQ - 1, len(STICK) - 1) and g - 5 < n:
                    h, hf, kb, qs = cut(g - 5)
                    finish(h, hf)
            names[("att_end", 0)] = now(dve_done)
            names[("att_end2", 0)] = now(dve_done)

        def second_dve(dve):
            def finish(n, hf):
                main = slice(DH * (n % 2), DH * (n % 2) + DH)
                j = n // 2
                t = slice(hf * HALF, (hf + 1) * HALF)
                dve.wait_ge(act_done, at("swa_tmp", n, hf))
                dve.wait_ge(dve_done, now(dve_done))
                dve.tensor_tensor(d_o[main, hf, :], PS[main, 6 + hf, :], d_o[main, hf, :], ALU.add).then_inc(dve_done, 1)
                step(dve_done, "swa_o", n, hf)
                if n % 2:
                    dve.wait_ge(pe_done, at("unit", U_BRANCH - 1, 1))
                    dve.wait_ge(dve_done, now(dve_done))
                    dve.tensor_copy(opA[:, 0, j, t], d_o[:, hf, :]).then_inc(dve_done, 1)
                    step(dve_done)
                    dve.wait_ge(dve_done, now(dve_done))
                    dve.tensor_tensor(opA[:, 1, j, t], d_o[:, hf, :], opA[:, 0, j, t].bitcast(F32),
                                      ALU.subtract).then_inc(dve_done, 1)
                    step(dve_done, "swa_out", j, hf)

            def turned(n, hf):
                dve.wait_ge(act_done, at("swa_hi", n, hf))
                dve.wait_ge(dve_done, now(dve_done))
                dve.tensor_tensor(aT[:, 1, :], banks(4), aT[:, 0, :].bitcast(F32),
                                  ALU.subtract).then_inc(dve_done, 1)
                step(dve_done, "swa_lo", n, hf)

            def probs(n, hf):
                slope = 2.0 ** -(n + 1)
                s3 = prob[:, hf, :].rearrange("p (b k) -> p b k", b=NQ)
                m = small[:, MX + 4 * hf:MX + 4 * hf + 4]
                g = 2 * n + hf
                dve.wait_ge(pe_done, at("swa_S", n, hf))
                dve.wait_ge(pool_done, at("bias_w", 0))
                dve.wait_ge(pool_done, at("bias_w", 1))
                if n:
                    dve.wait_ge(pe_done, at("swa_T", n - 1, hf))
                else:
                    dve.wait_ge(x_moved, at("x_out", 1))
                dve.wait_ge(dve_done, now(dve_done))
                dve.scalar_tensor_tensor(out=prob[:, hf, :], in0=bias[:, hf, :], scalar=slope,
                                         in1=banks(2 * (g % 2)),
                                         op0=ALU.mult, op1=ALU.add).then_inc(dve_done, 1)
                step(dve_done, "swa_s", n, hf)
                dve.wait_ge(dve_done, now(dve_done))
                dve.tensor_reduce(m, s3, AX_X, ALU.max).then_inc(dve_done, 1)
                step(dve_done)
                dve.wait_ge(dve_done, now(dve_done))
                dve.tensor_scalar(m, m, small[:, SINK + n:SINK + n + 1], -1.0, ALU.max, ALU.mult).then_inc(dve_done, 1)
                step(dve_done, "swa_mx", n, hf)

            def weights(n, hf):
                r = small[:, RI + 4 * hf:RI + 4 * hf + 4]
                dve.wait_ge(act_done, at("swa_se", n, hf))
                dve.wait_ge(act_done, at("swa_e", n, hf))
                dve.wait_ge(dve_done, now(dve_done))
                dve.tensor_tensor(r, r, small[:, RS + 4 * hf:RS + 4 * hf + 4], ALU.add).then_inc(dve_done, 1)
                step(dve_done)
                dve.wait_ge(dve_done, now(dve_done))
                dve.reciprocal(r, r).then_inc(dve_done, 1)
                step(dve_done)
                for b in range(NQ):
                    c = RI + 4 * hf + b
                    p = prob[:, hf, b * 2 * P:(b + 1) * 2 * P]
                    dve.wait_ge(dve_done, now(dve_done))
                    dve.tensor_scalar(p, p, small[:, c:c + 1], None, ALU.mult).then_inc(dve_done, 1)
                    step(dve_done, "swa_p", n, hf)

            steps = [(n, hf) for n in range(SWA_HEADS) for hf in range(2)]
            for x in range(len(steps) + 1):
                if x < len(steps):
                    probs(*steps[x])
                if x:
                    turned(*steps[x - 1])
                    finish(*steps[x - 1])
                if x < len(steps):
                    weights(*steps[x])

            def diff_probs(j, i):
                w = (i + 1) * P
                for m in (1, 0):
                    mx = small[:, MX + m:MX + m + 1]
                    dve.wait_ge(pe_done, at("diff_S", j, i, m))
                    if m == 0:
                        if i or j:
                            dve.wait_ge(pe_done, at("diff_T", (8 * j + i - 1) // 8, (i - 1) % 8))
                        else:
                            dve.wait_ge(pe_done, at("swa_T", SWA_HEADS - 1, 1))
                    dve.wait_ge(dve_done, now(dve_done))
                    dve.tensor_tensor_reduce(out=prob[:, m, 0:w], in0=banks(2 * m)[:, 0:w],
                                             in1=bias[:, 1, T - w:], scale=1.0, scalar=MASKED * 1e3,
                                             op0=ALU.add, op1=ALU.max, accum_out=mx).then_inc(dve_done, 1)
                    step(dve_done, "diff_s", j, i, m)
                    dve.wait_ge(dve_done, now(dve_done))
                    dve.tensor_scalar(mx, mx, -1.0, None, ALU.mult).then_inc(dve_done, 1)
                    step(dve_done, "diff_mx", j, i, m)

            def diff_weights(j, i):
                w = (i + 1) * P
                r = small[:, RI:RI + 2]
                dve.wait_ge(act_done, at("diff_e", j, i, 0))
                dve.wait_ge(act_done, at("diff_e", j, i, 1))
                dve.wait_ge(dve_done, now(dve_done))
                dve.reciprocal(r, small[:, RS:RS + 2]).then_inc(dve_done, 1)
                step(dve_done)
                dve.wait_ge(dve_done, now(dve_done))
                dve.tensor_scalar(small[:, RI + 1:RI + 2], small[:, RI + 1:RI + 2],
                                  small[:, LAMS:LAMS + 1], None, ALU.mult).then_inc(dve_done, 1)
                step(dve_done)
                dve.wait_ge(dve_done, now(dve_done))
                dve.tensor_scalar(prob[:, 0, 0:w], prob[:, 0, 0:w], small[:, RI:RI + 1], None, ALU.mult).then_inc(dve_done, 1)
                step(dve_done)
                dve.wait_ge(dve_done, now(dve_done))
                dve.scalar_tensor_tensor(out=prob[:, 0, 0:w], in0=prob[:, 1, 0:w],
                                         scalar=small[:, RI + 1:RI + 2], in1=prob[:, 0, 0:w],
                                         op0=ALU.mult, op1=ALU.add).then_inc(dve_done, 1)
                step(dve_done, "diff_a", j, i)

            def diff_turned(j, i):
                w = (i + 1) * P
                dve.wait_ge(act_done, at("diff_hi", j, i))
                dve.wait_ge(dve_done, now(dve_done))
                dve.tensor_tensor(aT[:, 1, 0:w], banks(4)[:, 0:w], aT[:, 0, 0:w].bitcast(F32), ALU.subtract).then_inc(dve_done, 1)
                step(dve_done, "diff_lo", j, i)

            def diff_finish(j, hf):
                t = slice(hf * HALF, (hf + 1) * HALF)
                dve.wait_ge(act_done, at("diff_r", j, hf))
                dve.wait_ge(dve_done, now(dve_done))
                dve.scalar_tensor_tensor(out=d_o[:, 1, :], in0=PS[:, 6, :], scalar=small[:, SUBG:SUBG + 1],
                                         in1=d_o[:, 0, :], op0=ALU.mult, op1=ALU.mult).then_inc(dve_done, 1)
                step(dve_done, "diff_o", j, hf)
                dve.wait_ge(act_done, at("diff_ohi", j, hf))
                dve.wait_ge(dve_done, now(dve_done))
                dve.tensor_tensor(opA[:, 1, 4 + j, t], d_o[:, 1, :], opA[:, 0, 4 + j, t].bitcast(F32),
                                  ALU.subtract).then_inc(dve_done, 1)
                step(dve_done, "diff_olo", j, hf)
                names[("diff_out", j, hf)] = names[("diff_olo", j, hf)]

            steps = [(j, i) for j in range(DIFF_HEADS) for i in range(NT)]
            for x in range(len(steps) + 2):
                if x < len(steps):
                    if steps[x][1] == 0:
                        dve.wait_ge(pool_done, at("bias_d"))
                        dve.wait_ge(dve_done, now(dve_done))
                        dve.tensor_scalar(bias[:, 1, :], bias[:, 1, :], 0.25, None, ALU.mult).then_inc(dve_done, 1)
                        step(dve_done)
                    diff_probs(*steps[x])
                if 1 <= x <= len(steps):
                    diff_turned(*steps[x - 1])
                if x >= 2 and (x - 2) % NQ == NQ - 1:
                    diff_finish(steps[x - 2][0], steps[x - 2][1] // NQ)
                if x < len(steps):
                    diff_weights(*steps[x])
            names[("att_end", 1)] = names[("att_end2", 1)] = now(dve_done)

        @block.sync
        def _(sp):
            sp.wait_ge(dve_done, at("vec_zero"))
            for t, rs in enumerate((ROWS0, ROWS1, ROWS2)):
                r = 0
                for n, many in rs:
                    v = a[n]
                    dims = " ".join(f"d{i}" for i in range(len(v.shape)))
                    v = v.rearrange(f"{dims} -> ({dims})").rearrange("(r p) -> r p", p=P)
                    sp.dma_start(vec_rows[r:r + many, t, :], v).then_inc(vec_in, 16)
                    step(vec_in, "vec_in", by=16)
                    r += many
            sp.dma_start(small[:, SINK:SINK + 8], a["swa_sinks_2"].to_broadcast([P, 8])).then_inc(vec_in, 16)
            step(vec_in, "vec_in", by=16)
            sp.dma_start(M[0][:, 0:256], a["diff_lambda_2"].rearrange("o f d -> o (f d)").to_broadcast([P, 256])).then_inc(vec_in, 16)
            step(vec_in, "vec_in", by=16)
            for tb in range(NT):
                sp.dma_start(x_rows[:, tb, :], a["x"][0, tb * P:(tb + 1) * P, :]).then_inc(x_in[tb], 16)
                step(x_in[tb], "x_in", tb, by=16)

            mod_n = [0]

            def mod_loads(g):
                name, part, _ = MODS[g]
                w = a[name]
                if len(w.shape) == 3:
                    w = w[0]
                for kc in range(KC):
                    for h in range(2):
                        n = mod_n[0]
                        if not (n < 2):
                            sp.wait_ge(dve_done, at("mod_step", n - 2))
                        sp.dma_start(mod_raw[:, n % 2, :],
                                     w[kc * P:(kc + 1) * P, part * D + h * HALF:part * D + (h + 1) * HALF]).then_inc(mod_in[n % 2], 16)
                        step(mod_in[n % 2], "mod_in", n, by=16)
                        mod_n[0] += 1

            def weights(u):
                if not (u < 2):
                    sp.wait_ge(pool_done, at("split", u - 2))
                for n, (w, col0, row0, chunks, k0) in enumerate(source(u)):
                    src = w[row0:row0 + chunks * P, col0:col0 + P].rearrange("(k p) n -> p k n", p=P)
                    sp.dma_start(w_raw[:, u % 2, k0:k0 + chunks, :], src).then_inc(w_in[u % 2], 16)
                    step(w_in[u % 2], "w_in", u, by=16)

            def spill(n):
                sp.wait_ge(dve_done, at("x_free", n))
                sp.dma_start(x_dram, X[:].rearrange("p k t -> p (k t)")).then_inc(x_moved, 16)
                step(x_moved, "x_out", n, by=16)

            def reload(n):
                sp.wait_ge(x_moved, at("x_out", n))
                sp.wait_ge(dve_done, at("att_end", n))
                sp.wait_ge(dve_done, at("att_end2", n))
                sp.dma_start(X[:].rearrange("p k t -> p (k t)"), x_dram).then_inc(x_moved, 16)
                step(x_moved, "x_back", n, by=16)

            def head_loads(h):
                s = h % 2
                if h >= 2:
                    sp.wait_ge(pe_done, at("stick_free", h - 2))
                for u in (U_KV + KC - 1, U_KV + KC - 2, U_QZ + KC - 1, U_QZ + KC - 2):
                    sp.wait_ge(stored[u % 2], at("stored", u))
                for u in (U_KV + 2 * KC - 1, U_KV + 2 * KC - 2):
                    sp.wait_ge(v_stored[u % 2], at("v_stored", u))
                rows = slice(h * DH, (h + 1) * DH)
                key = f"head_in{s}"
                hi_at = slice(DH * (h % 2), DH * (h % 2) + DH)
                lo_at = slice(DH * (1 - h % 2), DH * (1 - h % 2) + DH)
                sp.dma_start(hin[hi_at, s, 0, :].bitcast(F32), k_dram[0, rows, :]).then_inc(head_in[h % 2], 16)
                step(head_in[h % 2], "head_in", h, by=16)
                sp.dma_start(hin[lo_at, s, 0, :].bitcast(F32), k_dram[1, rows, :]).then_inc(head_in[h % 2], 16)
                step(head_in[h % 2], "head_in", h, by=16)
                for part in range(2):
                    for place in (hi_at, lo_at):
                        sp.dma_start(hin[place, s, 1 + part, :].bitcast(F32), q_dram[part, rows, :]).then_inc(head_in[h % 2], 16)
                        step(head_in[h % 2], "head_in", h, by=16)
                sp.dma_start(hin[:, s, 3, :].bitcast(F32), v_dram[h // 2, :, h % 2, :]).then_inc(head_in[h % 2], 16)
                step(head_in[h % 2], "head_in", h, by=16)

            for g in (0, 1):
                mod_loads(g)
            weights(0)
            weights(1)
            for u in range(2, len(UNITS)):
                if u == U_BOUT:
                    spill(0)
                    for h in range(HEADS):
                        head_loads(h)
                    reload(0)
                if u == U_BRANCH:
                    spill(1)
                    second_loads(sp)
                if u == U_BRANCH + 4:
                    reload(1)
                weights(u)
                if u >= U_AIN + 3 and (u - 3) % 4 == 0 and (u - 3) // 4 < KC:
                    for g in MODS_AT[(u - 3) // 4]:
                        mod_loads(g)

        @block.gpsimd
        def _(pool):
            pool.wait_ge(pool_done, now(pool_done))
            pool.memset(ident[:], 0.0).then_inc(pool_done, 1)
            step(pool_done)
            pool.wait_ge(pool_done, now(pool_done))
            pool.affine_select(out=ident[:], in_=ident[:], compare_op=ALU.not_equal, fill=1.0, base=0,
                               pattern=[[-1, P]], channel_multiplier=1).then_inc(pool_done, 1)
            step(pool_done)
            pool.wait_ge(pool_done, now(pool_done))
            pool.memset(ones[:], 1.0).then_inc(pool_done, 1)
            step(pool_done)
            pool.wait_ge(pool_done, now(pool_done))
            pool.memset(small[:, EPS_COL:EPS_COL + 1], EPS).then_inc(pool_done, 1)
            step(pool_done, "consts")

            def split(u):
                s = u % 2
                chunks = UNITS[u][3]
                raw, hi, lo = w_raw[:, s, 0:chunks], w_hi[:, s, 0:chunks], w_lo[:, s, 0:chunks]
                pool.wait_ge(w_in[u % 2], at("w_in", u))
                if u >= 2:
                    pool.wait_ge(pe_done, at("unit", u - 2, 1))
                pool.wait_ge(pool_done, now(pool_done))
                pool.tensor_copy(hi, raw).then_inc(pool_done, 1)
                step(pool_done)
                pool.wait_ge(pool_done, now(pool_done))
                pool.tensor_tensor(lo, raw, hi.bitcast(F32), ALU.subtract).then_inc(pool_done, 1)
                step(pool_done, "split", u)

            def stick_pool():
                pool.wait_ge(x_moved, at("x_out", 0))
                pool.wait_ge(pool_done, now(pool_done))
                pool.memset(tri[:], -1.0).then_inc(pool_done, 1)
                step(pool_done)
                pool.wait_ge(pool_done, now(pool_done))
                pool.affine_select(out=tri[:], in_=tri[:], compare_op=ALU.is_ge, fill=0.0, base=0,
                                   pattern=[[-1, P]], channel_multiplier=1).then_inc(pool_done, 1)
                step(pool_done)
                pool.wait_ge(pool_done, now(pool_done))
                pool.memset(nones[:], -1.0).then_inc(pool_done, 1)
                step(pool_done)
                pool.wait_ge(pool_done, now(pool_done))
                pool.memset(masks[:], 0.0).then_inc(pool_done, 1)
                step(pool_done)
                pool.wait_ge(pool_done, now(pool_done))
                pool.affine_select(out=masks[:], in_=masks[:], compare_op=ALU.is_gt, fill=MASKED, base=0,
                                   pattern=[[1, P]], channel_multiplier=-1).then_inc(pool_done, 1)
                step(pool_done)
                pool.wait_ge(pool_done, now(pool_done))
                pool.tensor_copy(mask_r[:], masks[:]).then_inc(pool_done, 1)
                step(pool_done)
                pool.wait_ge(pool_done, now(pool_done))
                pool.tensor_copy(ident_r[:], ident[:]).then_inc(pool_done, 1)
                step(pool_done, "stick_consts")
                for h in range(HEADS):
                    for i, (hf, kb) in enumerate(STICK):
                        g = h * len(STICK) + i
                        qs = max(0, (kb - NQ * hf) * P)
                        if kb == NQ * hf + NQ - 1:
                            if g:
                                pool.wait_ge(pe_done, at("stick_b", g - 1))
                            pool.wait_ge(pool_done, now(pool_done))
                            pool.memset(s_p[:, :, :], 0.0).then_inc(pool_done, 1)
                            step(pool_done)
                        if kb > 0:
                            pool.wait_ge(dve_done, at("stick_sp", g))
                            if g:
                                pool.wait_ge(pe_done, at("stick_b", g - 1))
                            pool.wait_ge(pool_done, now(pool_done))
                            pool.tensor_tensor(s_p[:, g % 2, qs:], s_p[:, 1 - g % 2, qs:],
                                               s_sp[:, g % 2, qs:], ALU.add).then_inc(pool_done, 1)
                            step(pool_done, "stick_p", g)

            def second_pool():
                far = MASKED * 256
                for hf in range(2):
                    w = bias[:, hf, :].rearrange("p (b k) -> p b k", b=NQ)
                    pool.wait_ge(x_moved, at("x_out", 1))
                    pool.wait_ge(pool_done, now(pool_done))
                    pool.iota(w, pattern=[[0, NQ], [1, 2 * P]], base=-P, channel_multiplier=-1,
                              allow_small_or_imprecise_dtypes=True).then_inc(pool_done, 1)
                    step(pool_done)
                    pool.wait_ge(pool_done, now(pool_done))
                    pool.affine_select(out=w, in_=w, compare_op=ALU.is_ge, fill=far, base=P,
                                       pattern=[[0, NQ], [-1, 2 * P]], channel_multiplier=1).then_inc(pool_done, 1)
                    step(pool_done)
                    pool.wait_ge(pool_done, now(pool_done))
                    pool.affine_select(out=w, in_=w, compare_op=ALU.is_gt, fill=far, base=0,
                                       pattern=[[0, NQ], [1, 2 * P]], channel_multiplier=-1).then_inc(pool_done, 1)
                    step(pool_done, "bias_w", hf)
                pool.wait_ge(pool_done, now(pool_done))
                pool.memset(bias[:, 0, 0:P], far).then_inc(pool_done, 1)
                step(pool_done, "bias_w", 0)
                row = bias[:, 1, :]
                pool.wait_ge(dve_done, at("swa_s", SWA_HEADS - 1, 1))
                pool.wait_ge(pool_done, now(pool_done))
                pool.iota(row, pattern=[[1, T]], base=-(T - P), channel_multiplier=-1,
                          allow_small_or_imprecise_dtypes=True).then_inc(pool_done, 1)
                step(pool_done)
                pool.wait_ge(pool_done, now(pool_done))
                pool.affine_select(out=row, in_=row, compare_op=ALU.is_ge, fill=MASKED * 256,
                                   base=T - P, pattern=[[-1, T]], channel_multiplier=1).then_inc(pool_done, 1)
                step(pool_done, "bias_d")

            for u in range(len(UNITS)):
                if u == U_BOUT:
                    stick_pool()
                if u == U_BRANCH:
                    second_pool()
                split(u)

        @block.tensor
        def _(pe):
            def product(ps, hi_w, lo_w, rhs, chunks, k0, name, ready=None, hf=0):
                for k in range(chunks):
                    if ready is not None:
                        pe.wait_ge(dve_done, at("h_" + ready, k, hf))
                    for n, (w, part) in enumerate(((hi_w, 0), (lo_w, 0), (hi_w, 1))):
                        ins = pe.matmul(ps, w[:, k0 + k, :], rhs(part, k0 + k), start=(k == 0 and n == 0),
                                        stop=(k == chunks - 1 and n == 2))
                ins.then_inc(pe_done, 1)
                step(pe_done, *(name or ()))

            def unit(u, op_in, ready=None):
                s = u % 2
                pe.wait_ge(pool_done, at("split", u))
                if u >= 2:
                    pe.wait_ge(reader(u - 2), at("free", u - 2))
                for hf in range(2):
                    rhs = lambda part, k: op_in[:, part, k, hf * HALF:(hf + 1) * HALF]
                    product(PS[:, 2 * s + hf, :], w_hi[:, s], w_lo[:, s], rhs, UNITS[u][3], 0, ("unit", u, hf), ready, hf)

            def norm_sum(n):
                for hf in range(2):
                    pe.wait_ge(dve_done, at("ssum", n))
                    pe.wait_ge(pool_done, at("consts"))
                    if n in MISC_FREE:
                        pe.wait_ge(act_done, at("rstd", MISC_FREE[n], 1))
                    pe.matmul(PS[:, 4 + hf, :], ones[:], M[1][:, hf * HALF:(hf + 1) * HALF], start=True, stop=True).then_inc(pe_done, 1)
                    step(pe_done, "norm_sum", n, hf)

            def mod_sum(g):
                pe.wait_ge(dve_done, at("mod_acc", g))
                if g:
                    pe.wait_ge(dve_done, at("mod_out", g - 1))
                for j in range(KC):
                    ins = pe.matmul(PS[:, 6, j:j + 1], mod_acc[:, j * P:(j + 1) * P], ones[:, 0:1], start=True, stop=True)
                ins.then_inc(pe_done, 1)
                step(pe_done, "mod_sum", g)

            pe.wait_ge(pool_done, at("consts"))
            pe.wait_ge(vec_in, at("vec_in"))
            for t in range(3):
                ins = pe.transpose(PS[:, 7, t * P:(t + 1) * P], vec_rows[:, t, :], ident[:])
            ins.then_inc(pe_done, 1)
            step(pe_done, "vec_T")
            for j in range(KC):
                for hf in range(2):
                    n = 2 * j + hf
                    if n >= 4:
                        pe.wait_ge(act_done, at("x_set", n - 4))
                    for b in range(4):
                        pe.wait_ge(x_in[(4 * hf + b)], at("x_in", 4 * hf + b))
                    for b in range(4):
                        ins = pe.transpose(PS[:, n % 4, b * P:(b + 1) * P],
                                           x_rows[:, 4 * hf + b, j * P:(j + 1) * P], ident[:])
                    ins.then_inc(pe_done, 1)
                    step(pe_done, "x_T", n)
            for g in (0, 1):
                mod_sum(g)
            norm_sum("a")
            pe.wait_ge(act_done, at("x_set", 15))
            for j in range(KC):
                for q in range(4):
                    u = U_AIN + 4 * j + q
                    unit(u, opA, "a" if j == 0 and q == 0 else None)
                    if q == 1 and j and len(MODS_AT[j - 1]) > 1:
                        mod_sum(MODS_AT[j - 1][1])
                    if q == 3:
                        mod_sum(MODS_AT[j][0])
            for n in range(KC):
                pe.wait_ge(dve_done, at("y", KC - 1, 1))
                unit(U_AOUT + n, opB)
            norm_sum("kv")
            for n in range(2 * KC):
                unit(U_KV + n, opA, "kv" if n == 0 else None)
                if n > KC:
                    turn_v(pe, U_KV + n - 1)
            turn_v(pe, U_KV + 2 * KC - 1)
            for n in range(2 * KC):
                unit(U_QZ + n, opA, "b" if n == 0 else None)
            stick_pe(pe)
            for n in range(KC):
                pe.wait_ge(dve_done, at("stick_out", HEADS // 2 - 1, 1))
                unit(U_BOUT + n, opA)
            norm_sum("fin1")
            norm_sum("n1")
            for n in range(34):
                unit(U_IN2 + n, opA, "n1" if n == 0 else None)
                if 13 < n <= 18:
                    turn_v(pe, U_IN2 + n - 1)
            second_pe(pe)
            for n in range(KC):
                u = U_BRANCH + n
                s = u % 2
                pe.wait_ge(pool_done, at("split", u))
                if u >= 2:
                    pe.wait_ge(reader(u - 2), at("free", u - 2))
                pe.wait_ge(dve_done, at("diff_out", DIFF_HEADS - 1, 1))
                pe.wait_ge(dve_done, at("swa_out", 3, 1))
                for hf in range(2):
                    rhs = lambda part, k: opA[:, part, k, hf * HALF:(hf + 1) * HALF]
                    product(PS[:, 2 * s + hf, :], w_hi[:, s], w_lo[:, s], rhs, 4, 0, ("unit_a", u, hf))
                    product(PS[:, 4 + 2 * s + hf, :], w_hi[:, s], w_lo[:, s], rhs, 4, 4, ("unit", u, hf))
            for n in range(KC):
                pe.wait_ge(dve_done, at("merged", KC - 1, 1))
                unit(U_OUT2 + n, opB)
            norm_sum("n2")
            u = U_FFN
            for first, many in FGROUPS:
                for f in range(2 * many):
                    unit(u, opA, "n2" if u == U_FFN else None)
                    u += 1
                for n in range(KC):
                    pe.wait_ge(dve_done, at("ff", first + many - 1, 1))
                    unit(u, opB)
                    u += 1
            norm_sum("fin2")
            for tb in range(NT):
                pe.wait_ge(dve_done, at("x_fin2", KC - 1))
                if tb >= 2:
                    pe.wait_ge(dve_done, at("row_out", tb - 2))
                pe.wait_ge(reader(len(UNITS) - 1), at("free", len(UNITS) - 1))
                pe.wait_ge(reader(len(UNITS) - 2), at("free", len(UNITS) - 2))
                for j in range(KC):
                    ins = pe.transpose(PS[:, 2 * (tb % 2) + j // 4, (j % 4) * P:(j % 4 + 1) * P],
                                       X[:, j, tb * P:(tb + 1) * P], ident[:])
                ins.then_inc(pe_done, 1)
                step(pe_done, "row_T", tb)

        @block.scalar
        def _(act):
            def act_norm(n, shift, x_free=None):
                for hf in range(2):
                    r = M[1][:, hf * HALF:(hf + 1) * HALF]
                    act.wait_ge(pe_done, at("norm_sum", n, hf))
                    act.wait_ge(pe_done, at("norm_sum", n, 1))
                    act.wait_ge(act_done, now(act_done))
                    act.activation(r, PS[:, 4 + hf, :], ACT.Ln, bias=small[:, EPS_COL:EPS_COL + 1],
                                   scale=1.0 / D).then_inc(act_done, 1)
                    step(act_done)
                    act.wait_ge(act_done, now(act_done))
                    act.activation(r, r, ACT.Exp, scale=-0.5).then_inc(act_done, 1)
                    step(act_done, "rstd", n, hf)

            def act_parts(n, shift):
                for hf in range(2):
                    for j in range(KC):
                        x = hf * KC + j
                        s = x % 2
                        act.wait_ge(dve_done, at("xn", n, x))
                        if x >= 2:
                            act.wait_ge(dve_done, at("lo", n, x - 2))
                        act.wait_ge(act_done, now(act_done))
                        act.activation(hn[:, s, :], xn[:, s, :], ACT.Identity, bias=mod[:, shift, j:j + 1],
                                       scale=small[:, GS + j:GS + j + 1]).then_inc(act_done, 1)
                        step(act_done, "hn", n, x)
                        act.wait_ge(act_done, now(act_done))
                        act.activation(opA[:, 0, j, hf * HALF:(hf + 1) * HALF], hn[:, s, :], ACT.Copy).then_inc(act_done, 1)
                        step(act_done, "hi", n, x)

            def square(n, j):
                slot = M[0] if j % 2 == 0 else M[2]
                if n != "a":
                    act.wait_ge(dve_done, at("x_new", n, j))
                if j >= 2:
                    act.wait_ge(dve_done, at("sq_add", n, j - 2))
                else:
                    act.wait_ge(dve_done, at("lam_sum"))
                act.wait_ge(act_done, now(act_done))
                act.activation(slot[:], X[:, j, :], ACT.Square).then_inc(act_done, 1)
                step(act_done, "sq", n, j)

            act.wait_ge(dve_done, at("cols"))
            act.wait_ge(act_done, now(act_done))
            act.activation(small[:, SILU_C:SILU_C + 16], cols[:, 0:16], ACT.Silu).then_inc(act_done, 1)
            step(act_done, "silu_c")
            for j in range(KC):
                for hf in range(2):
                    n = 2 * j + hf
                    act.wait_ge(pe_done, at("x_T", n))
                    act.wait_ge(act_done, now(act_done))
                    act.activation(X[:, j, hf * HALF:(hf + 1) * HALF], PS[:, n % 4, :], ACT.Copy).then_inc(act_done, 1)
                    step(act_done, "x_set", n)
                square("a", j)
            act.wait_ge(dve_done, at("lam_sum"))
            act.wait_ge(act_done, now(act_done))
            act.activation(small[:, LAM + 2:LAM + 4], small[:, LAM:LAM + 2], ACT.Exp).then_inc(act_done, 1)
            step(act_done, "lam_exp")
            act_norm("a", A_SHIFT)
            act_parts("a", A_SHIFT)
            for j in range(KC):
                u = U_AIN + 4 * j
                for hf in range(2):
                    act.wait_ge(pe_done, at("unit", u, 1))
                    if j:
                        act.wait_ge(dve_done, at("yz", j - 1, hf))
                    act.wait_ge(act_done, at("hi", "a", 15))
                    act.wait_ge(dve_done, at("lo", "a", 15))
                    act.wait_ge(act_done, now(act_done))
                    act.activation(cs[:, hf, :], PS[:, 2 * (u % 2) + hf, :], ACT.Copy).then_inc(act_done, 1)
                    step(act_done, "cs", j, hf)
                names[("free", u)] = names[("cs", j, 1)]
                for hf in range(2):
                    act.wait_ge(pe_done, at("unit", u + 3, 1))
                    act.wait_ge(dve_done, at("cu", j, hf))
                    act.wait_ge(act_done, now(act_done))
                    act.activation(cs[:, hf, :], PS[:, 2 * ((u + 3) % 2) + hf, :], ACT.Silu).then_inc(act_done, 1)
                    step(act_done, "sz", j, hf)
                names[("free", u + 3)] = names[("sz", j, 1)]
                for hf in range(2):
                    act.wait_ge(dve_done, at("yz", j, hf))
                    act.wait_ge(act_done, now(act_done))
                    act.activation(opB[:, 0, j, hf * HALF:(hf + 1) * HALF], yt[:, hf, :], ACT.Copy).then_inc(act_done, 1)
                    step(act_done, "yh", j, hf)
            for n in range(KC):
                square("kv", n)
            act_norm("kv", KV_SHIFT)
            act_parts("kv", KV_SHIFT)

            def act_hl(u, x, scale, dram, row0, name):
                s = u % 2
                act.wait_ge(pe_done, at("unit", u, 1))
                if x >= 2:
                    act.wait_ge(stored[(u - 2) % 2], at("stored", u - 2))
                else:
                    if U_QZ <= u < U_BOUT:
                        act.wait_ge(stored[(U_KV + KC - 2 + x) % 2], at("stored", U_KV + KC - 2 + x))
                act.wait_ge(act_done, now(act_done))
                act.activation(stage[:, x % 2, 0, :], banks(2 * s), ACT.Copy, scale=scale).then_inc(act_done, 1)
                step(act_done, "hl_hi", u)

            def store_hl(u, x, dram, row0):
                act.wait_ge(dve_done, at("hl_lo", u))
                act.wait_ge(act_done, at("hl_hi", u))
                act.dma_start(dram[:, row0:row0 + P, :].rearrange("c p t -> p c t"), stage[:, x % 2, :, :].bitcast(F32)).then_inc(stored[u % 2], 16)
                step(stored[u % 2], "stored", u, by=16)

            def act_v(u, x):
                s = u % 2
                act.wait_ge(pe_done, at("unit", u, 1))
                if not (u in FIRST_V):
                    act.wait_ge(pe_done, at("v_T", u - 1))
                if u < U_IN2:
                    act.wait_ge(dve_done, at("norm_end"))
                else:
                    act.wait_ge(dve_done, at("x_free", 1))
                act.wait_ge(act_done, now(act_done))
                act.activation(vt[:], banks(2 * s), ACT.Copy).then_inc(act_done, 1)
                step(act_done, "vt", u)
                names[("free", u)] = names[("vt", u)]

            def act_v_hi(u, x, kind):
                s = u % 2
                src = PS[:, 4:6, :].rearrange("p b (k e d) -> p (b k) e d", k=4, e=2)
                if kind == "stick" or kind == "swa":
                    for e in range(2):
                        place = 0 if kind == "swa" else e
                        dst = vstage[:, s, e, :].rearrange("p (k s d) -> p k s d", k=NT, s=2)[:, :, place, :]
                        act.wait_ge(pe_done, at("v_T", u))
                        if x >= 2:
                            act.wait_ge(v_stored[(u - 2) % 2], at("v_stored", u - 2))
                        act.wait_ge(act_done, now(act_done))
                        act.activation(dst, src[:, :, e, :], ACT.Copy).then_inc(act_done, 1)
                        step(act_done, "v_hi", u)
                else:
                    act.wait_ge(pe_done, at("v_T", u))
                    if x >= 2:
                        act.wait_ge(v_stored[(u - 2) % 2], at("v_stored", u - 2))
                    act.wait_ge(act_done, now(act_done))
                    act.activation(vstage[:, s, 0, :], banks(4), ACT.Copy).then_inc(act_done, 1)
                    step(act_done, "v_hi", u)

            def store_v(u, x, dst):
                act.wait_ge(dve_done, at("v_split", u))
                act.dma_start(dst, vstage[:, u % 2, :, :].bitcast(F32)).then_inc(v_stored[u % 2], 16)
                step(v_stored[u % 2], "v_stored", u, by=16)

            for n in range(KC):
                act_hl(U_KV + n, n, 1.0, k_dram, n * P, "k")
                if n:
                    store_hl(U_KV + n - 1, n - 1, k_dram, (n - 1) * P)
            store_hl(U_KV + KC - 1, KC - 1, k_dram, (KC - 1) * P)
            for n in range(KC):
                act_v(U_KV + KC + n, n)
                act_v_hi(U_KV + KC + n, n, "stick")
                store_v(U_KV + KC + n, n, v_dram[n])
            act_parts("b", B_SHIFT)
            for n in range(KC):
                act_hl(U_QZ + n, n, QSCALE, q_dram, n * P, "q")
                if n:
                    store_hl(U_QZ + n - 1, n - 1, q_dram, (n - 1) * P)
            store_hl(U_QZ + KC - 1, KC - 1, q_dram, (KC - 1) * P)
            for n in range(KC):
                u = U_QZ + KC + n
                s = u % 2
                act.wait_ge(pe_done, at("unit", u, 1))
                act.wait_ge(act_done, now(act_done))
                act.activation(sz[:, n, :], banks(2 * s), ACT.Silu).then_inc(act_done, 1)
                step(act_done, "free", u)
            stick_act(act)
            for n in range(KC):
                square("fin1", n)
            act_norm("fin1", None)
            for n in range(KC):
                square("n1", n)
            act_norm("n1", SHIFT1)
            act_parts("n1", SHIFT1)
            dst = [(q2_dram, n * P) for n in range(8)] + [(k2_dram, n * P) for n in range(5)]
            for n in range(13):
                act_hl(U_IN2 + n, n, QSCALE if n < 8 else 1.0, None, None, None)
                if n:
                    store_hl(U_IN2 + n - 1, n - 1, *dst[n - 1])
            store_hl(U_IN2 + 12, 12, *dst[12])
            for n in range(5):
                u = U_IN2 + 13 + n
                act_v(u, n)
                act_v_hi(u, n, "diff" if n else "swa")
                store_v(u, n, va_dram if n == 0 else vd_dram[n - 1])
            for n in range(16):
                u = U_IN2 + 18 + n
                s = u % 2
                act.wait_ge(pe_done, at("unit", u, 1))
                act.wait_ge(stored[(U_IN2 + 12) % 2], at("stored", U_IN2 + 12))
                act.wait_ge(stored[(U_IN2 + 11) % 2], at("stored", U_IN2 + 11))
                act.wait_ge(v_stored[(U_IN2 + 17) % 2], at("v_stored", U_IN2 + 17))
                act.wait_ge(v_stored[(U_IN2 + 16) % 2], at("v_stored", U_IN2 + 16))
                act.wait_ge(act_done, now(act_done))
                act.activation(gates[:, n, :], banks(2 * s), ACT.Sigmoid).then_inc(act_done, 1)
                step(act_done, "free", u)
            second_act(act)
            for n in range(KC):
                for hf in range(2):
                    act.wait_ge(dve_done, at("mz", n, hf))
                    act.wait_ge(act_done, now(act_done))
                    act.activation(opB[:, 0, n, hf * HALF:(hf + 1) * HALF], d_o[:, hf, :], ACT.Copy).then_inc(act_done, 1)
                    step(act_done, "mh", n, hf)
            for n in range(KC):
                square("n2", n)
            act_norm("n2", SHIFT2)
            act_parts("n2", SHIFT2)
            u = U_FFN
            for first, many in FGROUPS:
                for f in range(first, first + many):
                    for hf in range(2):
                        act.wait_ge(pe_done, at("unit", u, 1))
                        if f:
                            act.wait_ge(dve_done, at("fconv", f - 1, 1))
                        else:
                            act.wait_ge(dve_done, at("lo", "n2", 15))
                        act.wait_ge(act_done, now(act_done))
                        act.activation(M[0][:, hf * HALF:(hf + 1) * HALF], PS[:, 2 * (u % 2) + hf, :],
                                       ACT.Copy).then_inc(act_done, 1)
                        step(act_done, "fa", f, hf)
                    names[("free", u)] = names[("fa", f, 1)]
                    for hf in range(2):
                        act.wait_ge(dve_done, at("fconv", f, hf))
                        act.wait_ge(act_done, now(act_done))
                        act.activation(yt[:, hf, :], yt[:, hf, :], ACT.Gelu).then_inc(act_done, 1)
                        step(act_done, "fg", f, hf)
                    for hf in range(2):
                        act.wait_ge(dve_done, at("fz", f, hf))
                        if first:
                            act.wait_ge(pe_done, at("unit", U_FFN + 2 * first + KC * FGROUPS.index((first, many)) - 1, 1))
                        act.wait_ge(act_done, now(act_done))
                        act.activation(opB[:, 0, f - first, hf * HALF:(hf + 1) * HALF], yt[:, hf, :],
                                       ACT.Copy).then_inc(act_done, 1)
                        step(act_done, "fh", f, hf)
                    u += 2
                u += KC
            for n in range(KC):
                square("fin2", n)
            act_norm("fin2", None)
            for tb in range(NT):
                act.wait_ge(dve_done, at("row_out", tb))
                act.dma_start(out[0, tb * P:(tb + 1) * P, :], M[tb % 4 + 1][:]).then_inc(row_gone[tb % 4], 16)
                step(row_gone[tb % 4], "row_gone", tb, by=16)
            for tb in range(NT - 4, NT):
                act.wait_ge(row_gone[tb % 4], at("row_gone", tb))

        @block.vector
        def _(dve):
            mod_n = [0]

            def mod_steps(g):
                src = SILU_C + 8 * MODS[g][2]
                for kc in range(KC):
                    for h in range(2):
                        n = mod_n[0]
                        acc = mod_acc[:, h * HALF:(h + 1) * HALF]
                        c = small[:, src + kc:src + kc + 1]
                        dve.wait_ge(mod_in[n % 2], at("mod_in", n))
                        dve.wait_ge(act_done, at("silu_c"))
                        if g:
                            dve.wait_ge(pe_done, at("mod_sum", g - 1))
                        if kc == 0:
                            dve.wait_ge(dve_done, now(dve_done))
                            dve.tensor_scalar(acc, mod_raw[:, n % 2, :], c, None, ALU.mult).then_inc(dve_done, 1)
                            step(dve_done, "mod_step", n)
                        else:
                            dve.wait_ge(dve_done, now(dve_done))
                            dve.scalar_tensor_tensor(out=acc, in0=mod_raw[:, n % 2, :], scalar=c, in1=acc,
                                                     op0=ALU.mult, op1=ALU.add).then_inc(dve_done, 1)
                            step(dve_done, "mod_step", n)
                        mod_n[0] += 1
                names[("mod_acc", g)] = names[("mod_step", mod_n[0] - 1)]

            def mod_out(g):
                name, part, _ = MODS[g]
                b = C[MOD_BIAS[name]] + part * KC
                dve.wait_ge(pe_done, at("mod_sum", g))
                dve.wait_ge(dve_done, now(dve_done))
                dve.tensor_tensor(mod[:, g, :], PS[:, 6, 0:KC], cols[:, b:b + KC], ALU.add).then_inc(dve_done, 1)
                step(dve_done, "mod_out", g)

            def gains(gname, scale):
                g = cols[:, C[gname]:C[gname] + KC]
                dve.wait_ge(dve_done, now(dve_done))
                dve.scalar_tensor_tensor(out=small[:, GS:GS + KC], in0=mod[:, scale, :], scalar=1.0, in1=g,
                                         op0=ALU.add, op1=ALU.mult).then_inc(dve_done, 1)
                step(dve_done)

            def sq_add(n, j):
                slot = M[0] if j % 2 == 0 else M[2]
                if j == 0:
                    dve.wait_ge(act_done, at("sq", n, j))
                    dve.wait_ge(dve_done, now(dve_done))
                    dve.tensor_copy(M[1][:], slot[:]).then_inc(dve_done, 1)
                    step(dve_done, "sq_add", n, j)
                else:
                    dve.wait_ge(act_done, at("sq", n, j))
                    dve.wait_ge(dve_done, now(dve_done))
                    dve.tensor_tensor(M[1][:], M[1][:], slot[:], ALU.add).then_inc(dve_done, 1)
                    step(dve_done, "sq_add", n, j)
                if j == KC - 1:
                    names[("ssum", n)] = names[("sq_add", n, j)]

            def parts(n, gname, scale, last_use):
                gains(gname, scale)
                for x in range(2 * KC + 1):
                    if x < 2 * KC:
                        hf, j = divmod(x, KC)
                        t = slice(hf * HALF, (hf + 1) * HALF)
                        dve.wait_ge(act_done, at("rstd", "kv" if n == "b" else n, hf))
                        if x >= 2:
                            dve.wait_ge(act_done, at("hn", n, x - 2))
                        if last_use is not None:
                            dve.wait_ge(pe_done, at(*last_use))
                        dve.wait_ge(dve_done, now(dve_done))
                        dve.tensor_tensor(xn[:, x % 2, :], X[:, j, t], M[1][:, t], ALU.mult).then_inc(dve_done, 1)
                        step(dve_done, "xn", n, x)
                    if x:
                        y = x - 1
                        hf, j = divmod(y, KC)
                        t = slice(hf * HALF, (hf + 1) * HALF)
                        dve.wait_ge(act_done, at("hi", n, y))
                        dve.wait_ge(dve_done, now(dve_done))
                        dve.tensor_tensor(opA[:, 1, j, t], hn[:, y % 2, :], opA[:, 0, j, t].bitcast(F32),
                                          ALU.subtract).then_inc(dve_done, 1)
                        step(dve_done, "lo", n, y)
                        names[("h_" + n, j, hf)] = names[("lo", n, y)]

            dve.wait_ge(dve_done, now(dve_done))
            dve.memset(vec_rows[:], 0.0).then_inc(dve_done, 1)
            step(dve_done, "vec_zero")
            dve.wait_ge(pe_done, at("vec_T"))
            dve.wait_ge(dve_done, now(dve_done))
            dve.tensor_copy(cols[:], PS[:, 7, 0:3 * P]).then_inc(dve_done, 1)
            step(dve_done, "cols")
            for i in range(2):
                dve.wait_ge(vec_in, at("vec_in"))
                dve.wait_ge(dve_done, now(dve_done))
                dve.tensor_tensor(M[0][:, 512 + 64 * i:576 + 64 * i], M[0][:, 128 * i:128 * i + 64],
                                  M[0][:, 128 * i + 64:128 * i + 128], ALU.mult).then_inc(dve_done, 1)
                step(dve_done)
            dve.wait_ge(dve_done, now(dve_done))
            dve.reduce_sum(small[:, LAM:LAM + 2], M[0][:, 512:640].rearrange("p (i d) -> p i d", i=2), AX_X).then_inc(dve_done, 1)
            step(dve_done, "lam_sum")
            for j in range(KC):
                sq_add("a", j)
            for g in (0, 1):
                mod_steps(g)
                mod_out(g)
            dve.wait_ge(act_done, at("lam_exp"))
            dve.wait_ge(dve_done, now(dve_done))
            dve.scalar_tensor_tensor(out=small[:, LAMS:LAMS + 1], in0=small[:, LAM + 3:LAM + 4],
                                     scalar=-LAM_INIT, in1=small[:, LAM + 2:LAM + 3], op0=ALU.add,
                                     op1=ALU.subtract).then_inc(dve_done, 1)
            step(dve_done)
            dve.wait_ge(dve_done, now(dve_done))
            dve.tensor_scalar(small[:, SUBG:SUBG + 1], cols[:, C["diff_subln_g_2"]:C["diff_subln_g_2"] + 1],
                              1.0 - LAM_INIT, None, ALU.mult).then_inc(dve_done, 1)
            step(dve_done)
            parts("a", "a_norm_g", A_SCALE, None)
            cw = C["a_conv_w"]

            def conv(src, w, j, kc, hf, bias_col, name):
                t0 = hf * HALF
                b = None if bias_col is None else cols[:, bias_col:bias_col + 1]
                o = yt[:, hf, :]
                w_of = lambda tap: cols[:, w + tap * kc + j:w + tap * kc + j + 1]
                if b is None:
                    dve.wait_ge(dve_done, now(dve_done))
                    dve.tensor_scalar(o, src[:, t0:t0 + HALF], w_of(2), None, ALU.mult).then_inc(dve_done, 1)
                    step(dve_done)
                else:
                    dve.wait_ge(dve_done, now(dve_done))
                    dve.tensor_scalar(o, src[:, t0:t0 + HALF], w_of(2), b, ALU.mult, ALU.add).then_inc(dve_done, 1)
                    step(dve_done)
                for tap, back in ((1, 1), (0, 2)):
                    lo = max(0, back - t0)
                    dve.wait_ge(dve_done, now(dve_done))
                    dve.scalar_tensor_tensor(out=o[:, lo:], in0=src[:, t0 + lo - back:t0 + HALF - back],
                                             scalar=w_of(tap), in1=o[:, lo:], op0=ALU.mult, op1=ALU.add).then_inc(dve_done, 1)
                    step(dve_done, *(name or ()))

            for j in range(KC):
                u = U_AIN + 4 * j
                for hf in range(2):
                    t = slice(hf * HALF, (hf + 1) * HALF)
                    dve.wait_ge(pe_done, at("unit", u + 1, 1))
                    dve.wait_ge(act_done, at("cs", j, hf))
                    dve.wait_ge(dve_done, now(dve_done))
                    dve.tensor_tensor(M[0][:, t], cs[:, hf, :], PS[:, 2 * ((u + 1) % 2) + hf, :], ALU.mult).then_inc(dve_done, 1)
                    step(dve_done, "cu", j, hf)
                names[("free", u + 1)] = names[("cu", j, 1)]
                for hf in range(2):
                    if j:
                        dve.wait_ge(act_done, at("yh", j - 1, hf))
                    conv(M[0], cw, j, KC, hf, None, None)
                if j and len(MODS_AT[j - 1]) > 1:
                    mod_out(MODS_AT[j - 1][1])
                mod_steps(MODS_AT[j][0])
                for hf in range(2):
                    dve.wait_ge(pe_done, at("unit", u + 2, 1))
                    dve.wait_ge(dve_done, now(dve_done))
                    dve.tensor_tensor(yt[:, hf, :], yt[:, hf, :], PS[:, 2 * ((u + 2) % 2) + hf, :], ALU.mult).then_inc(dve_done, 1)
                    step(dve_done)
                did_free = now(dve_done)
                names[("free", u + 2)] = did_free
                for hf in range(2):
                    dve.wait_ge(act_done, at("sz", j, hf))
                    dve.wait_ge(dve_done, now(dve_done))
                    dve.tensor_tensor(yt[:, hf, :], yt[:, hf, :], cs[:, hf, :], ALU.mult).then_inc(dve_done, 1)
                    step(dve_done, "yz", j, hf)
                for hf in range(2):
                    t = slice(hf * HALF, (hf + 1) * HALF)
                    dve.wait_ge(act_done, at("yh", j, hf))
                    dve.wait_ge(dve_done, now(dve_done))
                    dve.tensor_tensor(opB[:, 1, j, t], yt[:, hf, :], opB[:, 0, j, t].bitcast(F32),
                                      ALU.subtract).then_inc(dve_done, 1)
                    step(dve_done, "y", j, hf)
                mod_out(MODS_AT[j][0])
                if len(MODS_AT[j]) > 1:
                    mod_steps(MODS_AT[j][1])

            def residual(n, u, gate, j, first_need=None):
                for hf in range(2):
                    t = slice(hf * HALF, (hf + 1) * HALF)
                    dve.wait_ge(pe_done, at("unit", u, 1))
                    if first_need is not None:
                        dve.wait_ge(x_moved, at(*first_need))
                    dve.wait_ge(dve_done, now(dve_done))
                    dve.scalar_tensor_tensor(out=X[:, j, t], in0=PS[:, 2 * (u % 2) + hf, :],
                                             scalar=mod[:, gate, j:j + 1], in1=X[:, j, t], op0=ALU.mult,
                                             op1=ALU.add).then_inc(dve_done, 1)
                    step(dve_done, "x_new", n, j)
                names[("free", u)] = names[("x_new", n, j)]

            def residuals(n, u0, gate, first_need=None, sums=True):
                for j in range(KC):
                    residual(n, u0 + j, gate, j, first_need)
                    if sums:
                        if j:
                            sq_add(n, j - 1)
                if sums:
                    sq_add(n, KC - 1)

            residuals("kv", U_AOUT, A_GATE)
            parts("kv", "kv_norm_g", KV_SCALE, ("unit", U_AOUT - 1, 1))
            names[("norm_end",)] = now(dve_done)

            def hl_lo(u, x, scale):
                s = u % 2
                dve.wait_ge(act_done, at("hl_hi", u))
                dve.wait_ge(dve_done, now(dve_done))
                dve.scalar_tensor_tensor(out=stage[:, x % 2, 1, :], in0=banks(2 * s),
                                         scalar=scale, in1=stage[:, x % 2, 0, :].bitcast(F32), op0=ALU.mult,
                                         op1=ALU.subtract).then_inc(dve_done, 1)
                step(dve_done, "hl_lo", u)
                names[("free", u)] = names[("hl_lo", u)]

            def v_lo(u, x, kind):
                s = u % 2
                src = PS[:, 4:6, :].rearrange("p b (k e d) -> p (b k) e d", k=4, e=2)
                if kind in ("stick", "swa"):
                    for e in range(2):
                        place = 0 if kind == "swa" else e
                        v = vstage[:, s, e, :].rearrange("p (k s d) -> p k s d", k=NT, s=2)
                        dve.wait_ge(act_done, at("v_hi", u))
                        dve.wait_ge(dve_done, now(dve_done))
                        dve.tensor_tensor(v[:, :, 1 - place, :], src[:, :, e, :], v[:, :, place, :].bitcast(F32),
                                          ALU.subtract).then_inc(dve_done, 1)
                        step(dve_done, "v_split", u)
                else:
                    dve.wait_ge(act_done, at("v_hi", u))
                    dve.wait_ge(dve_done, now(dve_done))
                    dve.tensor_tensor(vstage[:, s, 1, :], banks(4),
                                      vstage[:, s, 0, :].bitcast(F32), ALU.subtract).then_inc(dve_done, 1)
                    step(dve_done, "v_split", u)

            for n in range(KC):
                hl_lo(U_KV + n, n, 1.0)
            for n in range(KC):
                v_lo(U_KV + KC + n, n, "stick")
            parts("b", "b_norm_g", B_SCALE, ("unit", U_QZ - 1, 1))
            names[("x_free", 0)] = now(dve_done)
            for n in range(KC):
                hl_lo(U_QZ + n, n, QSCALE)
            stick_dve(dve)
            residuals("fin1", U_BOUT, B_GATE, ("x_back", 0))

            def scale_x(n, gname):
                for j in range(KC):
                    c = C[gname] + j
                    dve.wait_ge(act_done, at("rstd", n, 0))
                    dve.wait_ge(act_done, at("rstd", n, 1))
                    dve.wait_ge(dve_done, now(dve_done))
                    dve.scalar_tensor_tensor(out=X[:, j, :], in0=X[:, j, :], scalar=cols[:, c:c + 1],
                                             in1=M[1][:], op0=ALU.mult, op1=ALU.mult).then_inc(dve_done, 1)
                    step(dve_done, "x_" + n, j)

            scale_x("fin1", "final_norm_g")
            for j in range(KC):
                names[("x_new", "n1", j)] = names[("x_fin1", j)]
            for j in range(KC):
                sq_add("n1", j)
            parts("n1", "norm1_g_2", SCALE1, ("unit", U_IN2 - 1, 1))
            names[("x_free", 1)] = now(dve_done)
            for n in range(13):
                hl_lo(U_IN2 + n, n, QSCALE if n < 8 else 1.0)
            for n in range(5):
                v_lo(U_IN2 + 13 + n, n, "diff" if n else "swa")
            second_dve(dve)
            for n in range(KC):
                u = U_BRANCH + n
                s = u % 2
                for hf in range(2):
                    t = slice(hf * HALF, (hf + 1) * HALF)
                    dve.wait_ge(pe_done, at("unit", u, 1))
                    if n:
                        dve.wait_ge(act_done, at("mh", n - 1, hf))
                    else:
                        dve.wait_ge(dve_done, at("diff_olo", 3, 1))
                    dve.wait_ge(dve_done, now(dve_done))
                    dve.tensor_tensor(d_o[:, hf, :], gates[:, n, t], PS[:, 2 * s + hf, :], ALU.mult).then_inc(dve_done, 1)
                    step(dve_done)
                    dve.wait_ge(pe_done, at("diff_pv", DIFF_HEADS - 1, NT - 1))
                    dve.wait_ge(dve_done, now(dve_done))
                    dve.tensor_tensor(M[4 - 1][:, t], gates[:, KC + n, t], PS[:, 4 + 2 * s + hf, :], ALU.mult).then_inc(dve_done, 1)
                    step(dve_done)
                names[("free", u)] = now(dve_done)
                for hf in range(2):
                    t = slice(hf * HALF, (hf + 1) * HALF)
                    dve.wait_ge(dve_done, now(dve_done))
                    dve.tensor_tensor(d_o[:, hf, :], d_o[:, hf, :], M[3][:, t], ALU.add).then_inc(dve_done, 1)
                    step(dve_done, "mz", n, hf)
                for hf in range(2):
                    t = slice(hf * HALF, (hf + 1) * HALF)
                    dve.wait_ge(act_done, at("mh", n, hf))
                    dve.wait_ge(dve_done, now(dve_done))
                    dve.tensor_tensor(opB[:, 1, n, t], d_o[:, hf, :], opB[:, 0, n, t].bitcast(F32),
                                      ALU.subtract).then_inc(dve_done, 1)
                    step(dve_done, "merged", n, hf)
            residuals("n2", U_OUT2, GATE1, ("x_back", 1))
            parts("n2", "norm2_g_2", SCALE2, ("unit", U_OUT2 - 1, 1))
            u = U_FFN
            for gi, (first, many) in enumerate(FGROUPS):
                for f in range(first, first + many):
                    for hf in range(2):
                        dve.wait_ge(act_done, at("fa", f, 1))
                        if f:
                            dve.wait_ge(act_done, at("fh", f - 1, hf))
                        conv(M[0], C["conv_w_2"], f, FC, hf, C["conv_b_2"] + f, ("fconv", f, hf))
                    for hf in range(2):
                        dve.wait_ge(act_done, at("fg", f, hf))
                        dve.wait_ge(pe_done, at("unit", u + 1, 1))
                        dve.wait_ge(dve_done, now(dve_done))
                        dve.tensor_tensor(yt[:, hf, :], yt[:, hf, :], PS[:, 2 * ((u + 1) % 2) + hf, :], ALU.mult).then_inc(dve_done, 1)
                        step(dve_done, "fz", f, hf)
                    names[("free", u + 1)] = names[("fz", f, 1)]
                    for hf in range(2):
                        t = slice(hf * HALF, (hf + 1) * HALF)
                        dve.wait_ge(act_done, at("fh", f, hf))
                        dve.wait_ge(dve_done, now(dve_done))
                        dve.tensor_tensor(opB[:, 1, f - first, t], yt[:, hf, :],
                                          opB[:, 0, f - first, t].bitcast(F32), ALU.subtract).then_inc(dve_done, 1)
                        step(dve_done, "ff", f, hf)
                    u += 2
                end = gi == len(FGROUPS) - 1
                residuals("fin2" if end else ("g", gi), u, GATE2, None, sums=end)
                u += KC
            scale_x("fin2", "final_g_2")
            for tb in range(NT):
                row = M[tb % 4 + 1]
                dve.wait_ge(pe_done, at("row_T", tb))
                if tb >= 4:
                    dve.wait_ge(row_gone[(tb - 4) % 4], at("row_gone", tb - 4))
                dve.wait_ge(dve_done, now(dve_done))
                dve.tensor_copy(row[:], banks(2 * (tb % 2))).then_inc(dve_done, 1)
                step(dve_done, "row_out", tb)

    return names


def kernel(**inputs):
    import concourse.bacc as bacc
    from concourse.bass_utils import run_bass_kernel_spmd

    arrays = {f"in_{k}": np.ascontiguousarray(v) for k, v in inputs.items()}
    known = {}
    for _ in range(2):
        nc = bacc.Bacc("TRN2", target_bir_lowering=False, num_devices=1)
        args = {k[3:]: nc.dram_tensor(k, list(v.shape), F32, kind="ExternalInput").ap() for k, v in arrays.items()}
        out = nc.dram_tensor("out_0", [1, T, D], F32, kind="ExternalOutput").ap()
        known = program(nc, args, out, known)
    r = run_bass_kernel_spmd(nc, [arrays], core_ids=[0])
    return r.results[0]["out_0"]
```

```python
from contextlib import ExitStack

import numpy as np

import concourse.bass as bass
from concourse import mybir

F32 = mybir.dt.float32
F32R = mybir.dt.float32r
ALU = mybir.AluOpType
ACT = mybir.ActivationFunctionType
AX_X = mybir.AxisListType.X

P = 128
T = 1024
D = 1024
KC = D // P
HALF = T // 2
NQ = HALF // P
NT = T // P
DH = 64
HEADS = 16
EPS = 1e-6
MASKED = -1e30
SWA_HEADS = 8
DIFF_HEADS = 4
LAM_INIT = 0.8 - 0.6
D_FF = 2816
FC = D_FF // P
FGROUPS = [(0, 8), (8, 8), (16, 6)]
SWA_COL, KA_COL, VA_COL, QD_COL, KD_COL, VD_COL, GA_COL, GD_COL = 0, 512, 640, 768, 1280, 1792, 2304, 3328
QSCALE = DH ** -0.5

ROWS0 = [("c", 8), ("c_2", 8), ("a_mod_b", 24), ("a_norm_g", 8), ("a_conv_w", 24), ("kv_mod_b", 16),
         ("b_mod_b", 24), ("kv_norm_g", 8), ("b_norm_g", 8)]
ROWS1 = [("b_ada_2", 48), ("final_norm_g", 8), ("norm1_g_2", 8), ("norm2_g_2", 8), ("final_g_2", 8),
         ("conv_b_2", 22), ("diff_subln_g_2", 1)]
ROWS2 = [("conv_w_2", 66)]
MODS = [("a_mod_w", 0, 0), ("a_mod_w", 1, 0), ("a_mod_w", 2, 0), ("kv_mod_w", 0, 0), ("kv_mod_w", 1, 0),
        ("b_mod_w", 0, 0), ("b_mod_w", 1, 0), ("b_mod_w", 2, 0)] + [("w_ada_2", g, 1) for g in range(6)]
MOD_BIAS = {"a_mod_w": "a_mod_b", "kv_mod_w": "kv_mod_b", "b_mod_w": "b_mod_b", "w_ada_2": "b_ada_2"}
A_SHIFT, A_SCALE, A_GATE, KV_SHIFT, KV_SCALE, B_SHIFT, B_SCALE, B_GATE = range(8)
SHIFT1, SCALE1, GATE1, SHIFT2, SCALE2, GATE2 = range(8, 14)
MOD_PIECES = 2 * KC
MOD_STEPS = 4
FIRST_MODS = 2
MOD_UNITS = (14 - FIRST_MODS) * MOD_PIECES // MOD_STEPS


def unit_list():
    units = []
    for j in range(KC):
        for part in (1, 2, 0, 3):
            units.append(("a_w_in", part * D + j * P, 0, KC))
    units += [("a_w_out", n * P, 0, KC) for n in range(KC)]
    units += [("w_kv", n * P, 0, KC) for n in range(2 * KC)]
    units += [("b_w_qz", n * P, 0, KC) for n in range(2 * KC)]
    units += [("b_w_out", n * P, 0, KC) for n in range(KC)]
    cols = ([SWA_COL + n * P for n in range(4)] + [QD_COL + n * P for n in range(4)] + [KA_COL]
            + [KD_COL + n * P for n in range(4)] + [VA_COL] + [VD_COL + n * P for n in range(4)]
            + [GA_COL + n * P for n in range(8)] + [GD_COL + n * P for n in range(8)])
    units += [("w_in_2", col, 0, KC) for col in cols]
    units += [("branch", n * P, 0, KC) for n in range(KC)]
    units += [("w_out_2", n * P, 0, KC) for n in range(KC)]
    for first, many in FGROUPS:
        for f in range(first, first + many):
            units += [("w_up_2", f * P, 0, KC), ("w_up_2", D_FF + f * P, 0, KC)]
        units += [("w_down_2", n * P, first * P, many) for n in range(KC)]
    return units


UNITS = unit_list()
U_AIN = 0
U_AOUT = U_AIN + 4 * KC
U_KV = U_AOUT + KC
U_QZ = U_KV + 2 * KC
U_BOUT = U_QZ + 2 * KC
U_IN2 = U_BOUT + KC
U_BRANCH = U_IN2 + 34
U_OUT2 = U_BRANCH + KC
U_FFN = U_OUT2 + KC

FIRST_V = (U_KV + KC, U_IN2 + 13)

LAG_B, LAG_A, LAG_H, LAG_V = 3, 4, 5, 6
RING = (0, 1, 2, 3, 6, 7)
STICK = [(0, kb) for kb in range(NQ - 1, -1, -1)] + [(1, kb) for kb in range(NT - 1, -1, -1)]


SWA_STEPS = 2 * SWA_HEADS
STEPS = SWA_STEPS + NT * DIFF_HEADS


def second_schedule():
    events, pieces, later = [], [], []
    valued = 0

    def pass_on():
        for item in list(later):
            item[0] -= 1
            if item[0] == 0:
                later.remove(item)
                kind, n = item[1]
                if kind == "rms":
                    turn((None, n))
                    later.append([1, ("scaled", n)])
                    later.append([2, ("parts", n)])
                else:
                    events.append((kind, n))

    def values_upto(c):
        nonlocal valued
        while valued <= min(c, len(pieces) - 1):
            x, p = pieces[valued]
            if x is not None:
                events.append(("values", valued))
                i = (x - SWA_STEPS) % NT
                if x < SWA_STEPS:
                    if p == 1:
                        later.append([2, ("out", x)])
                elif i % NQ == NQ - 1 and p == i // NQ:
                    events.append(("square", (x - SWA_STEPS) // NQ))
                    later.append([2, ("rms", (x - SWA_STEPS) // NQ)])
            valued += 1

    def turn(piece):
        values_upto(len(pieces) - 2)
        pieces.append(piece)
        events.append(("turn", len(pieces) - 1) if piece[0] is not None else ("rms", piece[1]))

    line = list(range(SWA_STEPS)) + [None] + list(range(SWA_STEPS, STEPS)) + [None, None]
    for t, x in enumerate(line):
        if x is not None:
            events.append(("scores", x))
        if t >= 1 and line[t - 1] is not None:
            events.append(("norm", line[t - 1]))
        if t >= 2 and line[t - 2] is not None:
            x = line[t - 2]
            for p in range(2 if x < SWA_STEPS else (x - SWA_STEPS) % NT // NQ + 1):
                turn((x, p))
                pass_on()
    values_upto(len(pieces))
    while later:
        pass_on()
    return events, pieces


SECOND, PIECES = second_schedule()
PLACE = {piece: c for c, piece in enumerate(PIECES)}


def last_piece(x):
    return max(c for c, (y, _) in enumerate(PIECES) if y == x)


def program(nc, a, out, known):
    names = {}
    ctx = ExitStack()
    with ctx:
        def sem(name):
            return ctx.enter_context(nc.semaphore(name))

        base = -(-nc.sbuf_base // 64) * 64
        KIB = 1024
        AT_X, AT_A, AT_B = base, base + 32 * KIB, base + 96 * KIB
        AT_W = base + 160 * KIB
        AT_M = AT_W + 24 * KIB
        AT_C = AT_M + 20 * KIB

        def at(name, offset, shape, dt=F32):
            return nc.alloc_sbuf_tensor_at(name, [P] + shape, dt, offset=offset)

        X = at("X", AT_X, [KC, T])
        opA = at("opA", AT_A, [2, KC, T], F32R)
        opB = at("opB", AT_B, [2, KC, T], F32R)
        w_raw = at("w_raw", AT_W, [2, KC, P])
        w_hi = at("w_hi", AT_W + 8 * KIB, [2, KC, P], F32R)
        w_lo = at("w_lo", AT_W + 16 * KIB, [2, KC, P], F32R)
        M = [at(f"M{i}", AT_M + 4 * KIB * i, [T]) for i in range(5)]
        ident = at("ident", AT_C, [P])
        ones = at("ones", AT_C + 512, [P])
        cols = at("cols", AT_C + 1024, [3 * P])
        small = at("small", AT_C + 2560, [100])
        mod = at("mod", AT_C + 2560 + 416, [14, KC])
        x_rows = at("x_rows", AT_B, [NT, D])
        vec_rows = at("vec_rows", AT_A, [3, P])
        mod_acc = M[3]
        mod_raw = at("mod_raw", AT_M + 16 * KIB, [2, HALF])
        cs = at("cs", AT_M + 4 * KIB, [2, HALF])
        yt = at("yt", AT_M + 8 * KIB, [2, HALF])
        hn = at("hn", AT_M + 8 * KIB, [2, HALF])
        xn = at("xn", AT_M, [2, HALF])
        stage = at("stage", AT_B + 32 * KIB, [2, 2, T], F32R)
        vstage = at("vstage", AT_B + 48 * KIB, [2, 2, T], F32R)
        vt = at("vt", AT_M + 8 * KIB, [T])
        sz = at("sz", AT_B, [KC, T])
        hin = at("hin", AT_B + 32 * KIB, [2, 4, T], F32R)
        s_t = at("s_t", AT_X, [3, HALF])
        s_sp = at("s_sp", AT_X + 6 * KIB, [3, HALF])
        s_p = at("s_p", AT_X + 12 * KIB, [3, HALF])
        s_a = at("s_a", AT_X + 18 * KIB, [3, HALF])
        s_ah = at("s_ah", AT_M + 4 * KIB, [3, HALF], F32R)
        s_al = at("s_al", AT_M + 10 * KIB, [3, HALF], F32R)
        s_o = at("s_o", AT_X + 24 * KIB, [2, HALF])
        s_tmp = at("s_tmp", AT_X + 28 * KIB, [HALF])
        tri = at("tri", AT_X + 30 * KIB, [P])
        nones = at("nones", AT_X + 30 * KIB + 512, [P])
        ident_r = at("ident_r", AT_X + 31 * KIB, [P], F32R)
        mask_r = at("mask_r", AT_X + 31 * KIB + 512, [P], F32R)
        masks = at("masks", AT_M, [P])
        keys = at("keys", AT_X, [2, 2, T], F32R)
        vals = [[at("vals00", AT_X + 16 * KIB, [T], F32R), at("vals01", AT_X + 20 * KIB, [T], F32R)],
                [at("vals10", AT_W + 12 * KIB, [T], F32R), at("vals11", AT_W + 20 * KIB, [T], F32R)]]
        bias = at("bias", AT_X + 24 * KIB, [2, T])
        prob = [at("prob0", AT_M, [T]), at("prob1", AT_M + 4 * KIB, [T]), at("prob2", AT_W, [T]),
                at("prob3", AT_W + 4 * KIB, [T])]
        pair = [(prob[2], prob[3]), (at("prob4", AT_W + 8 * KIB, [T]), at("prob5", AT_W + 16 * KIB, [T])),
                (prob[0], prob[1])]
        swa_diag = at("swa_diag", AT_W + 4 * KIB, [2, NQ, P])
        diff_diag = at("diff_diag", AT_X + 28 * KIB, [4, P])
        aT = at("aT", AT_M + 8 * KIB, [2, 2, HALF], F32R)
        d_o = at("d_o", AT_M + 16 * KIB, [2, HALF])
        gates = at("gates", AT_B, [2 * KC, T])

        PS = ctx.enter_context(nc.psum_tensor("PS", [P, 8, HALF], F32))

        def scratch(name, shape, dt=F32):
            return nc.dram_tensor(name, shape, dt).ap()

        x_dram = scratch("x_dram", [P, KC * T], F32)
        k_dram = scratch("k_dram", [2, D, T])
        q_dram = scratch("q_dram", [2, D, T])
        v_dram = scratch("v_dram", [KC, P, 2, T])
        q2_dram = scratch("q2_dram", [2, D, T])
        k2_dram = scratch("k2_dram", [2, D, T])
        va_dram = scratch("va_dram", [P, 2, T])
        vd_dram = scratch("vd_dram", [DIFF_HEADS, P, 2, T])

        def banks(b):
            return PS[:, b:b + 2, :].rearrange("p b t -> p (b t)")

        pe_done, act_done, dve_done, pool_done = sem("pe_done"), sem("act_done"), sem("dve_done"), sem("pool_done")
        vec_in = sem("vec_in")
        x_in = [sem(f"x_in{tb}") for tb in range(NT)]
        w_in = [sem(f"w_in{s}") for s in range(2)]
        mod_in = [sem(f"mod_in{s}") for s in range(2)]
        x_moved = sem("x_moved")
        stored = [sem(f"stored{s}") for s in range(2)]
        v_stored = [sem(f"v_stored{s}") for s in range(2)]
        head_in = [sem(f"head_in{s}") for s in range(2)]
        q_in = [sem(f"q_in{c}") for c in range(KC)]
        k_in, v_in = [sem(f"k_in{s}") for s in range(2)], [sem(f"v_in{s}") for s in range(2)]
        row_gone = [sem(f"row_gone{s}") for s in range(4)]
        total = {}

        def now(s):
            return total.get(id(s), 0)

        def step(s, *name, by=1):
            total[id(s)] = now(s) + by
            if name:
                names[name] = now(s)

        def at(*name):
            return known.get(name, 0)

        def reader(u):
            if u < U_AOUT:
                return act_done if u % 4 in (0, 3) else dve_done
            if u >= U_FFN:
                first = [f for f, many in FGROUPS if U_FFN + 2 * f + KC * FGROUPS.index((f, many)) <= u][-1]
                gi = [f for f, _ in FGROUPS].index(first)
                n = u - (U_FFN + 2 * first + KC * gi)
                return act_done if n < 2 * FGROUPS[gi][1] and n % 2 == 0 else dve_done
            on_act = (range(U_KV + KC, U_QZ), range(U_QZ + KC, U_BOUT), range(U_IN2 + 13, U_BRANCH))
            return act_done if any(u in r for r in on_act) else dve_done

        def col(rows, name):
            at0 = 0
            for t, rs in enumerate((ROWS0, ROWS1, ROWS2)):
                at0 = t * P
                for n, many in rs:
                    if n == name:
                        return at0
                    at0 += many
            raise KeyError(name)

        C = {n: col(None, n) for rs in (ROWS0, ROWS1, ROWS2) for n, _ in rs}
        EPS_COL, SILU_C, GS, SINK, LAM = 0, 1, 17, 25, 33
        LAMS, SUBG, NSINK, MX, RS, RI = 37, 38, 39, 47, 63, 79

        block = ctx.enter_context(nc.Block())

        MISC_FREE = {"kv": "a", "n1": "fin1", "fin2": "n2"}

        def source(u):
            name, col0, row0, chunks = UNITS[u]
            if name == "branch":
                return [(a["w_branch_swa_2"][0], col0, 0, 4, 0), (a["w_branch_diff_2"][0], col0, 0, 4, 4)]
            w = a[name]
            if len(w.shape) == 3:
                w = w[0]
            return [(w, col0, row0, chunks, 0)]

        def second_loads(sp):
            def keys_values(load):
                slot = load % 2
                if load >= 2:
                    sp.wait_ge(pe_done, at("sec_S", 8 * load - 9, 0))
                for part in range(2):
                    if load < 2:
                        for place in range(2):
                            sp.dma_start(keys[place * DH:(place + 1) * DH, slot, part, :].bitcast(F32),
                                         k2_dram[part, load * DH:(load + 1) * DH, :]).then_inc(k_in[load % 2], 16)
                            step(k_in[load % 2], "k_in", load, by=16)
                    else:
                        sp.dma_start(keys[:, slot, part, :].bitcast(F32),
                                     k2_dram[part, (load - 1) * P:load * P, :]).then_inc(k_in[load % 2], 16)
                        step(k_in[load % 2], "k_in", load, by=16)
                if load >= 2:
                    sp.wait_ge(pe_done, at("sec_pv", last_piece(8 * load - 9)))
                else:
                    sp.wait_ge(pe_done, at("unit", U_BRANCH - 1, 1))
                for n in range(2):
                    if load >= 2:
                        sp.dma_start(vals[slot][n][:].bitcast(F32), vd_dram[load - 2, :, n, :]).then_inc(v_in[load % 2], 16)
                        step(v_in[load % 2], "v_in", load, by=16)
                    elif n == 0:
                        sp.dma_start(vals[slot][n][:].bitcast(F32), va_dram[:, load, :]).then_inc(v_in[load % 2], 16)
                        step(v_in[load % 2], "v_in", load, by=16)
                    else:
                        src = va_dram[:, load, :].rearrange("p (b s d) -> p b s d", b=NT, s=2)
                        dst = vals[slot][n][:].bitcast(F32).rearrange("p (b s d) -> p b s d", b=NT, s=2)
                        for s in range(2):
                            sp.dma_start(dst[:, :, 1 - s, :], src[:, :, s, :]).then_inc(v_in[load % 2], 16)
                            step(v_in[load % 2], "v_in", load, by=16)

            def queries(c):
                sp.dma_start(opA[:, :, c, :].bitcast(F32), q2_dram[:, c * P:(c + 1) * P, :].rearrange("s p t -> p s t")).then_inc(q_in[c], 16)
                step(q_in[c], "q_in", c, by=16)

            sp.wait_ge(stored[(U_IN2 + 11) % 2], at("stored", U_IN2 + 11))
            sp.wait_ge(stored[(U_IN2 + 12) % 2], at("stored", U_IN2 + 12))
            sp.wait_ge(v_stored[(U_IN2 + 16) % 2], at("v_stored", U_IN2 + 16))
            sp.wait_ge(v_stored[(U_IN2 + 17) % 2], at("v_stored", U_IN2 + 17))
            sp.wait_ge(x_moved, at("x_out", 1))
            keys_values(0)
            sp.wait_ge(pe_done, at("unit", U_BRANCH - 1, 1))
            for c in range(4):
                queries(c)
                if c == 1:
                    keys_values(1)
            for j in range(DIFF_HEADS):
                queries(4 + j)
            for j in range(DIFF_HEADS):
                keys_values(2 + j)

        def turn_v(pe, u):
            pe.wait_ge(act_done, at("vt", u))
            if not (u in FIRST_V):
                pe.wait_ge(dve_done, at("v_split", u - 1))
            for kb in range(NT):
                ins = pe.transpose(PS[:, 4 + kb // 4, (kb % 4) * P:(kb % 4 + 1) * P], vt[:, kb * P:(kb + 1) * P], ident[:])
            ins.then_inc(pe_done, 1)
            step(pe_done, "v_T", u)

        def cut(g):
            h, i = divmod(g, len(STICK))
            hf, kb = STICK[i]
            return h, i, hf, kb, max(0, (kb - NQ * hf) * P)

        def scores_of(g, q0):
            return PS[:, RING[g % len(RING)], q0:]

        def stick_pe(pe):
            def scores(g):
                h, i, hf, kb, qs = cut(g)
                s = h % 2
                pe.wait_ge(head_in[h % 2], at("head_in", h))
                pe.wait_ge(pool_done, at("stick_consts"))
                if g >= len(RING):
                    pe.wait_ge(act_done, at("stick_a", g - len(RING)))
                q = slice(hf * HALF + qs, (hf + 1) * HALF)
                k = hin[:, s, 0, kb * P:(kb + 1) * P]
                pe.matmul(scores_of(g, qs), k, hin[:, s, 1, q], start=True, stop=False)
                ins = pe.matmul(scores_of(g, qs), k, hin[:, s, 2, q], start=False, stop=True)
                if kb >= NQ * hf:
                    ins = pe.matmul(scores_of(g, qs)[:, 0:P], ident_r[:], mask_r[:], start=False, stop=True,
                                    skip_group_check=True)
                ins.then_inc(pe_done, 1)
                step(pe_done, "stick_s", g)

            def sums(g):
                h, i, hf, kb, qs = cut(g)
                pe.wait_ge(dve_done, at("stick_sp", g))
                ins = pe.matmul(scores_of(g, qs), tri[:], s_sp[:, g % 3, qs:], start=False, stop=True,
                                skip_group_check=True)
                if kb != NQ * hf + NQ - 1:
                    pe.wait_ge(pool_done, at("stick_p", g - 1))
                    qp = max(0, (kb + 1 - NQ * hf) * P)
                    ins = pe.matmul(scores_of(g, qp), nones[:], s_p[:, (g - 1) % 3, qp:], start=False, stop=True,
                                    skip_group_check=True)
                ins.then_inc(pe_done, 1)
                step(pe_done, "stick_b", g)

            def values(g):
                h, i, hf, kb, qs = cut(g)
                s, o = h % 2, 4 + hf
                top = kb == NQ * hf + NQ - 1
                pe.wait_ge(dve_done, at("stick_al", g))
                if h and top:
                    pe.wait_ge(dve_done, at("stick_o", h - 1, hf))
                v = hin[:, s, 3, kb * P:(kb + 1) * P]
                pe.matmul(PS[:, o, qs:], v, s_ah[:, g % 3, qs:], start=top, stop=False, skip_group_check=True)
                ins = pe.matmul(PS[:, o, qs:], v, s_al[:, g % 3, qs:], start=False, stop=(kb == 0),
                                skip_group_check=True)
                ins.then_inc(pe_done, 1)
                step(pe_done, "stick_c", g)
                if i == len(STICK) - 1:
                    names[("stick_free", h)] = names[("stick_c", g)]

            n = HEADS * len(STICK)
            pe.wait_ge(reader(U_BOUT - 1), at("free", U_BOUT - 1))
            pe.wait_ge(reader(U_BOUT - 2), at("free", U_BOUT - 2))
            for g in range(n + LAG_V):
                if g < n:
                    scores(g)
                if 0 <= g - LAG_B < n:
                    sums(g - LAG_B)
                if 0 <= g - LAG_V < n:
                    values(g - LAG_V)

        def piece_width(c):
            x, p = PIECES[c]
            return HALF if x < SWA_STEPS else (min(NQ * p + NQ, (x - SWA_STEPS) % NT + 1) - NQ * p) * P

        def second_pe(pe):
            def swa_scores(x):
                n, hf = divmod(x, 2)
                pe.wait_ge(q_in[(n // 2)], at("q_in", n // 2))
                pe.wait_ge(k_in[(n // 4) % 2], at("k_in", n // 4))
                if x >= 2:
                    pe.wait_ge(dve_done, at("sec_p", x - 2, 0))
                r = slice(DH * (n % 2), DH * (n % 2) + DH)
                for b in range(NQ):
                    i = NQ * hf + b
                    pieces = [(0, (i - 1) * P, 2 * P)] if i else [(0, 0, P), (P, 0, P)]
                    for at0, k0, width in pieces:
                        dst = PS[:, 2 * (x % 2) + b // 2, (b % 2) * 2 * P + at0:(b % 2) * 2 * P + at0 + width]
                        for y, (pq, pk) in enumerate(((0, 0), (1, 0), (0, 1))):
                            ins = pe.matmul(dst, opA[r, pq, n // 2, i * P:(i + 1) * P],
                                            keys[r, n // 4, pk, k0:k0 + width], start=(y == 0), stop=(y == 2))
                ins.then_inc(pe_done, 1)
                step(pe_done, "sec_S", x, 0)

            def diff_scores(x):
                j, i = divmod(x - SWA_STEPS, NT)
                pe.wait_ge(q_in[(4 + j)], at("q_in", 4 + j))
                pe.wait_ge(k_in[(2 + j) % 2], at("k_in", 2 + j))
                former = x - 1 if i >= NQ or i == 0 else x - 2
                for m in (1, 0):
                    if former >= SWA_STEPS:
                        pe.wait_ge(dve_done, at("sec_p", former, m))
                    else:
                        pe.wait_ge(dve_done, at("sec_p", SWA_STEPS - 1, 0))
                    r = slice(DH * m, DH * (m + 1))
                    for k0 in range(0, (i + 1) * P, HALF):
                        width = min(HALF, (i + 1) * P - k0)
                        bank = 2 * m + (i % 2 if i < NQ else k0 // HALF)
                        for y, (pq, pk) in enumerate(((0, 0), (1, 0), (0, 1))):
                            ins = pe.matmul(PS[:, bank, 0:width], opA[r, pq, 4 + j, i * P:(i + 1) * P],
                                            keys[r, j % 2, pk, k0:k0 + width], start=(y == 0), stop=(y == 2))
                    ins.then_inc(pe_done, 1)
                    step(pe_done, "sec_S", x, m)

            def turn(c):
                x, p = PIECES[c]
                bank = 4 + c % 2
                pe.wait_ge(pool_done, at("sec_g", x))
                if c >= 2:
                    pe.wait_ge(dve_done, at("sec_lo", c - 2))
                if x < SWA_STEPS:
                    for y in range(4):
                        ins = pe.matmul(PS[:, bank, y * P:(y + 1) * P], prob[x % 3][:, (4 * p + y) * P:(4 * p + y + 1) * P],
                                        swa_diag[:, x % 2, 2 * p + y // 2, :], start=True, stop=True)
                else:
                    pe.wait_ge(dve_done, at("sec_a", x))
                    i = (x - SWA_STEPS) % NT
                    for kb in range(4 * p, min(4 * p + 4, i + 1)):
                        ins = pe.matmul(PS[:, bank, (kb - 4 * p) * P:(kb - 4 * p + 1) * P],
                                        pair[x % 3][0][:, kb * P:(kb + 1) * P], diff_diag[:, x % 4, :],
                                        start=True, stop=True)
                ins.then_inc(pe_done, 1)
                step(pe_done, "sec_T", c)

            def values(c):
                x, p = PIECES[c]
                pe.wait_ge(v_in[(x // 8) % 2], at("v_in", x // 8))
                pe.wait_ge(dve_done, at("sec_lo", c))
                if x < SWA_STEPS:
                    n, hf = divmod(x, 2)
                    if x >= 2:
                        pe.wait_ge(dve_done, at("sec_o", x - 2))
                    for b in (2 * p, 2 * p + 1):
                        i = NQ * hf + b
                        steps = [(w, part) for w in range(2) if i or w for part in range(2)]
                        for y, (w, part) in enumerate(steps):
                            kb = i - 1 + w
                            ins = pe.matmul(PS[:, 6 + hf, b * P:(b + 1) * P], vals[n // 4][n % 2][:, kb * P:(kb + 1) * P],
                                            aT[:, c % 2, part, (2 * b + w - 4 * p) * P:(2 * b + w - 4 * p + 1) * P],
                                            start=(y == 0), stop=(y == len(steps) - 1))
                else:
                    j, i = divmod(x - SWA_STEPS, NT)
                    h = 2 * j + i // NQ
                    if i % NQ == 0:
                        pe.wait_ge(dve_done, at("sec_o", SWA_STEPS + h - 2))
                    for kb in range(4 * p, min(4 * p + 4, i + 1)):
                        for y, (pv, pa) in enumerate(((0, 0), (1, 0), (0, 1))):
                            ins = pe.matmul(PS[:, 6 + i // NQ, (i % NQ) * P:(i % NQ + 1) * P],
                                            vals[j % 2][pv][:, kb * P:(kb + 1) * P],
                                            aT[:, c % 2, pa, (kb - 4 * p) * P:(kb - 4 * p + 1) * P],
                                            start=(kb == 0 and y == 0), stop=(kb == i and y == 2))
                ins.then_inc(pe_done, 1)
                step(pe_done, "sec_pv", c)

            def rms(h):
                c = PLACE[None, h]
                pe.wait_ge(act_done, at("sec_sq", h))
                pe.wait_ge(dve_done, at("sec_lo", c - 2))
                pe.matmul(PS[:, 4 + c % 2, :], ones[:], d_o[:, 0, :], start=True, stop=True).then_inc(pe_done, 1)
                step(pe_done, "sec_ss", h)

            pe.wait_ge(reader(U_BRANCH - 1), at("free", U_BRANCH - 1))
            pe.wait_ge(reader(U_BRANCH - 2), at("free", U_BRANCH - 2))
            pe.wait_ge(dve_done, at("v_split", U_IN2 + 17))
            for kind, n in SECOND:
                if kind == "scores" and n < SWA_STEPS:
                    swa_scores(n)
                elif kind == "scores":
                    diff_scores(n)
                elif kind == "turn":
                    turn(n)
                elif kind == "values":
                    values(n)
                elif kind == "rms":
                    rms(n)

        def stick_act(act):
            def output(g):
                h, i, hf, kb, qs = cut(g)
                other = slice(DH * (1 - h % 2), DH * (1 - h % 2) + DH)
                main = slice(DH * (h % 2), DH * (h % 2) + DH)
                act.wait_ge(pe_done, at("stick_c", g))
                if h or hf:
                    act.wait_ge(dve_done, at("stick_o", (2 * h + hf - 1) // 2, (hf + 1) % 2))
                act.activation(s_tmp[main, :], PS[other, 4 + hf, :], ACT.Copy).then_inc(act_done, 1)
                step(act_done, "stick_tmp", h, hf)

            n = HEADS * len(STICK)
            act.preload_act_table_set("natural_log_exp_and_others")
            for g in range(n + LAG_V + 2):
                if g < n:
                    h, i, hf, kb, qs = cut(g)
                    act.wait_ge(pe_done, at("stick_s", g))
                    if g >= 3:
                        act.wait_ge(dve_done, at("stick_sp", g - 3))
                    else:
                        act.wait_ge(x_moved, at("x_out", 0))
                    act.activation(s_t[:, g % 3, qs:], scores_of(g, qs), ACT.Abs).then_inc(act_done, 1)
                    step(act_done, "stick_t", g)
                if 0 <= g - 1 < n:
                    e = g - 1
                    h, i, hf, kb, qs = cut(e)
                    act.wait_ge(act_done, at("stick_t", e))
                    act.activation(s_t[:, e % 3, qs:], s_t[:, e % 3, qs:], ACT.Exp, scale=-1.0).then_inc(act_done, 1)
                    step(act_done, "stick_e", e)
                if 0 <= g - LAG_A < n:
                    e = g - LAG_A
                    h, i, hf, kb, qs = cut(e)
                    act.wait_ge(pe_done, at("stick_b", e))
                    if e >= 3:
                        act.wait_ge(dve_done, at("stick_al", e - 3))
                    act.activation(s_a[:, e % 3, qs:], scores_of(e, qs), ACT.Exp).then_inc(act_done, 1)
                    step(act_done, "stick_a", e)
                if 0 <= g - 1 < n:
                    e = g - 1
                    h, i, hf, kb, qs = cut(e)
                    act.wait_ge(act_done, at("stick_e", e))
                    act.activation(s_t[:, e % 3, qs:], s_t[:, e % 3, qs:], ACT.Ln, bias=1.0).then_inc(act_done, 1)
                    step(act_done, "stick_l", e)
                e = g - LAG_V - 1
                if 0 <= e < n and e % len(STICK) in (NQ - 1, len(STICK) - 1):
                    output(e)

        def second_act(act):
            act.preload_act_table_set("natural_log_exp_and_others")

            def exps(x):
                n, hf = divmod(x, 2)
                for b in range(NQ):
                    c = x % 4 * 4 + b
                    p = prob[x % 3][:, b * 2 * P:(b + 1) * 2 * P]
                    act.wait_ge(dve_done, at("sec_p", x, 0))
                    act.activation(p, p, ACT.Exp, bias=small[:, MX + c:MX + c + 1], scale=-1.0,
                                   accum_out=small[:, RS + c:RS + c + 1]).then_inc(act_done, 1)
                    step(act_done, "sec_e", x, 0)
                c = x % 4 * 4
                act.activation(small[:, RI + c:RI + c + 4], small[:, MX + c:MX + c + 4],
                               ACT.Exp, bias=small[:, SINK + n:SINK + n + 1]).then_inc(act_done, 1)
                step(act_done, "sec_e", x, 0)

            def rows_exp(x):
                w = ((x - SWA_STEPS) % NT + 1) * P
                for m in (1, 0):
                    c = x % 4 * 4 + m
                    p = pair[x % 3][m][:, 0:w]
                    act.wait_ge(dve_done, at("sec_p", x, m))
                    act.activation(p, p, ACT.Exp, bias=small[:, MX + c:MX + c + 1], scale=-1.0,
                                   accum_out=small[:, RS + c:RS + c + 1]).then_inc(act_done, 1)
                    step(act_done, "sec_e", x, m)

            def high(c):
                w = piece_width(c)
                act.wait_ge(pe_done, at("sec_T", c))
                if c >= 2 and PIECES[c - 2][0] is not None:
                    act.wait_ge(pe_done, at("sec_pv", c - 2))
                act.activation(aT[:, c % 2, 0, 0:w], PS[:, 4 + c % 2, 0:w], ACT.Copy).then_inc(act_done, 1)
                step(act_done, "sec_hi", c)

            def out(x):
                n, hf = divmod(x, 2)
                other = slice(DH * (1 - n % 2), DH * (1 - n % 2) + DH)
                main = slice(DH * (n % 2), DH * (n % 2) + DH)
                act.wait_ge(pe_done, at("sec_pv", last_piece(x)))
                if n >= 2:
                    act.wait_ge(dve_done, at("swa_out", n // 2 - 1, hf))
                act.activation(d_o[main, hf, :], PS[other, 6 + hf, :], ACT.Copy).then_inc(act_done, 1)
                step(act_done, "sec_tmp", x)

            for kind, n in SECOND:
                if kind == "scores" and n < SWA_STEPS:
                    exps(n)
                elif kind == "scores":
                    rows_exp(n)
                elif kind == "turn":
                    high(n)
                elif kind == "out":
                    out(n)
                elif kind == "square":
                    act.wait_ge(pe_done, at("sec_pv", last_piece(SWA_STEPS + NQ * n + NQ - 1)))
                    act.wait_ge(dve_done, at("swa_out", 3, 1))
                    act.wait_ge(dve_done, at("swa_out", 3, 0))
                    act.wait_ge(dve_done, at("sec_o", SWA_STEPS + n - 1))
                    act.activation(d_o[:, 0, :], PS[:, 6 + n % 2, :], ACT.Square).then_inc(act_done, 1)
                    step(act_done, "sec_sq", n)
                elif kind == "rms":
                    act.wait_ge(dve_done, at("sec_lo", PLACE[None, n]))
                    act.activation(d_o[:, 0, :], d_o[:, 0, :], ACT.Ln, bias=small[:, EPS_COL:EPS_COL + 1],
                                   scale=1.0 / P).then_inc(act_done, 1)
                    step(act_done, "sec_ln", n)
                    act.wait_ge(act_done, at("sec_ln", n))
                    act.activation(d_o[:, 0, :], d_o[:, 0, :], ACT.Exp, scale=-0.5).then_inc(act_done, 1)
                    step(act_done, "sec_rr", n)
                elif kind == "parts":
                    j, hf = divmod(n, 2)
                    act.wait_ge(dve_done, at("sec_o", SWA_STEPS + n))
                    act.activation(opA[:, 0, 4 + j, hf * HALF:(hf + 1) * HALF], d_o[:, 1, :], ACT.Copy).then_inc(act_done, 1)
                    step(act_done, "sec_ohi", n)

        def stick_dve(dve):
            def finish(h, hf):
                main = slice(DH * (h % 2), DH * (h % 2) + DH)
                j = h // 2
                t = slice(hf * HALF, (hf + 1) * HALF)
                dve.wait_ge(act_done, at("stick_tmp", h, hf))
                dve.wait_ge(dve_done, now(dve_done))
                dve.tensor_tensor(s_o[main, hf, :], PS[main, 4 + hf, :], s_tmp[main, :], ALU.add).then_inc(dve_done, 1)
                step(dve_done, "stick_o", h, hf)
                if h % 2:
                    dve.wait_ge(reader(U_BOUT - 1), at("free", U_BOUT - 1))
                    dve.wait_ge(dve_done, now(dve_done))
                    dve.tensor_tensor(s_o[:, hf, :], s_o[:, hf, :], sz[:, j, t], ALU.mult).then_inc(dve_done, 1)
                    step(dve_done)
                    dve.wait_ge(pe_done, at("unit", U_BOUT - 1, 1))
                    dve.wait_ge(dve_done, now(dve_done))
                    dve.tensor_copy(opA[:, 0, j, t], s_o[:, hf, :]).then_inc(dve_done, 1)
                    step(dve_done)
                    dve.wait_ge(dve_done, now(dve_done))
                    dve.tensor_tensor(opA[:, 1, j, t], s_o[:, hf, :], opA[:, 0, j, t].bitcast(F32),
                                      ALU.subtract).then_inc(dve_done, 1)
                    step(dve_done, "stick_out", j, hf)

            n = HEADS * len(STICK)
            for g in range(n + LAG_V + 3):
                if 0 <= g - 2 < n:
                    e = g - 2
                    h, i, hf, kb, qs = cut(e)
                    dve.wait_ge(act_done, at("stick_l", e))
                    if e >= 3:
                        dve.wait_ge(pe_done, at("stick_b", e - 3))
                    if e >= 3 and cut(e - 3)[3] > 0:
                        dve.wait_ge(pool_done, at("stick_p", e - 3))
                    dve.scalar_tensor_tensor(out=s_sp[:, e % 3, qs:], in0=scores_of(e, qs), scalar=0.0,
                                             in1=s_t[:, e % 3, qs:], op0=ALU.max, op1=ALU.add).then_inc(dve_done, 1)
                    step(dve_done, "stick_sp", e)
                if 0 <= g - LAG_H < n:
                    e = g - LAG_H
                    h, i, hf, kb, qs = cut(e)
                    dve.wait_ge(act_done, at("stick_a", e))
                    if e >= 3:
                        dve.wait_ge(pe_done, at("stick_c", e - 3))
                    dve.tensor_copy(s_ah[:, e % 3, qs:], s_a[:, e % 3, qs:]).then_inc(dve_done, 1)
                    step(dve_done, "stick_ah", e)
                    dve.wait_ge(dve_done, at("stick_ah", e))
                    dve.tensor_tensor(s_al[:, e % 3, qs:], s_a[:, e % 3, qs:],
                                      s_ah[:, e % 3, qs:].bitcast(F32), ALU.subtract).then_inc(dve_done, 1)
                    step(dve_done, "stick_al", e)
                e = g - LAG_V - 2
                if 0 <= e < n and e % len(STICK) in (NQ - 1, len(STICK) - 1):
                    h, i, hf, kb, qs = cut(e)
                    finish(h, hf)
            names[("att_end", 0)] = now(dve_done)
            names[("att_end2", 0)] = now(dve_done)

        def second_dve(dve):
            def swa_probs(x):
                n, hf = divmod(x, 2)
                m = small[:, MX + x % 4 * 4:MX + x % 4 * 4 + 4]
                dve.wait_ge(pe_done, at("sec_S", x, 0))
                dve.wait_ge(pool_done, at("bias_s", n, hf))
                if x >= 3:
                    dve.wait_ge(pe_done, at("sec_T", last_piece(x - 3)))
                else:
                    dve.wait_ge(pool_done, at("split", U_BRANCH - 1))
                for b in range(NQ):
                    k = slice(b * 2 * P, (b + 1) * 2 * P)
                    dve.tensor_tensor_reduce(out=prob[x % 3][:, k], in0=bias[:, hf, k],
                                             in1=banks(2 * (x % 2))[:, k], scale=1.0,
                                             scalar=-MASKED * 1e3, op0=ALU.add, op1=ALU.min,
                                             accum_out=m[:, b:b + 1]).then_inc(dve_done, 1)
                    step(dve_done)
                dve.wait_ge(dve_done, now(dve_done))
                dve.tensor_scalar(m, m, small[:, NSINK + n:NSINK + n + 1], None, ALU.min).then_inc(dve_done, 1)
                step(dve_done, "sec_p", x, 0)

            def diff_probs(x):
                w = ((x - SWA_STEPS) % NT + 1) * P
                if x % 8 == 0:
                    dve.wait_ge(pool_done, at("bias_d"))
                    dve.wait_ge(dve_done, now(dve_done))
                    dve.tensor_scalar(bias[:, 0, :], bias[:, 0, :], 0.25, None, ALU.mult).then_inc(dve_done, 1)
                    step(dve_done)
                for m in (1, 0):
                    bank = 2 * m + (x % 2 if w <= HALF else 0)
                    c = MX + x % 4 * 4 + m
                    dve.wait_ge(pe_done, at("sec_S", x, m))
                    if x > SWA_STEPS:
                        dve.wait_ge(pe_done, at("sec_T", last_piece(max(x - 3, SWA_STEPS - 1))))
                    else:
                        dve.wait_ge(pe_done, at("unit", U_BRANCH - 1, 1))
                    dve.wait_ge(dve_done, now(dve_done))
                    dve.tensor_tensor_reduce(out=pair[x % 3][m][:, 0:w], in0=bias[:, 0, T - w:],
                                             in1=PS[:].rearrange("p b t -> p (b t)")[:, bank * HALF:bank * HALF + w],
                                             scale=1.0, scalar=-MASKED * 1e3, op0=ALU.add, op1=ALU.min,
                                             accum_out=small[:, c:c + 1]).then_inc(dve_done, 1)
                    step(dve_done, "sec_p", x, m)

            def norm(x):
                c = x % 4 * 4
                if x < SWA_STEPS:
                    r = small[:, RI + c:RI + c + 4]
                    dve.wait_ge(act_done, at("sec_e", x, 0))
                    dve.wait_ge(dve_done, now(dve_done))
                    dve.tensor_tensor(r, r, small[:, RS + c:RS + c + 4], ALU.add).then_inc(dve_done, 1)
                    step(dve_done)
                    dve.wait_ge(dve_done, now(dve_done))
                    dve.reciprocal(r, r).then_inc(dve_done, 1)
                    step(dve_done, "sec_r", x)
                else:
                    w = ((x - SWA_STEPS) % NT + 1) * P
                    r = small[:, RI + c:RI + c + 2]
                    dve.wait_ge(act_done, at("sec_e", x, 0))
                    dve.wait_ge(dve_done, now(dve_done))
                    dve.reciprocal(r, small[:, RS + c:RS + c + 2]).then_inc(dve_done, 1)
                    step(dve_done, "sec_r", x)
                    dve.wait_ge(dve_done, now(dve_done))
                    dve.scalar_tensor_tensor(out=small[:, RI + c + 1:RI + c + 2], in0=r[:, 1:2],
                                             scalar=small[:, LAMS:LAMS + 1], in1=small[:, RS + c:RS + c + 1],
                                             op0=ALU.mult, op1=ALU.mult).then_inc(dve_done, 1)
                    step(dve_done)
                    dve.wait_ge(dve_done, now(dve_done))
                    dve.scalar_tensor_tensor(out=pair[x % 3][0][:, 0:w], in0=pair[x % 3][1][:, 0:w],
                                             scalar=small[:, RI + c + 1:RI + c + 2],
                                             in1=pair[x % 3][0][:, 0:w], op0=ALU.mult, op1=ALU.add).then_inc(dve_done, 1)
                    step(dve_done, "sec_a", x)

            def out(x):
                n, hf = divmod(x, 2)
                main = slice(DH * (n % 2), DH * (n % 2) + DH)
                j = n // 2
                t = slice(hf * HALF, (hf + 1) * HALF)
                dve.wait_ge(act_done, at("sec_tmp", x))
                dve.wait_ge(dve_done, now(dve_done))
                dve.tensor_tensor(d_o[main, hf, :], PS[main, 6 + hf, :], d_o[main, hf, :], ALU.add).then_inc(dve_done, 1)
                step(dve_done, "sec_o", x)
                if n % 2:
                    dve.wait_ge(dve_done, now(dve_done))
                    dve.tensor_copy(opA[:, 0, j, t], d_o[:, hf, :]).then_inc(dve_done, 1)
                    step(dve_done)
                    dve.wait_ge(dve_done, now(dve_done))
                    dve.tensor_tensor(opA[:, 1, j, t], d_o[:, hf, :], opA[:, 0, j, t].bitcast(F32),
                                      ALU.subtract).then_inc(dve_done, 1)
                    step(dve_done, "swa_out", j, hf)

            for kind, n in SECOND:
                if kind == "scores" and n < SWA_STEPS:
                    swa_probs(n)
                elif kind == "scores":
                    diff_probs(n)
                elif kind == "norm":
                    norm(n)
                elif kind == "turn":
                    w = piece_width(n)
                    dve.wait_ge(act_done, at("sec_hi", n))
                    dve.tensor_tensor(aT[:, n % 2, 1, 0:w], PS[:, 4 + n % 2, 0:w],
                                      aT[:, n % 2, 0, 0:w].bitcast(F32), ALU.subtract).then_inc(dve_done, 1)
                    step(dve_done, "sec_lo", n)
                elif kind == "out":
                    out(n)
                elif kind == "rms":
                    dve.wait_ge(pe_done, at("sec_ss", n))
                    dve.tensor_copy(d_o[:, 0, :], PS[:, 4 + PLACE[None, n] % 2, :]).then_inc(dve_done, 1)
                    step(dve_done, "sec_lo", PLACE[None, n])
                elif kind == "scaled":
                    dve.wait_ge(act_done, at("sec_rr", n))
                    dve.wait_ge(dve_done, now(dve_done))
                    dve.scalar_tensor_tensor(out=d_o[:, 1, :], in0=PS[:, 6 + n % 2, :],
                                             scalar=small[:, SUBG:SUBG + 1], in1=d_o[:, 0, :], op0=ALU.mult,
                                             op1=ALU.mult).then_inc(dve_done, 1)
                    step(dve_done, "sec_o", SWA_STEPS + n)
                elif kind == "parts":
                    j, hf = divmod(n, 2)
                    t = slice(hf * HALF, (hf + 1) * HALF)
                    dve.wait_ge(act_done, at("sec_ohi", n))
                    dve.wait_ge(dve_done, now(dve_done))
                    dve.tensor_tensor(opA[:, 1, 4 + j, t], d_o[:, 1, :], opA[:, 0, 4 + j, t].bitcast(F32),
                                      ALU.subtract).then_inc(dve_done, 1)
                    step(dve_done, "sec_out", n)
            names[("att_end", 1)] = names[("att_end2", 1)] = now(dve_done)

        @block.sync
        def _(sp):
            sp.wait_ge(dve_done, at("vec_zero"))
            for t, rs in enumerate((ROWS0, ROWS1, ROWS2)):
                r = 0
                for n, many in rs:
                    v = a[n]
                    dims = " ".join(f"d{i}" for i in range(len(v.shape)))
                    v = v.rearrange(f"{dims} -> ({dims})").rearrange("(r p) -> r p", p=P)
                    sp.dma_start(vec_rows[r:r + many, t, :], v).then_inc(vec_in, 16)
                    step(vec_in, "vec_in", by=16)
                    r += many
            sp.dma_start(small[:, SINK:SINK + 8], a["swa_sinks_2"].to_broadcast([P, 8])).then_inc(vec_in, 16)
            step(vec_in, "vec_in", by=16)
            sp.dma_start(M[0][:, 0:256], a["diff_lambda_2"].rearrange("o f d -> o (f d)").to_broadcast([P, 256])).then_inc(vec_in, 16)
            step(vec_in, "vec_in", by=16)
            for tb in range(NT):
                sp.dma_start(x_rows[:, tb, :], a["x"][0, tb * P:(tb + 1) * P, :]).then_inc(x_in[tb], 16)
                step(x_in[tb], "x_in", tb, by=16)

            def mod_loads(pieces):
                for n in pieces:
                    name, part, _ = MODS[n // MOD_PIECES]
                    kc, h = divmod(n % MOD_PIECES, 2)
                    w = a[name]
                    if len(w.shape) == 3:
                        w = w[0]
                    if not (n < 2):
                        sp.wait_ge(dve_done, at("mod_step", n - 2))
                    sp.dma_start(mod_raw[:, n % 2, :],
                                 w[kc * P:(kc + 1) * P, part * D + h * HALF:part * D + (h + 1) * HALF]).then_inc(mod_in[n % 2], 16)
                    step(mod_in[n % 2], "mod_in", n, by=16)

            def weights(u):
                if not (u < 2):
                    sp.wait_ge(pool_done, at("split", u - 2))
                for n, (w, col0, row0, chunks, k0) in enumerate(source(u)):
                    src = w[row0:row0 + chunks * P, col0:col0 + P].rearrange("(k p) n -> p k n", p=P)
                    sp.dma_start(w_raw[:, u % 2, k0:k0 + chunks, :], src).then_inc(w_in[u % 2], 16)
                    step(w_in[u % 2], "w_in", u, by=16)

            def spill(n):
                sp.wait_ge(dve_done, at("x_free", n))
                sp.dma_start(x_dram, X[:].rearrange("p k t -> p (k t)")).then_inc(x_moved, 16)
                step(x_moved, "x_out", n, by=16)

            def reload(n):
                sp.wait_ge(x_moved, at("x_out", n))
                sp.wait_ge(dve_done, at("att_end", n))
                sp.wait_ge(dve_done, at("att_end2", n))
                sp.dma_start(X[:].rearrange("p k t -> p (k t)"), x_dram).then_inc(x_moved, 16)
                step(x_moved, "x_back", n, by=16)

            def head_loads(h):
                s = h % 2
                if h >= 2:
                    sp.wait_ge(pe_done, at("stick_free", h - 2))
                for u in (U_KV + KC - 1, U_KV + KC - 2, U_QZ + KC - 1, U_QZ + KC - 2):
                    sp.wait_ge(stored[u % 2], at("stored", u))
                for u in (U_KV + 2 * KC - 1, U_KV + 2 * KC - 2):
                    sp.wait_ge(v_stored[u % 2], at("v_stored", u))
                rows = slice(h * DH, (h + 1) * DH)
                key = f"head_in{s}"
                hi_at = slice(DH * (h % 2), DH * (h % 2) + DH)
                lo_at = slice(DH * (1 - h % 2), DH * (1 - h % 2) + DH)
                sp.dma_start(hin[hi_at, s, 0, :].bitcast(F32), k_dram[0, rows, :]).then_inc(head_in[h % 2], 16)
                step(head_in[h % 2], "head_in", h, by=16)
                sp.dma_start(hin[lo_at, s, 0, :].bitcast(F32), k_dram[1, rows, :]).then_inc(head_in[h % 2], 16)
                step(head_in[h % 2], "head_in", h, by=16)
                for part in range(2):
                    for place in (hi_at, lo_at):
                        sp.dma_start(hin[place, s, 1 + part, :].bitcast(F32), q_dram[part, rows, :]).then_inc(head_in[h % 2], 16)
                        step(head_in[h % 2], "head_in", h, by=16)
                sp.dma_start(hin[:, s, 3, :].bitcast(F32), v_dram[h // 2, :, h % 2, :]).then_inc(head_in[h % 2], 16)
                step(head_in[h % 2], "head_in", h, by=16)

            mod_loads(range(FIRST_MODS * MOD_PIECES))
            weights(0)
            weights(1)
            for u in range(2, len(UNITS)):
                if u == U_QZ + 4:
                    spill(0)
                if u == U_BOUT:
                    for h in range(HEADS):
                        head_loads(h)
                    reload(0)
                if u == U_IN2 + 20:
                    spill(1)
                if u == U_BRANCH:
                    second_loads(sp)
                if U_BRANCH <= u <= U_BRANCH + 1:
                    sp.wait_ge(pe_done, at("sec_T", last_piece(STEPS - 3)))
                if u == U_BRANCH + 3:
                    reload(1)
                weights(u)
                if u - 2 < MOD_UNITS:
                    n = FIRST_MODS * MOD_PIECES + (u - 2) * MOD_STEPS
                    mod_loads(range(n, n + MOD_STEPS))

        @block.gpsimd
        def _(pool):
            pool.wait_ge(pool_done, now(pool_done))
            pool.memset(ident[:], 0.0).then_inc(pool_done, 1)
            step(pool_done)
            pool.wait_ge(pool_done, now(pool_done))
            pool.affine_select(out=ident[:], in_=ident[:], compare_op=ALU.not_equal, fill=1.0, base=0,
                               pattern=[[-1, P]], channel_multiplier=1).then_inc(pool_done, 1)
            step(pool_done)
            pool.wait_ge(pool_done, now(pool_done))
            pool.memset(ones[:], 1.0).then_inc(pool_done, 1)
            step(pool_done)
            pool.wait_ge(pool_done, now(pool_done))
            pool.memset(small[:, EPS_COL:EPS_COL + 1], EPS).then_inc(pool_done, 1)
            step(pool_done, "consts")

            def split(u):
                s = u % 2
                chunks = UNITS[u][3]
                raw, hi, lo = w_raw[:, s, 0:chunks], w_hi[:, s, 0:chunks], w_lo[:, s, 0:chunks]
                if u == U_BRANCH + 1:
                    pool.wait_ge(pe_done, at("sec_pv", len(PIECES) - 2))
                pool.wait_ge(w_in[u % 2], at("w_in", u))
                if u >= 2:
                    pool.wait_ge(pe_done, at("unit", u - 2, 1))
                pool.wait_ge(pool_done, now(pool_done))
                pool.tensor_copy(hi, raw).then_inc(pool_done, 1)
                step(pool_done)
                pool.wait_ge(pool_done, now(pool_done))
                pool.tensor_tensor(lo, raw, hi.bitcast(F32), ALU.subtract).then_inc(pool_done, 1)
                step(pool_done, "split", u)

            def stick_pool():
                pool.wait_ge(x_moved, at("x_out", 0))
                pool.wait_ge(pool_done, now(pool_done))
                pool.memset(tri[:], -1.0).then_inc(pool_done, 1)
                step(pool_done)
                pool.wait_ge(pool_done, now(pool_done))
                pool.affine_select(out=tri[:], in_=tri[:], compare_op=ALU.is_ge, fill=0.0, base=0,
                                   pattern=[[-1, P]], channel_multiplier=1).then_inc(pool_done, 1)
                step(pool_done)
                pool.wait_ge(pool_done, now(pool_done))
                pool.memset(nones[:], -1.0).then_inc(pool_done, 1)
                step(pool_done)
                pool.wait_ge(pool_done, now(pool_done))
                pool.memset(masks[:], 0.0).then_inc(pool_done, 1)
                step(pool_done)
                pool.wait_ge(pool_done, now(pool_done))
                pool.affine_select(out=masks[:], in_=masks[:], compare_op=ALU.is_gt, fill=MASKED, base=0,
                                   pattern=[[1, P]], channel_multiplier=-1).then_inc(pool_done, 1)
                step(pool_done)
                pool.wait_ge(pool_done, now(pool_done))
                pool.tensor_copy(mask_r[:], masks[:]).then_inc(pool_done, 1)
                step(pool_done)
                pool.wait_ge(pool_done, now(pool_done))
                pool.tensor_copy(ident_r[:], ident[:]).then_inc(pool_done, 1)
                step(pool_done, "stick_consts")
                for g in range(HEADS * len(STICK)):
                    h, i, hf, kb, qs = cut(g)
                    if kb > 0:
                        q0 = qs + P if kb >= NQ * hf else qs
                        pool.wait_ge(dve_done, at("stick_sp", g))
                        if g >= 2:
                            pool.wait_ge(pe_done, at("stick_b", g - 2))
                        if q0 > qs:
                            pool.wait_ge(pool_done, now(pool_done))
                            pool.tensor_copy(s_p[:, g % 3, qs:q0], s_sp[:, g % 3, qs:q0]).then_inc(pool_done, 1)
                            step(pool_done, "stick_p", g)
                        if q0 < HALF:
                            pool.wait_ge(pool_done, at("stick_p", g - 1))
                            pool.tensor_tensor(s_p[:, g % 3, q0:], s_p[:, (g - 1) % 3, q0:],
                                               s_sp[:, g % 3, q0:], ALU.add).then_inc(pool_done, 1)
                            step(pool_done, "stick_p", g)

            def second_pool():
                far = -MASKED * 512
                for hf in range(2):
                    w = bias[:, hf, :].rearrange("p (b k) -> p b k", b=NQ)
                    pool.wait_ge(x_moved, at("x_out", 1))
                    pool.wait_ge(pool_done, now(pool_done))
                    pool.iota(w, pattern=[[0, NQ], [-1, 2 * P]], base=P, channel_multiplier=1,
                              allow_small_or_imprecise_dtypes=True).then_inc(pool_done, 1)
                    step(pool_done)
                    pool.wait_ge(pool_done, now(pool_done))
                    pool.affine_select(out=w, in_=w, compare_op=ALU.is_ge, fill=far, base=P,
                                       pattern=[[0, NQ], [-1, 2 * P]], channel_multiplier=1).then_inc(pool_done, 1)
                    step(pool_done)
                    pool.wait_ge(pool_done, now(pool_done))
                    pool.affine_select(out=w, in_=w, compare_op=ALU.is_gt, fill=far, base=0,
                                       pattern=[[0, NQ], [1, 2 * P]], channel_multiplier=-1).then_inc(pool_done, 1)
                    step(pool_done)
                pool.wait_ge(pool_done, now(pool_done))
                pool.memset(bias[:, 0, 0:P], far).then_inc(pool_done, 1)
                step(pool_done)

                def slope(n, hf):
                    if n:
                        pool.wait_ge(dve_done, at("sec_p", 2 * n - 2 + hf, 0))
                    pool.wait_ge(pool_done, now(pool_done))
                    pool.tensor_scalar(bias[:, hf, :], bias[:, hf, :], 0.5, None, ALU.mult).then_inc(pool_done, 1)
                    step(pool_done, "bias_s", n, hf)

                slope(0, 0)
                slope(0, 1)
                for kind, x in SECOND:
                    if kind == "norm" and x < SWA_STEPS:
                        for b in range(NQ):
                            c = RI + x % 4 * 4 + b
                            pool.wait_ge(dve_done, at("sec_r", x))
                            if x >= 2:
                                pool.wait_ge(pe_done, at("sec_T", last_piece(x - 2)))
                            pool.tensor_scalar(swa_diag[:, x % 2, b, :], ident[:], small[:, c:c + 1], None,
                                               ALU.mult).then_inc(pool_done, 1)
                            step(pool_done, "sec_g", x)
                        if x < SWA_STEPS - 2:
                            slope(x // 2 + 1, x % 2)
                        if x == SWA_STEPS - 2:
                            row = bias[:, 0, :]
                            pool.wait_ge(dve_done, at("sec_p", x, 0))
                            pool.wait_ge(pool_done, now(pool_done))
                            pool.iota(row, pattern=[[-1, T]], base=T - P, channel_multiplier=1,
                                      allow_small_or_imprecise_dtypes=True).then_inc(pool_done, 1)
                            step(pool_done)
                            pool.wait_ge(pool_done, now(pool_done))
                            pool.affine_select(out=row, in_=row, compare_op=ALU.is_ge, fill=far,
                                               base=T - P, pattern=[[-1, T]], channel_multiplier=1).then_inc(pool_done, 1)
                            step(pool_done, "bias_d")
                    elif kind == "norm":
                        c = RI + x % 4 * 4
                        pool.wait_ge(dve_done, at("sec_r", x))
                        if x >= SWA_STEPS + 4:
                            pool.wait_ge(pe_done, at("sec_T", last_piece(x - 4)))
                        else:
                            pool.wait_ge(dve_done, at("sec_p", SWA_STEPS - 1, 0))
                        pool.tensor_scalar(diff_diag[:, x % 4, :], ident[:], small[:, c:c + 1], None, ALU.mult).then_inc(pool_done, 1)
                        step(pool_done, "sec_g", x)
                pool.wait_ge(pe_done, at("sec_T", last_piece(STEPS - 2)))

            for u in range(len(UNITS)):
                if u == U_BOUT:
                    stick_pool()
                if u == U_BRANCH:
                    second_pool()
                split(u)

        @block.tensor
        def _(pe):
            def product(ps, hi_w, lo_w, rhs, chunks, k0, name, ready=None, hf=0):
                for k in range(chunks):
                    if ready is not None:
                        pe.wait_ge(dve_done, at("h_" + ready, k, hf))
                    for n, (w, part) in enumerate(((hi_w, 0), (lo_w, 0), (hi_w, 1))):
                        ins = pe.matmul(ps, w[:, k0 + k, :], rhs(part, k0 + k), start=(k == 0 and n == 0),
                                        stop=(k == chunks - 1 and n == 2))
                ins.then_inc(pe_done, 1)
                step(pe_done, *(name or ()))

            def unit(u, op_in, ready=None):
                s = u % 2
                pe.wait_ge(pool_done, at("split", u))
                if u >= 2:
                    pe.wait_ge(reader(u - 2), at("free", u - 2))
                for hf in range(2):
                    rhs = lambda part, k: op_in[:, part, k, hf * HALF:(hf + 1) * HALF]
                    product(PS[:, 2 * s + hf, :], w_hi[:, s], w_lo[:, s], rhs, UNITS[u][3], 0, ("unit", u, hf), ready, hf)

            def norm_sum(n):
                for hf in range(2):
                    pe.wait_ge(dve_done, at("ssum", n))
                    pe.wait_ge(pool_done, at("consts"))
                    if n in MISC_FREE:
                        pe.wait_ge(act_done, at("rstd", MISC_FREE[n], 1))
                    pe.matmul(PS[:, 4 + hf, :], ones[:], M[1][:, hf * HALF:(hf + 1) * HALF], start=True, stop=True).then_inc(pe_done, 1)
                    step(pe_done, "norm_sum", n, hf)

            def mod_sum(g):
                pe.wait_ge(dve_done, at("mod_step", (g + 1) * MOD_PIECES - 1))
                if g:
                    pe.wait_ge(dve_done, at("mod_out", g - 1))
                for j in range(KC):
                    ins = pe.matmul(PS[:, 6, j:j + 1], mod_acc[:, j * P:(j + 1) * P], ones[:, 0:1], start=True, stop=True)
                ins.then_inc(pe_done, 1)
                step(pe_done, "mod_sum", g)

            pe.wait_ge(pool_done, at("consts"))
            pe.wait_ge(vec_in, at("vec_in"))
            for t in range(3):
                ins = pe.transpose(PS[:, 7, t * P:(t + 1) * P], vec_rows[:, t, :], ident[:])
            ins.then_inc(pe_done, 1)
            step(pe_done, "vec_T")
            for j in range(KC):
                for hf in range(2):
                    n = 2 * j + hf
                    if n >= 4:
                        pe.wait_ge(act_done, at("x_set", n - 4))
                    for b in range(4):
                        pe.wait_ge(x_in[(4 * hf + b)], at("x_in", 4 * hf + b))
                    for b in range(4):
                        ins = pe.transpose(PS[:, n % 4, b * P:(b + 1) * P],
                                           x_rows[:, 4 * hf + b, j * P:(j + 1) * P], ident[:])
                    ins.then_inc(pe_done, 1)
                    step(pe_done, "x_T", n)
            for g in (0, 1):
                mod_sum(g)
            norm_sum("a")
            pe.wait_ge(act_done, at("x_set", 15))
            for j in range(KC):
                for q in range(4):
                    u = U_AIN + 4 * j + q
                    unit(u, opA, "a" if j == 0 and q == 0 else None)
                mod_sum(FIRST_MODS + j)
            for n in range(KC):
                pe.wait_ge(dve_done, at("y", KC - 1, 1))
                unit(U_AOUT + n, opB)
                if n % 4 == 3:
                    mod_sum(FIRST_MODS + KC + n // 4)
            norm_sum("kv")
            for n in range(2 * KC):
                unit(U_KV + n, opA, "kv" if n == 0 else None)
                if n in (3, 7):
                    mod_sum(FIRST_MODS + KC + 2 + n // 4)
                if n > KC:
                    turn_v(pe, U_KV + n - 1)
            turn_v(pe, U_KV + 2 * KC - 1)
            for n in range(2 * KC):
                unit(U_QZ + n, opA, "b" if n == 0 else None)
            stick_pe(pe)
            for n in range(KC):
                pe.wait_ge(dve_done, at("stick_out", HEADS // 2 - 1, 1))
                unit(U_BOUT + n, opA)
            norm_sum("fin1")
            norm_sum("n1")
            for n in range(34):
                unit(U_IN2 + n, opA, "n1" if n == 0 else None)
                if 13 < n <= 18:
                    turn_v(pe, U_IN2 + n - 1)
            second_pe(pe)
            for n in range(KC):
                u = U_BRANCH + n
                s = u % 2
                pe.wait_ge(pool_done, at("split", u))
                if u >= 2:
                    pe.wait_ge(reader(u - 2), at("free", u - 2))
                pe.wait_ge(dve_done, at("sec_out", 2 * DIFF_HEADS - 1))
                for hf in range(2):
                    rhs = lambda part, k: opA[:, part, k, hf * HALF:(hf + 1) * HALF]
                    product(PS[:, 2 * s + hf, :], w_hi[:, s], w_lo[:, s], rhs, 4, 0, ("unit_a", u, hf))
                    product(PS[:, 4 + 2 * s + hf, :], w_hi[:, s], w_lo[:, s], rhs, 4, 4, ("unit", u, hf))
            for n in range(KC):
                pe.wait_ge(dve_done, at("merged", KC - 1, 1))
                unit(U_OUT2 + n, opB)
            norm_sum("n2")
            u = U_FFN
            for first, many in FGROUPS:
                for f in range(2 * many):
                    unit(u, opA, "n2" if u == U_FFN else None)
                    u += 1
                for n in range(KC):
                    pe.wait_ge(dve_done, at("ff", first + many - 1, 1))
                    unit(u, opB)
                    u += 1
            norm_sum("fin2")
            for tb in range(NT):
                pe.wait_ge(dve_done, at("x_fin2", KC - 1))
                if tb >= 2:
                    pe.wait_ge(dve_done, at("row_out", tb - 2))
                pe.wait_ge(reader(len(UNITS) - 1), at("free", len(UNITS) - 1))
                pe.wait_ge(reader(len(UNITS) - 2), at("free", len(UNITS) - 2))
                for j in range(KC):
                    ins = pe.transpose(PS[:, 2 * (tb % 2) + j // 4, (j % 4) * P:(j % 4 + 1) * P],
                                       X[:, j, tb * P:(tb + 1) * P], ident[:])
                ins.then_inc(pe_done, 1)
                step(pe_done, "row_T", tb)

        @block.scalar
        def _(act):
            def act_norm(n, shift, x_free=None):
                act.preload_act_table_set("natural_log_exp_and_others")
                for hf in range(2):
                    r = M[1][:, hf * HALF:(hf + 1) * HALF]
                    act.wait_ge(pe_done, at("norm_sum", n, hf))
                    act.wait_ge(pe_done, at("norm_sum", n, 1))
                    act.wait_ge(act_done, now(act_done))
                    act.activation(r, PS[:, 4 + hf, :], ACT.Ln, bias=small[:, EPS_COL:EPS_COL + 1],
                                   scale=1.0 / D).then_inc(act_done, 1)
                    step(act_done)
                    act.wait_ge(act_done, now(act_done))
                    act.activation(r, r, ACT.Exp, scale=-0.5).then_inc(act_done, 1)
                    step(act_done, "rstd", n, hf)

            def act_parts(n, shift):
                for hf in range(2):
                    for j in range(KC):
                        x = hf * KC + j
                        s = x % 2
                        act.wait_ge(dve_done, at("xn", n, x))
                        if x >= 2:
                            act.wait_ge(dve_done, at("lo", n, x - 2))
                        act.wait_ge(act_done, now(act_done))
                        act.activation(hn[:, s, :], xn[:, s, :], ACT.Identity, bias=mod[:, shift, j:j + 1],
                                       scale=small[:, GS + j:GS + j + 1]).then_inc(act_done, 1)
                        step(act_done, "hn", n, x)
                        act.wait_ge(act_done, now(act_done))
                        act.activation(opA[:, 0, j, hf * HALF:(hf + 1) * HALF], hn[:, s, :], ACT.Copy).then_inc(act_done, 1)
                        step(act_done, "hi", n, x)

            def square(n, j):
                slot = M[0] if j % 2 == 0 else M[2]
                if n != "a":
                    act.wait_ge(dve_done, at("x_new", n, j))
                if j >= 2:
                    act.wait_ge(dve_done, at("sq_add", n, j - 2))
                else:
                    act.wait_ge(dve_done, at("lam_sum"))
                act.wait_ge(act_done, now(act_done))
                act.activation(slot[:], X[:, j, :], ACT.Square).then_inc(act_done, 1)
                step(act_done, "sq", n, j)

            act.wait_ge(dve_done, at("cols"))
            act.wait_ge(act_done, now(act_done))
            act.activation(small[:, SILU_C:SILU_C + 16], cols[:, 0:16], ACT.Silu).then_inc(act_done, 1)
            step(act_done, "silu_c")
            for j in range(KC):
                for hf in range(2):
                    n = 2 * j + hf
                    act.wait_ge(pe_done, at("x_T", n))
                    act.wait_ge(act_done, now(act_done))
                    act.activation(X[:, j, hf * HALF:(hf + 1) * HALF], PS[:, n % 4, :], ACT.Copy).then_inc(act_done, 1)
                    step(act_done, "x_set", n)
                square("a", j)
            act.wait_ge(dve_done, at("lam_sum"))
            act.wait_ge(act_done, now(act_done))
            act.activation(small[:, LAM + 2:LAM + 4], small[:, LAM:LAM + 2], ACT.Exp).then_inc(act_done, 1)
            step(act_done, "lam_exp")
            act_norm("a", A_SHIFT)
            act_parts("a", A_SHIFT)
            for j in range(KC):
                u = U_AIN + 4 * j
                for hf in range(2):
                    act.wait_ge(pe_done, at("unit", u, 1))
                    if j:
                        act.wait_ge(dve_done, at("yz", j - 1, hf))
                    act.wait_ge(act_done, at("hi", "a", 15))
                    act.wait_ge(dve_done, at("lo", "a", 15))
                    act.wait_ge(act_done, now(act_done))
                    act.activation(cs[:, hf, :], PS[:, 2 * (u % 2) + hf, :], ACT.Copy).then_inc(act_done, 1)
                    step(act_done, "cs", j, hf)
                names[("free", u)] = names[("cs", j, 1)]
                for hf in range(2):
                    act.wait_ge(pe_done, at("unit", u + 3, 1))
                    act.wait_ge(dve_done, at("cu", j, hf))
                    act.wait_ge(act_done, now(act_done))
                    act.activation(cs[:, hf, :], PS[:, 2 * ((u + 3) % 2) + hf, :], ACT.Silu).then_inc(act_done, 1)
                    step(act_done, "sz", j, hf)
                names[("free", u + 3)] = names[("sz", j, 1)]
                for hf in range(2):
                    act.wait_ge(dve_done, at("yz", j, hf))
                    act.wait_ge(act_done, now(act_done))
                    act.activation(opB[:, 0, j, hf * HALF:(hf + 1) * HALF], yt[:, hf, :], ACT.Copy).then_inc(act_done, 1)
                    step(act_done, "yh", j, hf)
            for n in range(KC):
                square("kv", n)
            act_norm("kv", KV_SHIFT)
            act_parts("kv", KV_SHIFT)

            def act_hl(u, x, scale, dram, row0, name):
                s = u % 2
                act.wait_ge(pe_done, at("unit", u, 1))
                if x >= 2:
                    act.wait_ge(stored[(u - 2) % 2], at("stored", u - 2))
                else:
                    if U_QZ <= u < U_BOUT:
                        act.wait_ge(stored[(U_KV + KC - 2 + x) % 2], at("stored", U_KV + KC - 2 + x))
                act.wait_ge(act_done, now(act_done))
                act.activation(stage[:, x % 2, 0, :], banks(2 * s), ACT.Copy, scale=scale).then_inc(act_done, 1)
                step(act_done, "hl_hi", u)

            def store_hl(u, x, dram, row0):
                act.wait_ge(dve_done, at("hl_lo", u))
                act.wait_ge(act_done, at("hl_hi", u))
                act.dma_start(dram[:, row0:row0 + P, :].rearrange("c p t -> p c t"), stage[:, x % 2, :, :].bitcast(F32)).then_inc(stored[u % 2], 16)
                step(stored[u % 2], "stored", u, by=16)

            def act_v(u, x):
                s = u % 2
                act.wait_ge(pe_done, at("unit", u, 1))
                if not (u in FIRST_V):
                    act.wait_ge(pe_done, at("v_T", u - 1))
                if u < U_IN2:
                    act.wait_ge(dve_done, at("norm_end"))
                else:
                    act.wait_ge(dve_done, at("x_free", 1))
                act.wait_ge(act_done, now(act_done))
                act.activation(vt[:], banks(2 * s), ACT.Copy).then_inc(act_done, 1)
                step(act_done, "vt", u)
                names[("free", u)] = names[("vt", u)]

            def act_v_hi(u, x, kind):
                s = u % 2
                src = PS[:, 4:6, :].rearrange("p b (k e d) -> p (b k) e d", k=4, e=2)
                if kind == "stick" or kind == "swa":
                    for e in range(2):
                        place = 0 if kind == "swa" else e
                        dst = vstage[:, s, e, :].rearrange("p (k s d) -> p k s d", k=NT, s=2)[:, :, place, :]
                        act.wait_ge(pe_done, at("v_T", u))
                        if x >= 2:
                            act.wait_ge(v_stored[(u - 2) % 2], at("v_stored", u - 2))
                        act.wait_ge(act_done, now(act_done))
                        act.activation(dst, src[:, :, e, :], ACT.Copy).then_inc(act_done, 1)
                        step(act_done, "v_hi", u)
                else:
                    act.wait_ge(pe_done, at("v_T", u))
                    if x >= 2:
                        act.wait_ge(v_stored[(u - 2) % 2], at("v_stored", u - 2))
                    act.wait_ge(act_done, now(act_done))
                    act.activation(vstage[:, s, 0, :], banks(4), ACT.Copy).then_inc(act_done, 1)
                    step(act_done, "v_hi", u)

            def store_v(u, x, dst):
                act.wait_ge(dve_done, at("v_split", u))
                act.dma_start(dst, vstage[:, u % 2, :, :].bitcast(F32)).then_inc(v_stored[u % 2], 16)
                step(v_stored[u % 2], "v_stored", u, by=16)

            for n in range(KC):
                act_hl(U_KV + n, n, 1.0, k_dram, n * P, "k")
                if n:
                    store_hl(U_KV + n - 1, n - 1, k_dram, (n - 1) * P)
            store_hl(U_KV + KC - 1, KC - 1, k_dram, (KC - 1) * P)
            for n in range(KC):
                act_v(U_KV + KC + n, n)
                act_v_hi(U_KV + KC + n, n, "stick")
                store_v(U_KV + KC + n, n, v_dram[n])
            act_parts("b", B_SHIFT)
            for n in range(KC):
                act_hl(U_QZ + n, n, QSCALE, q_dram, n * P, "q")
                if n:
                    store_hl(U_QZ + n - 1, n - 1, q_dram, (n - 1) * P)
            store_hl(U_QZ + KC - 1, KC - 1, q_dram, (KC - 1) * P)
            for n in range(KC):
                u = U_QZ + KC + n
                s = u % 2
                act.wait_ge(pe_done, at("unit", u, 1))
                act.wait_ge(act_done, now(act_done))
                act.activation(sz[:, n, :], banks(2 * s), ACT.Silu).then_inc(act_done, 1)
                step(act_done, "free", u)
            stick_act(act)
            for n in range(KC):
                square("fin1", n)
            act_norm("fin1", None)
            for n in range(KC):
                square("n1", n)
            act_norm("n1", SHIFT1)
            act_parts("n1", SHIFT1)
            dst = [(q2_dram, n * P) for n in range(8)] + [(k2_dram, n * P) for n in range(5)]
            for n in range(13):
                act_hl(U_IN2 + n, n, -QSCALE if n < 8 else 1.0, None, None, None)
                if n:
                    store_hl(U_IN2 + n - 1, n - 1, *dst[n - 1])
            store_hl(U_IN2 + 12, 12, *dst[12])
            for n in range(5):
                u = U_IN2 + 13 + n
                act_v(u, n)
                act_v_hi(u, n, "diff" if n else "swa")
                store_v(u, n, va_dram if n == 0 else vd_dram[n - 1])
            for n in range(16):
                u = U_IN2 + 18 + n
                s = u % 2
                act.wait_ge(pe_done, at("unit", u, 1))
                act.wait_ge(stored[(U_IN2 + 12) % 2], at("stored", U_IN2 + 12))
                act.wait_ge(stored[(U_IN2 + 11) % 2], at("stored", U_IN2 + 11))
                act.wait_ge(v_stored[(U_IN2 + 17) % 2], at("v_stored", U_IN2 + 17))
                act.wait_ge(v_stored[(U_IN2 + 16) % 2], at("v_stored", U_IN2 + 16))
                act.wait_ge(act_done, now(act_done))
                act.activation(gates[:, n, :], banks(2 * s), ACT.Sigmoid).then_inc(act_done, 1)
                step(act_done, "free", u)
            second_act(act)
            for n in range(KC):
                for hf in range(2):
                    act.wait_ge(dve_done, at("mz", n, hf))
                    act.wait_ge(act_done, now(act_done))
                    act.activation(opB[:, 0, n, hf * HALF:(hf + 1) * HALF], d_o[:, hf, :], ACT.Copy).then_inc(act_done, 1)
                    step(act_done, "mh", n, hf)
            for n in range(KC):
                square("n2", n)
            act_norm("n2", SHIFT2)
            act_parts("n2", SHIFT2)
            u = U_FFN
            for first, many in FGROUPS:
                for f in range(first, first + many):
                    for hf in range(2):
                        act.wait_ge(pe_done, at("unit", u, 1))
                        if f:
                            act.wait_ge(dve_done, at("fconv", f - 1, 1))
                        else:
                            act.wait_ge(dve_done, at("lo", "n2", 15))
                        act.wait_ge(act_done, now(act_done))
                        act.activation(M[0][:, hf * HALF:(hf + 1) * HALF], PS[:, 2 * (u % 2) + hf, :],
                                       ACT.Copy).then_inc(act_done, 1)
                        step(act_done, "fa", f, hf)
                    names[("free", u)] = names[("fa", f, 1)]
                    for hf in range(2):
                        act.wait_ge(dve_done, at("fconv", f, hf))
                        act.wait_ge(act_done, now(act_done))
                        act.activation(yt[:, hf, :], yt[:, hf, :], ACT.Gelu).then_inc(act_done, 1)
                        step(act_done, "fg", f, hf)
                    for hf in range(2):
                        act.wait_ge(dve_done, at("fz", f, hf))
                        if first:
                            act.wait_ge(pe_done, at("unit", U_FFN + 2 * first + KC * FGROUPS.index((first, many)) - 1, 1))
                        act.wait_ge(act_done, now(act_done))
                        act.activation(opB[:, 0, f - first, hf * HALF:(hf + 1) * HALF], yt[:, hf, :],
                                       ACT.Copy).then_inc(act_done, 1)
                        step(act_done, "fh", f, hf)
                    u += 2
                u += KC
            for n in range(KC):
                square("fin2", n)
            act_norm("fin2", None)
            for tb in range(NT):
                act.wait_ge(dve_done, at("row_out", tb))
                act.dma_start(out[0, tb * P:(tb + 1) * P, :], M[tb % 4 + 1][:]).then_inc(row_gone[tb % 4], 16)
                step(row_gone[tb % 4], "row_gone", tb, by=16)
            for tb in range(NT - 4, NT):
                act.wait_ge(row_gone[tb % 4], at("row_gone", tb))

        @block.vector
        def _(dve):
            def mod_steps(pieces):
                for n in pieces:
                    g = n // MOD_PIECES
                    kc, h = divmod(n % MOD_PIECES, 2)
                    acc = mod_acc[:, h * HALF:(h + 1) * HALF]
                    src = SILU_C + 8 * MODS[g][2] + kc
                    c = small[:, src:src + 1]
                    dve.wait_ge(mod_in[n % 2], at("mod_in", n))
                    dve.wait_ge(act_done, at("silu_c"))
                    if g:
                        dve.wait_ge(pe_done, at("mod_sum", g - 1))
                    if kc == 0:
                        dve.wait_ge(dve_done, now(dve_done))
                        dve.tensor_scalar(acc, mod_raw[:, n % 2, :], c, None, ALU.mult).then_inc(dve_done, 1)
                        step(dve_done, "mod_step", n)
                    else:
                        dve.wait_ge(dve_done, now(dve_done))
                        dve.scalar_tensor_tensor(out=acc, in0=mod_raw[:, n % 2, :], scalar=c, in1=acc,
                                                 op0=ALU.mult, op1=ALU.add).then_inc(dve_done, 1)
                        step(dve_done, "mod_step", n)

            def mod_unit(u):
                if u > 0 and u % 4 == 0 and u <= MOD_UNITS:
                    mod_out(FIRST_MODS + u // 4 - 1)
                if u < MOD_UNITS:
                    n = FIRST_MODS * MOD_PIECES + u * MOD_STEPS
                    mod_steps(range(n, n + MOD_STEPS))

            def mod_out(g):
                name, part, _ = MODS[g]
                b = C[MOD_BIAS[name]] + part * KC
                dve.wait_ge(pe_done, at("mod_sum", g))
                dve.wait_ge(dve_done, now(dve_done))
                dve.tensor_tensor(mod[:, g, :], PS[:, 6, 0:KC], cols[:, b:b + KC], ALU.add).then_inc(dve_done, 1)
                step(dve_done, "mod_out", g)

            def gains(gname, scale):
                g = cols[:, C[gname]:C[gname] + KC]
                dve.wait_ge(dve_done, now(dve_done))
                dve.scalar_tensor_tensor(out=small[:, GS:GS + KC], in0=mod[:, scale, :], scalar=1.0, in1=g,
                                         op0=ALU.add, op1=ALU.mult).then_inc(dve_done, 1)
                step(dve_done)

            def sq_add(n, j):
                slot = M[0] if j % 2 == 0 else M[2]
                if j == 0:
                    dve.wait_ge(act_done, at("sq", n, j))
                    dve.wait_ge(dve_done, now(dve_done))
                    dve.tensor_copy(M[1][:], slot[:]).then_inc(dve_done, 1)
                    step(dve_done, "sq_add", n, j)
                else:
                    dve.wait_ge(act_done, at("sq", n, j))
                    dve.wait_ge(dve_done, now(dve_done))
                    dve.tensor_tensor(M[1][:], M[1][:], slot[:], ALU.add).then_inc(dve_done, 1)
                    step(dve_done, "sq_add", n, j)
                if j == KC - 1:
                    names[("ssum", n)] = names[("sq_add", n, j)]

            def parts(n, gname, scale, last_use):
                gains(gname, scale)
                for x in range(2 * KC + 1):
                    if x < 2 * KC:
                        hf, j = divmod(x, KC)
                        t = slice(hf * HALF, (hf + 1) * HALF)
                        dve.wait_ge(act_done, at("rstd", "kv" if n == "b" else n, hf))
                        if x >= 2:
                            dve.wait_ge(act_done, at("hn", n, x - 2))
                        if last_use is not None:
                            dve.wait_ge(pe_done, at(*last_use))
                        dve.wait_ge(dve_done, now(dve_done))
                        dve.tensor_tensor(xn[:, x % 2, :], X[:, j, t], M[1][:, t], ALU.mult).then_inc(dve_done, 1)
                        step(dve_done, "xn", n, x)
                    if x:
                        y = x - 1
                        hf, j = divmod(y, KC)
                        t = slice(hf * HALF, (hf + 1) * HALF)
                        dve.wait_ge(act_done, at("hi", n, y))
                        dve.wait_ge(dve_done, now(dve_done))
                        dve.tensor_tensor(opA[:, 1, j, t], hn[:, y % 2, :], opA[:, 0, j, t].bitcast(F32),
                                          ALU.subtract).then_inc(dve_done, 1)
                        step(dve_done, "lo", n, y)
                        names[("h_" + n, j, hf)] = names[("lo", n, y)]

            dve.wait_ge(dve_done, now(dve_done))
            dve.memset(vec_rows[:], 0.0).then_inc(dve_done, 1)
            step(dve_done, "vec_zero")
            dve.wait_ge(pe_done, at("vec_T"))
            dve.wait_ge(dve_done, now(dve_done))
            dve.tensor_copy(cols[:], PS[:, 7, 0:3 * P]).then_inc(dve_done, 1)
            step(dve_done, "cols")
            for i in range(2):
                dve.wait_ge(vec_in, at("vec_in"))
                dve.wait_ge(dve_done, now(dve_done))
                dve.tensor_tensor(M[0][:, 512 + 64 * i:576 + 64 * i], M[0][:, 128 * i:128 * i + 64],
                                  M[0][:, 128 * i + 64:128 * i + 128], ALU.mult).then_inc(dve_done, 1)
                step(dve_done)
            dve.wait_ge(dve_done, now(dve_done))
            dve.reduce_sum(small[:, LAM:LAM + 2], M[0][:, 512:640].rearrange("p (i d) -> p i d", i=2), AX_X).then_inc(dve_done, 1)
            step(dve_done, "lam_sum")
            for j in range(KC):
                sq_add("a", j)
            for g in range(FIRST_MODS):
                mod_steps(range(g * MOD_PIECES, (g + 1) * MOD_PIECES))
                mod_out(g)
            dve.wait_ge(act_done, at("lam_exp"))
            dve.wait_ge(dve_done, now(dve_done))
            dve.scalar_tensor_tensor(out=small[:, LAMS:LAMS + 1], in0=small[:, LAM + 3:LAM + 4],
                                     scalar=-LAM_INIT, in1=small[:, LAM + 2:LAM + 3], op0=ALU.add,
                                     op1=ALU.subtract).then_inc(dve_done, 1)
            step(dve_done)
            dve.wait_ge(dve_done, now(dve_done))
            dve.tensor_scalar(small[:, NSINK:NSINK + 8], small[:, SINK:SINK + 8], -1.0, None, ALU.mult).then_inc(dve_done, 1)
            step(dve_done)
            dve.wait_ge(dve_done, now(dve_done))
            dve.tensor_scalar(small[:, SUBG:SUBG + 1], cols[:, C["diff_subln_g_2"]:C["diff_subln_g_2"] + 1],
                              1.0 - LAM_INIT, None, ALU.mult).then_inc(dve_done, 1)
            step(dve_done)
            parts("a", "a_norm_g", A_SCALE, None)
            cw = C["a_conv_w"]

            def conv(src, w, j, kc, hf, bias_col, name):
                t0 = hf * HALF
                b = None if bias_col is None else cols[:, bias_col:bias_col + 1]
                o = yt[:, hf, :]
                w_of = lambda tap: cols[:, w + tap * kc + j:w + tap * kc + j + 1]
                if b is None:
                    dve.wait_ge(dve_done, now(dve_done))
                    dve.tensor_scalar(o, src[:, t0:t0 + HALF], w_of(2), None, ALU.mult).then_inc(dve_done, 1)
                    step(dve_done)
                else:
                    dve.wait_ge(dve_done, now(dve_done))
                    dve.tensor_scalar(o, src[:, t0:t0 + HALF], w_of(2), b, ALU.mult, ALU.add).then_inc(dve_done, 1)
                    step(dve_done)
                for tap, back in ((1, 1), (0, 2)):
                    lo = max(0, back - t0)
                    dve.wait_ge(dve_done, now(dve_done))
                    dve.scalar_tensor_tensor(out=o[:, lo:], in0=src[:, t0 + lo - back:t0 + HALF - back],
                                             scalar=w_of(tap), in1=o[:, lo:], op0=ALU.mult, op1=ALU.add).then_inc(dve_done, 1)
                    step(dve_done, *(name or ()))

            for j in range(KC):
                u = U_AIN + 4 * j
                mod_unit(u)
                mod_unit(u + 1)
                for hf in range(2):
                    t = slice(hf * HALF, (hf + 1) * HALF)
                    dve.wait_ge(pe_done, at("unit", u + 1, 1))
                    dve.wait_ge(act_done, at("cs", j, hf))
                    dve.wait_ge(dve_done, now(dve_done))
                    dve.tensor_tensor(M[0][:, t], cs[:, hf, :], PS[:, 2 * ((u + 1) % 2) + hf, :], ALU.mult).then_inc(dve_done, 1)
                    step(dve_done, "cu", j, hf)
                names[("free", u + 1)] = names[("cu", j, 1)]
                for hf in range(2):
                    if j:
                        dve.wait_ge(act_done, at("yh", j - 1, hf))
                    conv(M[0], cw, j, KC, hf, None, None)
                mod_unit(u + 2)
                for hf in range(2):
                    dve.wait_ge(pe_done, at("unit", u + 2, 1))
                    dve.wait_ge(dve_done, now(dve_done))
                    dve.tensor_tensor(yt[:, hf, :], yt[:, hf, :], PS[:, 2 * ((u + 2) % 2) + hf, :], ALU.mult).then_inc(dve_done, 1)
                    step(dve_done)
                did_free = now(dve_done)
                names[("free", u + 2)] = did_free
                mod_unit(u + 3)
                for hf in range(2):
                    dve.wait_ge(act_done, at("sz", j, hf))
                    dve.wait_ge(dve_done, now(dve_done))
                    dve.tensor_tensor(yt[:, hf, :], yt[:, hf, :], cs[:, hf, :], ALU.mult).then_inc(dve_done, 1)
                    step(dve_done, "yz", j, hf)
                for hf in range(2):
                    t = slice(hf * HALF, (hf + 1) * HALF)
                    dve.wait_ge(act_done, at("yh", j, hf))
                    dve.wait_ge(dve_done, now(dve_done))
                    dve.tensor_tensor(opB[:, 1, j, t], yt[:, hf, :], opB[:, 0, j, t].bitcast(F32),
                                      ALU.subtract).then_inc(dve_done, 1)
                    step(dve_done, "y", j, hf)

            def residual(n, u, gate, j, first_need=None):
                for hf in range(2):
                    t = slice(hf * HALF, (hf + 1) * HALF)
                    dve.wait_ge(pe_done, at("unit", u, 1))
                    if first_need is not None:
                        dve.wait_ge(x_moved, at(*first_need))
                    dve.wait_ge(dve_done, now(dve_done))
                    dve.scalar_tensor_tensor(out=X[:, j, t], in0=PS[:, 2 * (u % 2) + hf, :],
                                             scalar=mod[:, gate, j:j + 1], in1=X[:, j, t], op0=ALU.mult,
                                             op1=ALU.add).then_inc(dve_done, 1)
                    step(dve_done, "x_new", n, j)
                names[("free", u)] = names[("x_new", n, j)]

            def residuals(n, u0, gate, first_need=None, sums=True):
                for j in range(KC):
                    mod_unit(u0 + j)
                    residual(n, u0 + j, gate, j, first_need)
                    if sums:
                        if j:
                            sq_add(n, j - 1)
                if sums:
                    sq_add(n, KC - 1)

            residuals("kv", U_AOUT, A_GATE)
            parts("kv", "kv_norm_g", KV_SCALE, ("unit", U_AOUT - 1, 1))
            names[("norm_end",)] = now(dve_done)

            def hl_lo(u, x, scale):
                s = u % 2
                dve.wait_ge(act_done, at("hl_hi", u))
                dve.wait_ge(dve_done, now(dve_done))
                dve.scalar_tensor_tensor(out=stage[:, x % 2, 1, :], in0=banks(2 * s),
                                         scalar=scale, in1=stage[:, x % 2, 0, :].bitcast(F32), op0=ALU.mult,
                                         op1=ALU.subtract).then_inc(dve_done, 1)
                step(dve_done, "hl_lo", u)
                names[("free", u)] = names[("hl_lo", u)]

            def v_lo(u, x, kind):
                s = u % 2
                src = PS[:, 4:6, :].rearrange("p b (k e d) -> p (b k) e d", k=4, e=2)
                if kind in ("stick", "swa"):
                    for e in range(2):
                        place = 0 if kind == "swa" else e
                        v = vstage[:, s, e, :].rearrange("p (k s d) -> p k s d", k=NT, s=2)
                        dve.wait_ge(act_done, at("v_hi", u))
                        dve.wait_ge(dve_done, now(dve_done))
                        dve.tensor_tensor(v[:, :, 1 - place, :], src[:, :, e, :], v[:, :, place, :].bitcast(F32),
                                          ALU.subtract).then_inc(dve_done, 1)
                        step(dve_done, "v_split", u)
                else:
                    dve.wait_ge(act_done, at("v_hi", u))
                    dve.wait_ge(dve_done, now(dve_done))
                    dve.tensor_tensor(vstage[:, s, 1, :], banks(4),
                                      vstage[:, s, 0, :].bitcast(F32), ALU.subtract).then_inc(dve_done, 1)
                    step(dve_done, "v_split", u)

            for n in range(KC):
                mod_unit(U_KV + n)
                hl_lo(U_KV + n, n, 1.0)
            mod_unit(U_KV + KC)
            for n in range(KC):
                v_lo(U_KV + KC + n, n, "stick")
            parts("b", "b_norm_g", B_SCALE, ("unit", U_QZ - 1, 1))
            names[("x_free", 0)] = now(dve_done)
            for n in range(KC):
                hl_lo(U_QZ + n, n, QSCALE)
            stick_dve(dve)
            residuals("fin1", U_BOUT, B_GATE, ("x_back", 0))

            def scale_x(n, gname):
                for j in range(KC):
                    c = C[gname] + j
                    dve.wait_ge(act_done, at("rstd", n, 0))
                    dve.wait_ge(act_done, at("rstd", n, 1))
                    dve.wait_ge(dve_done, now(dve_done))
                    dve.scalar_tensor_tensor(out=X[:, j, :], in0=X[:, j, :], scalar=cols[:, c:c + 1],
                                             in1=M[1][:], op0=ALU.mult, op1=ALU.mult).then_inc(dve_done, 1)
                    step(dve_done, "x_" + n, j)

            scale_x("fin1", "final_norm_g")
            for j in range(KC):
                names[("x_new", "n1", j)] = names[("x_fin1", j)]
            for j in range(KC):
                sq_add("n1", j)
            parts("n1", "norm1_g_2", SCALE1, ("unit", U_IN2 - 1, 1))
            names[("x_free", 1)] = now(dve_done)
            for n in range(13):
                hl_lo(U_IN2 + n, n, -QSCALE if n < 8 else 1.0)
            for n in range(5):
                v_lo(U_IN2 + 13 + n, n, "diff" if n else "swa")
            second_dve(dve)
            for n in range(KC):
                u = U_BRANCH + n
                s = u % 2
                for hf in range(2):
                    t = slice(hf * HALF, (hf + 1) * HALF)
                    dve.wait_ge(pe_done, at("unit", u, 1))
                    if n:
                        dve.wait_ge(act_done, at("mh", n - 1, hf))
                    dve.wait_ge(dve_done, now(dve_done))
                    dve.tensor_tensor(d_o[:, hf, :], gates[:, n, t], PS[:, 2 * s + hf, :], ALU.mult).then_inc(dve_done, 1)
                    step(dve_done)
                    dve.wait_ge(pe_done, at("sec_pv", len(PIECES) - 2))
                    dve.wait_ge(dve_done, now(dve_done))
                    dve.tensor_tensor(M[4 - 1][:, t], gates[:, KC + n, t], PS[:, 4 + 2 * s + hf, :], ALU.mult).then_inc(dve_done, 1)
                    step(dve_done)
                names[("free", u)] = now(dve_done)
                for hf in range(2):
                    t = slice(hf * HALF, (hf + 1) * HALF)
                    dve.wait_ge(dve_done, now(dve_done))
                    dve.tensor_tensor(d_o[:, hf, :], d_o[:, hf, :], M[3][:, t], ALU.add).then_inc(dve_done, 1)
                    step(dve_done, "mz", n, hf)
                for hf in range(2):
                    t = slice(hf * HALF, (hf + 1) * HALF)
                    dve.wait_ge(act_done, at("mh", n, hf))
                    dve.wait_ge(dve_done, now(dve_done))
                    dve.tensor_tensor(opB[:, 1, n, t], d_o[:, hf, :], opB[:, 0, n, t].bitcast(F32),
                                      ALU.subtract).then_inc(dve_done, 1)
                    step(dve_done, "merged", n, hf)
            residuals("n2", U_OUT2, GATE1, ("x_back", 1))
            parts("n2", "norm2_g_2", SCALE2, ("unit", U_OUT2 - 1, 1))
            u = U_FFN
            for gi, (first, many) in enumerate(FGROUPS):
                for f in range(first, first + many):
                    for hf in range(2):
                        dve.wait_ge(act_done, at("fa", f, 1))
                        if f:
                            dve.wait_ge(act_done, at("fh", f - 1, hf))
                        conv(M[0], C["conv_w_2"], f, FC, hf, C["conv_b_2"] + f, ("fconv", f, hf))
                    for hf in range(2):
                        dve.wait_ge(act_done, at("fg", f, hf))
                        dve.wait_ge(pe_done, at("unit", u + 1, 1))
                        dve.wait_ge(dve_done, now(dve_done))
                        dve.tensor_tensor(yt[:, hf, :], yt[:, hf, :], PS[:, 2 * ((u + 1) % 2) + hf, :], ALU.mult).then_inc(dve_done, 1)
                        step(dve_done, "fz", f, hf)
                    names[("free", u + 1)] = names[("fz", f, 1)]
                    for hf in range(2):
                        t = slice(hf * HALF, (hf + 1) * HALF)
                        dve.wait_ge(act_done, at("fh", f, hf))
                        dve.wait_ge(dve_done, now(dve_done))
                        dve.tensor_tensor(opB[:, 1, f - first, t], yt[:, hf, :],
                                          opB[:, 0, f - first, t].bitcast(F32), ALU.subtract).then_inc(dve_done, 1)
                        step(dve_done, "ff", f, hf)
                    u += 2
                end = gi == len(FGROUPS) - 1
                residuals("fin2" if end else ("g", gi), u, GATE2, None, sums=end)
                u += KC
            scale_x("fin2", "final_g_2")
            for tb in range(NT):
                row = M[tb % 4 + 1]
                dve.wait_ge(pe_done, at("row_T", tb))
                if tb >= 4:
                    dve.wait_ge(row_gone[(tb - 4) % 4], at("row_gone", tb - 4))
                dve.wait_ge(dve_done, now(dve_done))
                dve.tensor_copy(row[:], banks(2 * (tb % 2))).then_inc(dve_done, 1)
                step(dve_done, "row_out", tb)

    return names


def kernel(**inputs):
    import concourse.bacc as bacc
    from concourse.bass_utils import run_bass_kernel_spmd

    arrays = {f"in_{k}": np.ascontiguousarray(v) for k, v in inputs.items()}
    known = {}
    for _ in range(2):
        nc = bacc.Bacc("TRN2", target_bir_lowering=False, num_devices=1)
        args = {k[3:]: nc.dram_tensor(k, list(v.shape), F32, kind="ExternalInput").ap() for k, v in arrays.items()}
        out = nc.dram_tensor("out_0", [1, T, D], F32, kind="ExternalOutput").ap()
        known = program(nc, args, out, known)
    r = run_bass_kernel_spmd(nc, [arrays], core_ids=[0])
    return r.results[0]["out_0"]
```

```python
from contextlib import ExitStack

import numpy as np

import concourse.bass as bass
from concourse import mybir

F32 = mybir.dt.float32
F32R = mybir.dt.float32r
ALU = mybir.AluOpType
ACT = mybir.ActivationFunctionType
AX_X = mybir.AxisListType.X

P = 128
T = 1024
D = 1024
KC = D // P
HALF = T // 2
NQ = HALF // P
NT = T // P
DH = 64
HEADS = 16
EPS = 1e-6
MASKED = -1e30
SWA_HEADS = 8
DIFF_HEADS = 4
LAM_INIT = 0.8 - 0.6
D_FF = 2816
FC = D_FF // P
FGROUPS = [(0, 8), (8, 8), (16, 6)]
SWA_COL, KA_COL, VA_COL, QD_COL, KD_COL, VD_COL, GA_COL, GD_COL = 0, 512, 640, 768, 1280, 1792, 2304, 3328
QSCALE = DH ** -0.5

ROWS0 = [("c", 8), ("c_2", 8), ("a_mod_b", 24), ("a_norm_g", 8), ("a_conv_w", 24), ("kv_mod_b", 16),
         ("b_mod_b", 24), ("kv_norm_g", 8), ("b_norm_g", 8)]
ROWS1 = [("b_ada_2", 48), ("final_norm_g", 8), ("norm1_g_2", 8), ("norm2_g_2", 8), ("final_g_2", 8),
         ("conv_b_2", 22), ("diff_subln_g_2", 1)]
ROWS2 = [("conv_w_2", 66)]
MODS = [("a_mod_w", 0, 0), ("a_mod_w", 1, 0), ("a_mod_w", 2, 0), ("kv_mod_w", 0, 0), ("kv_mod_w", 1, 0),
        ("b_mod_w", 0, 0), ("b_mod_w", 1, 0), ("b_mod_w", 2, 0)] + [("w_ada_2", g, 1) for g in range(6)]
MOD_BIAS = {"a_mod_w": "a_mod_b", "kv_mod_w": "kv_mod_b", "b_mod_w": "b_mod_b", "w_ada_2": "b_ada_2"}
A_SHIFT, A_SCALE, A_GATE, KV_SHIFT, KV_SCALE, B_SHIFT, B_SCALE, B_GATE = range(8)
SHIFT1, SCALE1, GATE1, SHIFT2, SCALE2, GATE2 = range(8, 14)
MOD_PIECES = 2 * KC
MOD_STEPS = 4
FIRST_MODS = 2
MOD_UNITS = (14 - FIRST_MODS) * MOD_PIECES // MOD_STEPS


def unit_list():
    units = []
    for j in range(KC):
        for part in (1, 2, 0, 3):
            units.append(("a_w_in", part * D + j * P, 0, KC))
    units += [("a_w_out", n * P, 0, KC) for n in range(KC)]
    units += [("w_kv", n * P, 0, KC) for n in range(2 * KC)]
    units += [("b_w_qz", n * P, 0, KC) for n in range(2 * KC)]
    units += [("b_w_out", n * P, 0, KC) for n in range(KC)]
    cols = ([SWA_COL + n * P for n in range(4)] + [QD_COL + n * P for n in range(4)] + [KA_COL]
            + [KD_COL + n * P for n in range(4)] + [VA_COL] + [VD_COL + n * P for n in range(4)]
            + [GA_COL + n * P for n in range(8)] + [GD_COL + n * P for n in range(8)])
    units += [("w_in_2", col, 0, KC) for col in cols]
    units += [("branch", n * P, 0, KC) for n in range(KC)]
    units += [("w_out_2", n * P, 0, KC) for n in range(KC)]
    for first, many in FGROUPS:
        for f in range(first, first + many):
            units += [("w_up_2", f * P, 0, KC), ("w_up_2", D_FF + f * P, 0, KC)]
        units += [("w_down_2", n * P, first * P, many) for n in range(KC)]
    return units


UNITS = unit_list()
U_AIN = 0
U_AOUT = U_AIN + 4 * KC
U_KV = U_AOUT + KC
U_QZ = U_KV + 2 * KC
U_BOUT = U_QZ + 2 * KC
U_IN2 = U_BOUT + KC
U_BRANCH = U_IN2 + 34
U_OUT2 = U_BRANCH + KC
U_FFN = U_OUT2 + KC

FIRST_V = (U_KV + KC, U_IN2 + 13)

LAG_B, LAG_A, LAG_H, LAG_V = 3, 4, 5, 6
RING = (0, 1, 2, 3, 6, 7)
AFTER_PAIR = {U_AIN + 2: "a", U_KV + 2: "kv", U_QZ + 2: "b", U_IN2 + 2: "n1", U_FFN + 2: "n2"}

STICK = [(0, kb) for kb in range(NQ - 1, -1, -1)] + [(1, kb) for kb in range(NT - 1, -1, -1)]


SWA_STEPS = 2 * SWA_HEADS
STEPS = SWA_STEPS + NT * DIFF_HEADS


def second_schedule():
    events, pieces, later = [], [], []
    valued = 0

    def pass_on():
        for item in list(later):
            item[0] -= 1
            if item[0] == 0:
                later.remove(item)
                kind, n = item[1]
                if kind == "rms":
                    turn((None, n))
                    later.append([1, ("scaled", n)])
                    later.append([2, ("parts", n)])
                else:
                    events.append((kind, n))

    def values_upto(c):
        nonlocal valued
        while valued <= min(c, len(pieces) - 1):
            x, p = pieces[valued]
            if x is not None:
                events.append(("values", valued))
                i = (x - SWA_STEPS) % NT
                if x < SWA_STEPS:
                    if p == 1:
                        later.append([2, ("out", x)])
                elif i % NQ == NQ - 1 and p == i // NQ:
                    events.append(("square", (x - SWA_STEPS) // NQ))
                    later.append([2, ("rms", (x - SWA_STEPS) // NQ)])
            valued += 1

    def turn(piece):
        values_upto(len(pieces) - 2)
        pieces.append(piece)
        events.append(("turn", len(pieces) - 1) if piece[0] is not None else ("rms", piece[1]))

    line = list(range(SWA_STEPS)) + [None] + list(range(SWA_STEPS, STEPS)) + [None, None]
    events.append(("scores", 0))
    for t, x in enumerate(line):
        former = line[t - 1] if t else None
        second = t > SWA_STEPS
        if former is not None and not second:
            events.append(("norm", former))
        if x is not None:
            events.append(("probs", x))
        if former is not None and second:
            events.append(("norm", former))
        y = line[t - 2] if t >= 2 else None
        pieces_of = [] if y is None else range(2 if y < SWA_STEPS else (y - SWA_STEPS) % NT // NQ + 1)
        for p in pieces_of:
            turn((y, p))
            if p == 0 and former is not None:
                events.append(("scales", former))
            pass_on()
        if not pieces_of and former is not None:
            events.append(("scales", former))
        if t + 1 < len(line) and line[t + 1] is not None:
            events.append(("scores", line[t + 1]))
        if x is not None:
            events.append(("exps", x))
    values_upto(len(pieces))
    while later:
        pass_on()
    return events, pieces


SECOND, PIECES = second_schedule()
PLACE = {piece: c for c, piece in enumerate(PIECES)}


def last_piece(x):
    return max(c for c, (y, _) in enumerate(PIECES) if y == x)


def program(nc, a, out, known):
    names = {}
    ctx = ExitStack()
    with ctx:
        def sem(name):
            return ctx.enter_context(nc.semaphore(name))

        base = -(-nc.sbuf_base // 64) * 64
        KIB = 1024
        AT_X, AT_A, AT_B = base, base + 32 * KIB, base + 96 * KIB
        AT_W = base + 160 * KIB
        AT_M = AT_W + 24 * KIB
        AT_C = AT_M + 20 * KIB

        def at(name, offset, shape, dt=F32):
            return nc.alloc_sbuf_tensor_at(name, [P] + shape, dt, offset=offset)

        X = at("X", AT_X, [KC, T])
        opA = at("opA", AT_A, [2, KC, T], F32R)
        opB = at("opB", AT_B, [2, KC, T], F32R)
        w_raw = at("w_raw", AT_W, [2, KC, P])
        w_hi = at("w_hi", AT_W + 8 * KIB, [2, KC, P], F32R)
        w_lo = at("w_lo", AT_W + 16 * KIB, [2, KC, P], F32R)
        M = [at(f"M{i}", AT_M + 4 * KIB * i, [T]) for i in range(5)]
        ident = at("ident", AT_C, [P])
        ones = at("ones", AT_C + 512, [P])
        cols = at("cols", AT_C + 1024, [3 * P])
        small = at("small", AT_C + 2560, [100])
        mod = at("mod", AT_C + 2560 + 416, [14, KC])
        x_rows = at("x_rows", AT_B, [NT, D])
        vec_rows = at("vec_rows", AT_A, [3, P])
        lam_rows = at("lam_rows", AT_A + 28 * KIB, [640])
        first_mods = [at("first_mod0", AT_A + 32 * KIB, [KC, D]), at("first_mod1", AT_B + 32 * KIB, [KC, D])]
        mod_acc = M[3]
        mod_raw = at("mod_raw", AT_M + 16 * KIB, [2, HALF])
        cs = at("cs", AT_M + 4 * KIB, [2, HALF])
        yt = at("yt", AT_M + 8 * KIB, [2, HALF])
        hn = at("hn", AT_M + 8 * KIB, [2, HALF])
        xn = at("xn", AT_M, [2, HALF])
        stage = at("stage", AT_B + 32 * KIB, [2, 2, T], F32R)
        vstage = at("vstage", AT_B + 48 * KIB, [2, 2, T], F32R)
        vt = at("vt", AT_M + 16 * KIB, [T])
        sz = at("sz", AT_B, [KC, T])
        hin = at("hin", AT_B + 32 * KIB, [2, 4, T], F32R)
        s_t = at("s_t", AT_X, [3, HALF])
        s_sp = at("s_sp", AT_X + 6 * KIB, [3, HALF])
        s_p = at("s_p", AT_X + 12 * KIB, [3, HALF])
        s_a = at("s_a", AT_X + 18 * KIB, [3, HALF])
        s_ah = at("s_ah", AT_M + 4 * KIB, [3, HALF], F32R)
        s_al = at("s_al", AT_M + 10 * KIB, [3, HALF], F32R)
        s_o = at("s_o", AT_X + 24 * KIB, [2, HALF])
        s_tmp = at("s_tmp", AT_X + 28 * KIB, [HALF])
        tri = at("tri", AT_X + 30 * KIB, [P])
        nones = at("nones", AT_X + 30 * KIB + 512, [P])
        ident_r = at("ident_r", AT_X + 31 * KIB, [P], F32R)
        mask_r = at("mask_r", AT_X + 31 * KIB + 512, [P], F32R)
        masks = at("masks", AT_M, [P])
        keys = at("keys", AT_X, [2, 2, T], F32R)
        vals = [[at("vals00", AT_X + 16 * KIB, [T], F32R), at("vals01", AT_X + 20 * KIB, [T], F32R)],
                [at("vals10", AT_W + 12 * KIB, [T], F32R), at("vals11", AT_W + 20 * KIB, [T], F32R)]]
        bias = at("bias", AT_X + 24 * KIB, [2, T])
        prob = [at("prob0", AT_M, [T]), at("prob1", AT_M + 4 * KIB, [T]), at("prob2", AT_W, [T]),
                at("prob3", AT_W + 4 * KIB, [T])]
        pair = [(prob[2], prob[3]), (at("prob4", AT_W + 8 * KIB, [T]), at("prob5", AT_W + 16 * KIB, [T])),
                (prob[0], prob[1])]
        swa_diag = at("swa_diag", AT_W + 4 * KIB, [2, NQ, P])
        diff_diag = at("diff_diag", AT_X + 28 * KIB, [4, P])
        aT = at("aT", AT_M + 8 * KIB, [2, 2, HALF], F32R)
        d_o = at("d_o", AT_M + 16 * KIB, [2, HALF])
        gates = at("gates", AT_B, [2 * KC, T])

        PS = ctx.enter_context(nc.psum_tensor("PS", [P, 8, HALF], F32))

        def scratch(name, shape, dt=F32):
            return nc.dram_tensor(name, shape, dt).ap()

        x_dram = scratch("x_dram", [P, KC * T], F32)
        k_dram = scratch("k_dram", [2, D, T])
        q_dram = scratch("q_dram", [2, D, T])
        v_dram = scratch("v_dram", [KC, P, 2, T])
        q2_dram = scratch("q2_dram", [2, D, T])
        k2_dram = scratch("k2_dram", [2, D, T])
        va_dram = scratch("va_dram", [P, 2, T])
        vd_dram = scratch("vd_dram", [DIFF_HEADS, P, 2, T])

        def banks(b):
            return PS[:, b:b + 2, :].rearrange("p b t -> p (b t)")

        pe_done, act_done, dve_done, pool_done = sem("pe_done"), sem("act_done"), sem("dve_done"), sem("pool_done")
        vec_in = [sem(f"vec_in{s}") for s in range(2)]
        first_mod_in = [[sem(f"first_mod_in{g}_{kc}") for kc in range(KC)] for g in range(FIRST_MODS)]
        x_in = [sem(f"x_in{tb}") for tb in range(NT)]
        w_in = [sem(f"w_in{s}") for s in range(2)]
        mod_in = [sem(f"mod_in{s}") for s in range(2)]
        x_out = sem("x_out")
        x_back = [sem(f"x_back{j}") for j in range(KC)]
        stored = [sem(f"stored{s}") for s in range(2)]
        v_stored = [sem(f"v_stored{s}") for s in range(2)]
        head_in = [sem(f"head_in{s}") for s in range(2)]
        q_in = [sem(f"q_in{c}") for c in range(KC)]
        k_in, v_in = [sem(f"k_in{s}") for s in range(2)], [sem(f"v_in{s}") for s in range(2)]
        row_gone = [sem(f"row_gone{s}") for s in range(4)]
        total = {}

        def now(s):
            return total.get(id(s), 0)

        def step(s, *name, by=1):
            total[id(s)] = now(s) + by
            if name:
                names[name] = now(s)

        def at(*name):
            return known.get(name, 0)

        def reader(u):
            if u < U_AOUT:
                return act_done if u % 4 in (0, 3) else dve_done
            if u >= U_FFN:
                first = [f for f, many in FGROUPS if U_FFN + 2 * f + KC * FGROUPS.index((f, many)) <= u][-1]
                gi = [f for f, _ in FGROUPS].index(first)
                n = u - (U_FFN + 2 * first + KC * gi)
                return act_done if n < 2 * FGROUPS[gi][1] and n % 2 == 0 else dve_done
            on_act = (range(U_KV + KC, U_QZ), range(U_QZ + KC, U_BOUT), range(U_IN2 + 13, U_BRANCH))
            return act_done if any(u in r for r in on_act) else dve_done

        def col(rows, name):
            at0 = 0
            for t, rs in enumerate((ROWS0, ROWS1, ROWS2)):
                at0 = t * P
                for n, many in rs:
                    if n == name:
                        return at0
                    at0 += many
            raise KeyError(name)

        C = {n: col(None, n) for rs in (ROWS0, ROWS1, ROWS2) for n, _ in rs}
        EPS_COL, SILU_C, GS, SINK, LAM = 0, 1, 17, 25, 33
        LAMS, SUBG, NSINK, MX, RS, RI = 37, 38, 39, 47, 63, 79

        block = ctx.enter_context(nc.Block())

        ROW_PLACES = (2, 3, 4, 0)
        MISC_FREE = {"kv": "a", "fin2": "n2"}

        def source(u):
            name, col0, row0, chunks = UNITS[u]
            if name == "branch":
                return [(a["w_branch_swa_2"][0], col0, 0, 4, 0), (a["w_branch_diff_2"][0], col0, 0, 4, 4)]
            w = a[name]
            if len(w.shape) == 3:
                w = w[0]
            return [(w, col0, row0, chunks, 0)]

        def second_loads(sp):
            def keys_values(load):
                slot = load % 2
                if load >= 2:
                    sp.wait_ge(pe_done, at("sec_S", 8 * load - 9, 0))
                for part in range(2):
                    if load < 2:
                        for place in range(2):
                            sp.dma_start(keys[place * DH:(place + 1) * DH, slot, part, :].bitcast(F32),
                                         k2_dram[part, load * DH:(load + 1) * DH, :]).then_inc(k_in[load % 2], 16)
                            step(k_in[load % 2], "k_in", load, by=16)
                    else:
                        sp.dma_start(keys[:, slot, part, :].bitcast(F32),
                                     k2_dram[part, (load - 1) * P:load * P, :]).then_inc(k_in[load % 2], 16)
                        step(k_in[load % 2], "k_in", load, by=16)
                if load >= 2:
                    sp.wait_ge(pe_done, at("sec_pv", last_piece(8 * load - 9)))
                else:
                    if load:
                        sp.wait_ge(pe_done, at("unit", U_BRANCH - 1, 1))
                for n in range(2):
                    if load >= 2:
                        sp.dma_start(vals[slot][n][:].bitcast(F32), vd_dram[load - 2, :, n, :]).then_inc(v_in[load % 2], 16)
                        step(v_in[load % 2], "v_in", load, by=16)
                    elif n == 0:
                        sp.dma_start(vals[slot][n][:].bitcast(F32), va_dram[:, load, :]).then_inc(v_in[load % 2], 16)
                        step(v_in[load % 2], "v_in", load, by=16)
                    else:
                        src = va_dram[:, load, :].rearrange("p (b s d) -> p b s d", b=NT, s=2)
                        dst = vals[slot][n][:].bitcast(F32).rearrange("p (b s d) -> p b s d", b=NT, s=2)
                        for s in range(2):
                            sp.dma_start(dst[:, :, 1 - s, :], src[:, :, s, :]).then_inc(v_in[load % 2], 16)
                            step(v_in[load % 2], "v_in", load, by=16)

            def queries(c):
                for part in range(2):
                    for hf in range(2):
                        t = slice(hf * HALF, (hf + 1) * HALF)
                        sp.dma_start(opA[:, part, c, t].bitcast(F32), q2_dram[part, c * P:(c + 1) * P, t]).then_inc(q_in[c], 16)
                        step(q_in[c], "q_in", c, by=16)

            sp.wait_ge(stored[(U_IN2 + 11) % 2], at("stored", U_IN2 + 11))
            sp.wait_ge(stored[(U_IN2 + 12) % 2], at("stored", U_IN2 + 12))
            sp.wait_ge(v_stored[(U_IN2 + 16) % 2], at("v_stored", U_IN2 + 16))
            sp.wait_ge(v_stored[(U_IN2 + 17) % 2], at("v_stored", U_IN2 + 17))
            sp.wait_ge(x_out, at("x_out", 1))
            keys_values(0)
            sp.wait_ge(pe_done, at("unit", U_BRANCH - 1, 1))
            for c in range(4):
                queries(c)
                if c == 1:
                    keys_values(1)
            for j in range(DIFF_HEADS):
                queries(4 + j)
            for j in range(DIFF_HEADS):
                keys_values(2 + j)

        def turn_v(pe, u):
            pe.wait_ge(act_done, at("vt", u))
            if not (u in FIRST_V):
                pe.wait_ge(dve_done, at("v_split", u - 1))
            for kb in range(NT):
                ins = pe.transpose(PS[:, 4 + kb // 4, (kb % 4) * P:(kb % 4 + 1) * P], vt[:, kb * P:(kb + 1) * P], ident[:])
            ins.then_inc(pe_done, 1)
            step(pe_done, "v_T", u)

        def cut(g):
            h, i = divmod(g, len(STICK))
            hf, kb = STICK[i]
            return h, i, hf, kb, max(0, (kb - NQ * hf) * P)

        def scores_of(g, q0):
            return PS[:, RING[g % len(RING)], q0:]

        def stick_pe(pe):
            def scores(g):
                h, i, hf, kb, qs = cut(g)
                s = h % 2
                if i == 0:
                    pe.wait_ge(head_in[h % 2], at("head_in", h))
                if g == 0:
                    pe.wait_ge(pool_done, at("stick_consts"))
                if g >= len(RING):
                    pe.wait_ge(act_done, at("stick_a", g - len(RING)))
                q = slice(hf * HALF + qs, (hf + 1) * HALF)
                k = hin[:, s, 0, kb * P:(kb + 1) * P]
                pe.matmul(scores_of(g, qs), k, hin[:, s, 1, q], start=True, stop=False)
                ins = pe.matmul(scores_of(g, qs), k, hin[:, s, 2, q], start=False, stop=True)
                if kb >= NQ * hf:
                    ins = pe.matmul(scores_of(g, qs)[:, 0:P], ident_r[:], mask_r[:], start=False, stop=True,
                                    skip_group_check=True)
                ins.then_inc(pe_done, 1)
                step(pe_done, "stick_s", g)

            def sums(g):
                h, i, hf, kb, qs = cut(g)
                pe.wait_ge(dve_done, at("stick_sp", g))
                ins = pe.matmul(scores_of(g, qs), tri[:], s_sp[:, g % 3, qs:], start=False, stop=True,
                                skip_group_check=True)
                if kb != NQ * hf + NQ - 1:
                    pe.wait_ge(pool_done, at("stick_p", g - 1))
                    qp = max(0, (kb + 1 - NQ * hf) * P)
                    ins = pe.matmul(scores_of(g, qp), nones[:], s_p[:, (g - 1) % 3, qp:], start=False, stop=True,
                                    skip_group_check=True)
                ins.then_inc(pe_done, 1)
                step(pe_done, "stick_b", g)

            def values(g):
                h, i, hf, kb, qs = cut(g)
                s, o = h % 2, 4 + hf
                top = kb == NQ * hf + NQ - 1
                pe.wait_ge(dve_done, at("stick_al", g))
                if h and top:
                    pe.wait_ge(dve_done, at("stick_o", h - 1, hf))
                v = hin[:, s, 3, kb * P:(kb + 1) * P]
                pe.matmul(PS[:, o, qs:], v, s_ah[:, g % 3, qs:], start=top, stop=False, skip_group_check=True)
                ins = pe.matmul(PS[:, o, qs:], v, s_al[:, g % 3, qs:], start=False, stop=(kb == 0),
                                skip_group_check=True)
                ins.then_inc(pe_done, 1)
                step(pe_done, "stick_c", g)
                if i == len(STICK) - 1:
                    names[("stick_free", h)] = names[("stick_c", g)]

            n = HEADS * len(STICK)
            pe.wait_ge(reader(U_BOUT - 1), at("free", U_BOUT - 1))
            pe.wait_ge(reader(U_BOUT - 2), at("free", U_BOUT - 2))
            for g in range(n + LAG_V):
                if g < n:
                    scores(g)
                if 0 <= g - LAG_B < n:
                    sums(g - LAG_B)
                if 0 <= g - LAG_V < n:
                    values(g - LAG_V)

        def piece_width(c):
            x, p = PIECES[c]
            return HALF if x < SWA_STEPS else (min(NQ * p + NQ, (x - SWA_STEPS) % NT + 1) - NQ * p) * P

        def second_pe(pe):
            def swa_scores(x):
                n, hf = divmod(x, 2)
                if x % 4 == 0:
                    pe.wait_ge(q_in[(n // 2)], at("q_in", n // 2))
                if x % 8 == 0:
                    pe.wait_ge(k_in[(n // 4) % 2], at("k_in", n // 4))
                if x >= 2:
                    pe.wait_ge(dve_done, at("sec_p", x - 2, 0))
                r = slice(DH * (n % 2), DH * (n % 2) + DH)
                for b in range(NQ):
                    i = NQ * hf + b
                    pieces = [(0, (i - 1) * P, 2 * P)] if i else [(0, 0, P), (P, 0, P)]
                    for at0, k0, width in pieces:
                        dst = PS[:, 2 * (x % 2) + b // 2, (b % 2) * 2 * P + at0:(b % 2) * 2 * P + at0 + width]
                        for y, (pq, pk) in enumerate(((0, 0), (1, 0), (0, 1))):
                            ins = pe.matmul(dst, opA[r, pq, n // 2, i * P:(i + 1) * P],
                                            keys[r, n // 4, pk, k0:k0 + width], start=(y == 0), stop=(y == 2))
                ins.then_inc(pe_done, 1)
                step(pe_done, "sec_S", x, 0)

            def diff_scores(x):
                j, i = divmod(x - SWA_STEPS, NT)
                if i == 0:
                    pe.wait_ge(q_in[(4 + j)], at("q_in", 4 + j))
                if i == 0:
                    pe.wait_ge(k_in[(2 + j) % 2], at("k_in", 2 + j))
                former = x - 1 if i >= NQ or i == 0 else x - 2
                for m in (1, 0):
                    if former >= SWA_STEPS:
                        pe.wait_ge(dve_done, at("sec_p", former, m))
                    else:
                        pe.wait_ge(dve_done, at("sec_p", SWA_STEPS - 1, 0))
                    r = slice(DH * m, DH * (m + 1))
                    for k0 in range(0, (i + 1) * P, HALF):
                        width = min(HALF, (i + 1) * P - k0)
                        bank = 2 * m + (i % 2 if i < NQ else k0 // HALF)
                        for y, (pq, pk) in enumerate(((0, 0), (1, 0), (0, 1))):
                            ins = pe.matmul(PS[:, bank, 0:width], opA[r, pq, 4 + j, i * P:(i + 1) * P],
                                            keys[r, j % 2, pk, k0:k0 + width], start=(y == 0), stop=(y == 2))
                    ins.then_inc(pe_done, 1)
                    step(pe_done, "sec_S", x, m)

            def turn(c):
                x, p = PIECES[c]
                bank = 4 + c % 2
                if c >= 2 and PIECES[c - 2][0] is None:
                    pe.wait_ge(dve_done, at("sec_lo", c - 2))
                if x < SWA_STEPS:
                    if p == 0:
                        pe.wait_ge(act_done, at("sec_g", x))
                    for y in range(4):
                        ins = pe.matmul(PS[:, bank, y * P:(y + 1) * P], prob[x % 3][:, (4 * p + y) * P:(4 * p + y + 1) * P],
                                        swa_diag[:, x % 2, 2 * p + y // 2, :], start=True, stop=True)
                else:
                    if p == 0:
                        pe.wait_ge(pool_done, at("sec_gd", x))
                    if p == 0:
                        pe.wait_ge(dve_done, at("sec_a", x))
                    i = (x - SWA_STEPS) % NT
                    for kb in range(4 * p, min(4 * p + 4, i + 1)):
                        ins = pe.matmul(PS[:, bank, (kb - 4 * p) * P:(kb - 4 * p + 1) * P],
                                        pair[x % 3][0][:, kb * P:(kb + 1) * P], diff_diag[:, x % 4, :],
                                        start=True, stop=True)
                ins.then_inc(pe_done, 1)
                step(pe_done, "sec_T", c)

            def values(c):
                x, p = PIECES[c]
                if x % 8 == 0 and p == 0:
                    pe.wait_ge(v_in[(x // 8) % 2], at("v_in", x // 8))
                pe.wait_ge(dve_done, at("sec_lo", c))
                if x < SWA_STEPS:
                    n, hf = divmod(x, 2)
                    if x >= 2 and p == 0:
                        pe.wait_ge(dve_done, at("sec_o", x - 2))
                    for b in (2 * p, 2 * p + 1):
                        i = NQ * hf + b
                        steps = [(w, part) for w in range(2) if i or w for part in range(2)]
                        for y, (w, part) in enumerate(steps):
                            kb = i - 1 + w
                            ins = pe.matmul(PS[:, 6 + hf, b * P:(b + 1) * P], vals[n // 4][n % 2][:, kb * P:(kb + 1) * P],
                                            aT[:, c % 2, part, (2 * b + w - 4 * p) * P:(2 * b + w - 4 * p + 1) * P],
                                            start=(y == 0), stop=(y == len(steps) - 1))
                else:
                    j, i = divmod(x - SWA_STEPS, NT)
                    h = 2 * j + i // NQ
                    if i % NQ == 0 and p == 0:
                        pe.wait_ge(dve_done, at("sec_o", SWA_STEPS + h - 2))
                    for kb in range(4 * p, min(4 * p + 4, i + 1)):
                        for y, (pv, pa) in enumerate(((0, 0), (1, 0), (0, 1))):
                            ins = pe.matmul(PS[:, 6 + i // NQ, (i % NQ) * P:(i % NQ + 1) * P],
                                            vals[j % 2][pv][:, kb * P:(kb + 1) * P],
                                            aT[:, c % 2, pa, (kb - 4 * p) * P:(kb - 4 * p + 1) * P],
                                            start=(kb == 0 and y == 0), stop=(kb == i and y == 2))
                ins.then_inc(pe_done, 1)
                step(pe_done, "sec_pv", c)

            def rms(h):
                c = PLACE[None, h]
                pe.wait_ge(act_done, at("sec_sq", h))
                pe.wait_ge(dve_done, at("sec_lo", c - 2))
                pe.matmul(PS[:, 4 + c % 2, :], ones[:], d_o[:, 0, :], start=True, stop=True).then_inc(pe_done, 1)
                step(pe_done, "sec_ss", h)

            pe.wait_ge(reader(U_BRANCH - 1), at("free", U_BRANCH - 1))
            pe.wait_ge(reader(U_BRANCH - 2), at("free", U_BRANCH - 2))
            pe.wait_ge(dve_done, at("v_split", U_IN2 + 17))
            for kind, n in SECOND:
                if kind == "scores" and n < SWA_STEPS:
                    swa_scores(n)
                elif kind == "scores":
                    diff_scores(n)
                elif kind == "turn":
                    turn(n)
                elif kind == "values":
                    values(n)
                elif kind == "rms":
                    rms(n)

        def stick_act(act):
            def output(g):
                h, i, hf, kb, qs = cut(g)
                other = slice(DH * (1 - h % 2), DH * (1 - h % 2) + DH)
                main = slice(DH * (h % 2), DH * (h % 2) + DH)
                act.wait_ge(pe_done, at("stick_c", g))
                if h or hf:
                    act.wait_ge(dve_done, at("stick_o", (2 * h + hf - 1) // 2, (hf + 1) % 2))
                act.activation(s_tmp[main, :], PS[other, 4 + hf, :], ACT.Copy).then_inc(act_done, 1)
                step(act_done, "stick_tmp", h, hf)

            n = HEADS * len(STICK)
            act.preload_act_table_set("natural_log_exp_and_others")
            for g in range(n + LAG_V + 2):
                if g < n:
                    h, i, hf, kb, qs = cut(g)
                    act.wait_ge(pe_done, at("stick_s", g))
                    if g >= 3:
                        act.wait_ge(dve_done, at("stick_sp", g - 3))
                    else:
                        act.wait_ge(x_out, at("x_out", 0))
                    act.activation(s_t[:, g % 3, qs:], scores_of(g, qs), ACT.Abs).then_inc(act_done, 1)
                    step(act_done, "stick_t", g)
                if 0 <= g - 1 < n:
                    e = g - 1
                    h, i, hf, kb, qs = cut(e)
                    if e == 0:
                        act.wait_ge(act_done, at("stick_t", e))
                    act.activation(s_t[:, e % 3, qs:], s_t[:, e % 3, qs:], ACT.Exp, scale=-1.0).then_inc(act_done, 1)
                    step(act_done, "stick_e", e)
                if 0 <= g - LAG_A < n:
                    e = g - LAG_A
                    h, i, hf, kb, qs = cut(e)
                    if g >= n:
                        act.wait_ge(pe_done, at("stick_b", e))
                    if g >= n:
                        act.wait_ge(dve_done, at("stick_al", e - 3))
                    act.activation(s_a[:, e % 3, qs:], scores_of(e, qs), ACT.Exp).then_inc(act_done, 1)
                    step(act_done, "stick_a", e)
                if 0 <= g - 1 < n:
                    e = g - 1
                    h, i, hf, kb, qs = cut(e)
                    act.wait_ge(act_done, at("stick_e", e))
                    act.activation(s_t[:, e % 3, qs:], s_t[:, e % 3, qs:], ACT.Ln, bias=1.0).then_inc(act_done, 1)
                    step(act_done, "stick_l", e)
                e = g - LAG_V - 1
                if 0 <= e < n and e % len(STICK) in (NQ - 1, len(STICK) - 1):
                    output(e)

        def second_act(act):
            act.preload_act_table_set("natural_log_exp_and_others")

            def exps(x):
                n, hf = divmod(x, 2)
                act.wait_ge(dve_done, at("sec_p", x, 0))
                for b in range(NQ):
                    c = x % 4 * 4 + b
                    p = prob[x % 3][:, b * 2 * P:(b + 1) * 2 * P]
                    act.activation(p, p, ACT.Exp, bias=small[:, MX + c:MX + c + 1], scale=-1.0,
                                   accum_out=small[:, RS + c:RS + c + 1]).then_inc(act_done, 1)
                    step(act_done, "sec_e", x, 0)
                c = x % 4 * 4
                act.activation(small[:, RI + c:RI + c + 4], small[:, MX + c:MX + c + 4],
                               ACT.Exp, bias=small[:, SINK + n:SINK + n + 1]).then_inc(act_done, 1)
                step(act_done, "sec_e", x, 0)

            def rows_exp(x):
                w = ((x - SWA_STEPS) % NT + 1) * P
                for m in (1, 0):
                    c = x % 4 * 4 + m
                    p = pair[x % 3][m][:, 0:w]
                    act.wait_ge(dve_done, at("sec_p", x, m))
                    act.activation(p, p, ACT.Exp, bias=small[:, MX + c:MX + c + 1], scale=-1.0,
                                   accum_out=small[:, RS + c:RS + c + 1]).then_inc(act_done, 1)
                    step(act_done, "sec_e", x, m)

            def high(c):
                w = piece_width(c)
                act.wait_ge(pe_done, at("sec_T", c))
                act.activation(aT[:, c % 2, 0, 0:w], PS[:, 4 + c % 2, 0:w], ACT.Copy).then_inc(act_done, 1)
                step(act_done, "sec_hi", c)

            def out(x):
                n, hf = divmod(x, 2)
                other = slice(DH * (1 - n % 2), DH * (1 - n % 2) + DH)
                main = slice(DH * (n % 2), DH * (n % 2) + DH)
                act.wait_ge(pe_done, at("sec_pv", last_piece(x)))
                if n >= 2:
                    act.wait_ge(dve_done, at("swa_out", n // 2 - 1, hf))
                act.activation(d_o[main, hf, :], PS[other, 6 + hf, :], ACT.Copy).then_inc(act_done, 1)
                step(act_done, "sec_tmp", x)

            for kind, n in SECOND:
                if kind == "exps" and n < SWA_STEPS:
                    exps(n)
                elif kind == "exps":
                    rows_exp(n)
                elif kind == "scales" and n < SWA_STEPS:
                    act.wait_ge(dve_done, at("sec_r", n))
                    if n >= 2:
                        act.wait_ge(pe_done, at("sec_T", last_piece(n - 2)))
                    for b in range(NQ):
                        c = RI + n % 4 * 4 + b
                        act.activation(swa_diag[:, n % 2, b, :], ident[:], ACT.Copy, scale=small[:, c:c + 1]).then_inc(act_done, 1)
                        step(act_done, "sec_g", n)
                elif kind == "turn":
                    high(n)
                elif kind == "out":
                    out(n)
                elif kind == "square":
                    act.wait_ge(pe_done, at("sec_pv", last_piece(SWA_STEPS + NQ * n + NQ - 1)))
                    if n == 0:
                        act.wait_ge(dve_done, at("swa_out", 3, 1))
                    act.wait_ge(dve_done, at("sec_o", SWA_STEPS + n - 1))
                    act.activation(d_o[:, 0, :], PS[:, 6 + n % 2, :], ACT.Square).then_inc(act_done, 1)
                    step(act_done, "sec_sq", n)
                elif kind == "rms":
                    act.wait_ge(dve_done, at("sec_lo", PLACE[None, n]))
                    act.activation(d_o[:, 0, :], d_o[:, 0, :], ACT.Ln, bias=small[:, EPS_COL:EPS_COL + 1],
                                   scale=1.0 / P).then_inc(act_done, 1)
                    step(act_done, "sec_ln", n)
                    act.wait_ge(act_done, at("sec_ln", n))
                    act.activation(d_o[:, 0, :], d_o[:, 0, :], ACT.Exp, scale=-0.5).then_inc(act_done, 1)
                    step(act_done, "sec_rr", n)
                elif kind == "parts":
                    j, hf = divmod(n, 2)
                    act.wait_ge(dve_done, at("sec_o", SWA_STEPS + n))
                    act.activation(opA[:, 0, 4 + j, hf * HALF:(hf + 1) * HALF], d_o[:, 1, :], ACT.Copy).then_inc(act_done, 1)
                    step(act_done, "sec_ohi", n)

        def stick_dve(dve):
            def finish(h, hf, part):
                main = slice(DH * (h % 2), DH * (h % 2) + DH)
                j = h // 2
                t = slice(hf * HALF, (hf + 1) * HALF)
                if part == 0:
                    dve.wait_ge(act_done, at("stick_tmp", h, hf))
                    dve.wait_ge(dve_done, now(dve_done))
                    dve.tensor_tensor(s_o[main, hf, :], PS[main, 4 + hf, :], s_tmp[main, :], ALU.add).then_inc(dve_done, 1)
                    step(dve_done, "stick_o", h, hf)
                elif h % 2 and part == 1:
                    dve.wait_ge(reader(U_BOUT - 1), at("free", U_BOUT - 1))
                    dve.wait_ge(dve_done, now(dve_done))
                    dve.tensor_tensor(s_o[:, hf, :], s_o[:, hf, :], sz[:, j, t], ALU.mult).then_inc(dve_done, 1)
                    step(dve_done)
                elif h % 2 and part == 2:
                    dve.wait_ge(pe_done, at("unit", U_BOUT - 1, 1))
                    dve.wait_ge(dve_done, now(dve_done))
                    dve.tensor_copy(opA[:, 0, j, t], s_o[:, hf, :]).then_inc(dve_done, 1)
                    step(dve_done)
                elif h % 2:
                    dve.wait_ge(dve_done, now(dve_done))
                    dve.tensor_tensor(opA[:, 1, j, t], s_o[:, hf, :], opA[:, 0, j, t].bitcast(F32),
                                      ALU.subtract).then_inc(dve_done, 1)
                    step(dve_done, "stick_out", j, hf)
                    names[("h_att", j, hf)] = names[("stick_out", j, hf)]

            n = HEADS * len(STICK)
            for g in range(n + LAG_V + 6):
                if 0 <= g - 2 < n:
                    e = g - 2
                    h, i, hf, kb, qs = cut(e)
                    dve.wait_ge(act_done, at("stick_l", e))
                    if e >= 3:
                        dve.wait_ge(pe_done, at("stick_b", e - 3))
                    if e >= 3 and cut(e - 3)[3] > 0:
                        dve.wait_ge(pool_done, at("stick_p", e - 3))
                    dve.scalar_tensor_tensor(out=s_sp[:, e % 3, qs:], in0=scores_of(e, qs), scalar=0.0,
                                             in1=s_t[:, e % 3, qs:], op0=ALU.max, op1=ALU.add).then_inc(dve_done, 1)
                    step(dve_done, "stick_sp", e)
                if 0 <= g - LAG_H < n:
                    e = g - LAG_H
                    h, i, hf, kb, qs = cut(e)
                    dve.wait_ge(act_done, at("stick_a", e))
                    if e >= 3:
                        dve.wait_ge(pe_done, at("stick_c", e - 3))
                    dve.tensor_copy(s_ah[:, e % 3, qs:], s_a[:, e % 3, qs:]).then_inc(dve_done, 1)
                    step(dve_done, "stick_ah", e)
                    dve.wait_ge(dve_done, at("stick_ah", e))
                    dve.tensor_tensor(s_al[:, e % 3, qs:], s_a[:, e % 3, qs:],
                                      s_ah[:, e % 3, qs:].bitcast(F32), ALU.subtract).then_inc(dve_done, 1)
                    step(dve_done, "stick_al", e)
                for part in range(4):
                    e = g - LAG_V - 2 - part
                    if 0 <= e < n and e % len(STICK) in (NQ - 1, len(STICK) - 1):
                        h, i, hf, kb, qs = cut(e)
                        finish(h, hf, part)
            names[("att_end", 0)] = now(dve_done)
            names[("att_end2", 0)] = now(dve_done)

        def second_dve(dve):
            def swa_probs(x):
                n, hf = divmod(x, 2)
                m = small[:, MX + x % 4 * 4:MX + x % 4 * 4 + 4]
                dve.wait_ge(pe_done, at("sec_S", x, 0))
                dve.wait_ge(pool_done, at("bias_s", n, hf))
                if x >= 3:
                    dve.wait_ge(pe_done, at("sec_T", last_piece(x - 3)))
                else:
                    dve.wait_ge(pool_done, at("split", U_BRANCH - 1))
                for b in range(NQ):
                    k = slice(b * 2 * P, (b + 1) * 2 * P)
                    dve.tensor_tensor_reduce(out=prob[x % 3][:, k], in0=bias[:, hf, k],
                                             in1=banks(2 * (x % 2))[:, k], scale=1.0,
                                             scalar=-MASKED * 1e3, op0=ALU.add, op1=ALU.min,
                                             accum_out=m[:, b:b + 1]).then_inc(dve_done, 1)
                    step(dve_done)
                dve.wait_ge(dve_done, now(dve_done))
                dve.tensor_scalar(m, m, small[:, NSINK + n:NSINK + n + 1], None, ALU.min).then_inc(dve_done, 1)
                step(dve_done, "sec_p", x, 0)

            def diff_probs(x):
                w = ((x - SWA_STEPS) % NT + 1) * P
                if x % 8 == 0:
                    dve.wait_ge(pool_done, at("bias_d"))
                    dve.wait_ge(dve_done, now(dve_done))
                    dve.tensor_scalar(bias[:, 0, :], bias[:, 0, :], 0.25, None, ALU.mult).then_inc(dve_done, 1)
                    step(dve_done)
                for m in (1, 0):
                    bank = 2 * m + (x % 2 if w <= HALF else 0)
                    c = MX + x % 4 * 4 + m
                    dve.wait_ge(pe_done, at("sec_S", x, m))
                    if x > SWA_STEPS:
                        dve.wait_ge(pe_done, at("sec_T", last_piece(max(x - 3, SWA_STEPS - 1))))
                    else:
                        dve.wait_ge(pe_done, at("unit", U_BRANCH - 1, 1))
                    dve.wait_ge(dve_done, now(dve_done))
                    dve.tensor_tensor_reduce(out=pair[x % 3][m][:, 0:w], in0=bias[:, 0, T - w:],
                                             in1=PS[:].rearrange("p b t -> p (b t)")[:, bank * HALF:bank * HALF + w],
                                             scale=1.0, scalar=-MASKED * 1e3, op0=ALU.add, op1=ALU.min,
                                             accum_out=small[:, c:c + 1]).then_inc(dve_done, 1)
                    step(dve_done, "sec_p", x, m)

            def norm(x):
                c = x % 4 * 4
                if x < SWA_STEPS:
                    r = small[:, RI + c:RI + c + 4]
                    dve.wait_ge(act_done, at("sec_e", x, 0))
                    dve.wait_ge(dve_done, now(dve_done))
                    dve.tensor_tensor(r, r, small[:, RS + c:RS + c + 4], ALU.add).then_inc(dve_done, 1)
                    step(dve_done)
                    dve.wait_ge(dve_done, now(dve_done))
                    dve.reciprocal(r, r).then_inc(dve_done, 1)
                    step(dve_done, "sec_r", x)
                else:
                    w = ((x - SWA_STEPS) % NT + 1) * P
                    r = small[:, RI + c:RI + c + 2]
                    dve.wait_ge(act_done, at("sec_e", x, 0))
                    dve.wait_ge(dve_done, now(dve_done))
                    dve.reciprocal(r, small[:, RS + c:RS + c + 2]).then_inc(dve_done, 1)
                    step(dve_done, "sec_r", x)
                    dve.wait_ge(dve_done, now(dve_done))
                    dve.scalar_tensor_tensor(out=small[:, RI + c + 1:RI + c + 2], in0=r[:, 1:2],
                                             scalar=small[:, LAMS:LAMS + 1], in1=small[:, RS + c:RS + c + 1],
                                             op0=ALU.mult, op1=ALU.mult).then_inc(dve_done, 1)
                    step(dve_done)
                    dve.wait_ge(dve_done, now(dve_done))
                    dve.scalar_tensor_tensor(out=pair[x % 3][0][:, 0:w], in0=pair[x % 3][1][:, 0:w],
                                             scalar=small[:, RI + c + 1:RI + c + 2],
                                             in1=pair[x % 3][0][:, 0:w], op0=ALU.mult, op1=ALU.add).then_inc(dve_done, 1)
                    step(dve_done, "sec_a", x)

            def out(x):
                n, hf = divmod(x, 2)
                main = slice(DH * (n % 2), DH * (n % 2) + DH)
                j = n // 2
                t = slice(hf * HALF, (hf + 1) * HALF)
                dve.wait_ge(act_done, at("sec_tmp", x))
                dve.wait_ge(dve_done, now(dve_done))
                dve.tensor_tensor(d_o[main, hf, :], PS[main, 6 + hf, :], d_o[main, hf, :], ALU.add).then_inc(dve_done, 1)
                step(dve_done, "sec_o", x)
                if n % 2:
                    dve.wait_ge(dve_done, now(dve_done))
                    dve.tensor_copy(opA[:, 0, j, t], d_o[:, hf, :]).then_inc(dve_done, 1)
                    step(dve_done)
                    dve.wait_ge(dve_done, now(dve_done))
                    dve.tensor_tensor(opA[:, 1, j, t], d_o[:, hf, :], opA[:, 0, j, t].bitcast(F32),
                                      ALU.subtract).then_inc(dve_done, 1)
                    step(dve_done, "swa_out", j, hf)

            for kind, n in SECOND:
                if kind == "probs" and n < SWA_STEPS:
                    swa_probs(n)
                elif kind == "probs":
                    diff_probs(n)
                elif kind == "norm":
                    norm(n)
                elif kind == "turn":
                    w = piece_width(n)
                    dve.wait_ge(act_done, at("sec_hi", n))
                    dve.tensor_tensor(aT[:, n % 2, 1, 0:w], PS[:, 4 + n % 2, 0:w],
                                      aT[:, n % 2, 0, 0:w].bitcast(F32), ALU.subtract).then_inc(dve_done, 1)
                    step(dve_done, "sec_lo", n)
                elif kind == "out":
                    out(n)
                elif kind == "rms":
                    dve.wait_ge(pe_done, at("sec_ss", n))
                    dve.tensor_copy(d_o[:, 0, :], PS[:, 4 + PLACE[None, n] % 2, :]).then_inc(dve_done, 1)
                    step(dve_done, "sec_lo", PLACE[None, n])
                elif kind == "scaled":
                    dve.wait_ge(act_done, at("sec_rr", n))
                    dve.wait_ge(dve_done, now(dve_done))
                    dve.scalar_tensor_tensor(out=d_o[:, 1, :], in0=PS[:, 6 + n % 2, :],
                                             scalar=small[:, SUBG:SUBG + 1], in1=d_o[:, 0, :], op0=ALU.mult,
                                             op1=ALU.mult).then_inc(dve_done, 1)
                    step(dve_done, "sec_o", SWA_STEPS + n)
                elif kind == "parts":
                    j, hf = divmod(n, 2)
                    t = slice(hf * HALF, (hf + 1) * HALF)
                    dve.wait_ge(act_done, at("sec_ohi", n))
                    dve.wait_ge(dve_done, now(dve_done))
                    dve.tensor_tensor(opA[:, 1, 4 + j, t], d_o[:, 1, :], opA[:, 0, 4 + j, t].bitcast(F32),
                                      ALU.subtract).then_inc(dve_done, 1)
                    step(dve_done, "sec_out", n)
            names[("att_end", 1)] = names[("att_end2", 1)] = now(dve_done)

        @block.sync
        def _(sp):
            def vectors(t, rs):
                r = 0
                for n, many in rs:
                    v = a[n]
                    dims = " ".join(f"d{i}" for i in range(len(v.shape)))
                    v = v.rearrange(f"{dims} -> ({dims})").rearrange("(r p) -> r p", p=P)
                    sp.dma_start(vec_rows[r:r + many, t, :], v).then_inc(vec_in[min(t, 1)], 16)
                    step(vec_in[min(t, 1)], "vec_in", min(t, 1), by=16)
                    r += many

            def first_mod(g, ks):
                name, part, _ = MODS[g]
                for kc in ks:
                    sp.dma_start(first_mods[g][:, kc, :], a[name][0, kc * P:(kc + 1) * P, part * D:(part + 1) * D]).then_inc(first_mod_in[g][kc], 16)
                    step(first_mod_in[g][kc], "first_mod_in", g, kc, by=16)

            vectors(0, ROWS0)
            first_mod(0, range(2))
            for tb in range(NT):
                sp.dma_start(x_rows[:, tb, :], a["x"][0, tb * P:(tb + 1) * P, :]).then_inc(x_in[tb], 16)
                step(x_in[tb], "x_in", tb, by=16)
            first_mod(0, range(2, KC))
            sp.wait_ge(dve_done, at("vec_zero"))
            vectors(1, ROWS1)
            vectors(2, ROWS2)
            sp.dma_start(small[:, SINK:SINK + 8], a["swa_sinks_2"].to_broadcast([P, 8])).then_inc(vec_in[1], 16)
            step(vec_in[1], "vec_in", 1, by=16)
            sp.dma_start(lam_rows[:, 0:256], a["diff_lambda_2"].rearrange("o f d -> o (f d)").to_broadcast([P, 256])).then_inc(vec_in[1], 16)
            step(vec_in[1], "vec_in", 1, by=16)

            def mod_loads(pieces):
                for n in pieces:
                    name, part, _ = MODS[n // MOD_PIECES]
                    kc, h = divmod(n % MOD_PIECES, 2)
                    w = a[name]
                    if len(w.shape) == 3:
                        w = w[0]
                    if n >= FIRST_MODS * MOD_PIECES + 2:
                        sp.wait_ge(dve_done, at("mod_step", n - 2))
                    sp.dma_start(mod_raw[:, n % 2, :],
                                 w[kc * P:(kc + 1) * P, part * D + h * HALF:part * D + (h + 1) * HALF]).then_inc(mod_in[n % 2], 16)
                    step(mod_in[n % 2], "mod_in", n, by=16)

            def weights(u):
                if not (u < 2):
                    sp.wait_ge(pool_done, at("split", u - 2))
                for n, (w, col0, row0, chunks, k0) in enumerate(source(u)):
                    src = w[row0:row0 + chunks * P, col0:col0 + P].rearrange("(k p) n -> p k n", p=P)
                    sp.dma_start(w_raw[:, u % 2, k0:k0 + chunks, :], src).then_inc(w_in[u % 2], 16)
                    step(w_in[u % 2], "w_in", u, by=16)

            def spill(n):
                sp.wait_ge(dve_done, at("x_free", n))
                sp.dma_start(x_dram, X[:].rearrange("p k t -> p (k t)")).then_inc(x_out, 16)
                step(x_out, "x_out", n, by=16)

            def reload(n):
                sp.wait_ge(x_out, at("x_out", n))
                sp.wait_ge(dve_done, at("att_end", n))
                sp.wait_ge(dve_done, at("att_end2", n))
                for j in range(KC):
                    sp.dma_start(X[:, j, :], x_dram[:, j * T:(j + 1) * T]).then_inc(x_back[j], 16)
                    step(x_back[j], "x_back", n, j, by=16)

            def head_loads(h):
                s = h % 2
                if h >= 2:
                    sp.wait_ge(pe_done, at("stick_free", h - 2))
                for u in (U_KV + KC - 1, U_KV + KC - 2, U_QZ + KC - 1, U_QZ + KC - 2):
                    sp.wait_ge(stored[u % 2], at("stored", u))
                for u in (U_KV + 2 * KC - 1, U_KV + 2 * KC - 2):
                    sp.wait_ge(v_stored[u % 2], at("v_stored", u))
                rows = slice(h * DH, (h + 1) * DH)
                key = f"head_in{s}"
                hi_at = slice(DH * (h % 2), DH * (h % 2) + DH)
                lo_at = slice(DH * (1 - h % 2), DH * (1 - h % 2) + DH)
                sp.dma_start(hin[hi_at, s, 0, :].bitcast(F32), k_dram[0, rows, :]).then_inc(head_in[h % 2], 16)
                step(head_in[h % 2], "head_in", h, by=16)
                sp.dma_start(hin[lo_at, s, 0, :].bitcast(F32), k_dram[1, rows, :]).then_inc(head_in[h % 2], 16)
                step(head_in[h % 2], "head_in", h, by=16)
                for part in range(2):
                    for place in (hi_at, lo_at):
                        sp.dma_start(hin[place, s, 1 + part, :].bitcast(F32), q_dram[part, rows, :]).then_inc(head_in[h % 2], 16)
                        step(head_in[h % 2], "head_in", h, by=16)
                sp.dma_start(hin[:, s, 3, :].bitcast(F32), v_dram[h // 2, :, h % 2, :]).then_inc(head_in[h % 2], 16)
                step(head_in[h % 2], "head_in", h, by=16)

            weights(0)
            first_mod(1, range(KC))
            weights(1)
            for u in range(2, len(UNITS)):
                if u == U_QZ + 4:
                    spill(0)
                if u == U_BOUT + 2:
                    head_loads(0)
                    head_loads(1)
                if u == U_BOUT + 3:
                    for h in range(2, HEADS):
                        head_loads(h)
                    reload(0)
                if u == U_IN2 + 20:
                    spill(1)
                if u == U_BRANCH:
                    second_loads(sp)
                if U_BRANCH <= u <= U_BRANCH + 1:
                    sp.wait_ge(pe_done, at("sec_T", last_piece(STEPS - 3)))
                if u == U_BRANCH + 3:
                    reload(1)
                weights(u)
                if u - 2 < MOD_UNITS:
                    n = FIRST_MODS * MOD_PIECES + (u - 2) * MOD_STEPS
                    mod_loads(range(n, n + MOD_STEPS))

            for tb in range(NT):
                sp.wait_ge(act_done, at("row_out", tb))
                sp.dma_start(out[0, tb * P:(tb + 1) * P, :], M[ROW_PLACES[tb % 4]][:]).then_inc(row_gone[tb % 4], 16)
                step(row_gone[tb % 4], "row_gone", tb, by=16)
            for tb in range(NT - 4, NT):
                sp.wait_ge(row_gone[tb % 4], at("row_gone", tb))

        @block.gpsimd
        def _(pool):
            pool.wait_ge(pool_done, now(pool_done))
            pool.memset(ident[:], 0.0).then_inc(pool_done, 1)
            step(pool_done)
            pool.wait_ge(pool_done, now(pool_done))
            pool.affine_select(out=ident[:], in_=ident[:], compare_op=ALU.not_equal, fill=1.0, base=0,
                               pattern=[[-1, P]], channel_multiplier=1).then_inc(pool_done, 1)
            step(pool_done)
            pool.wait_ge(pool_done, now(pool_done))
            pool.memset(ones[:], 1.0).then_inc(pool_done, 1)
            step(pool_done)
            pool.wait_ge(pool_done, now(pool_done))
            pool.memset(small[:, EPS_COL:EPS_COL + 1], EPS).then_inc(pool_done, 1)
            step(pool_done, "consts")

            def split(u):
                s = u % 2
                chunks = UNITS[u][3]
                raw, hi, lo = w_raw[:, s, 0:chunks], w_hi[:, s, 0:chunks], w_lo[:, s, 0:chunks]
                if u == U_BRANCH + 1:
                    pool.wait_ge(pe_done, at("sec_pv", len(PIECES) - 2))
                if u not in AFTER_PAIR:
                    pool.wait_ge(w_in[u % 2], at("w_in", u))
                    if u >= 2:
                        pool.wait_ge(pe_done, at("unit", u - 2, 1))
                    pool.wait_ge(pool_done, now(pool_done))
                    pool.tensor_copy(hi, raw).then_inc(pool_done, 1)
                    step(pool_done)
                if u in AFTER_PAIR:
                    pool.wait_ge(act_done, at("tile_hi", u))
                pool.wait_ge(pool_done, now(pool_done))
                pool.tensor_tensor(lo, raw, hi.bitcast(F32), ALU.subtract).then_inc(pool_done, 1)
                step(pool_done, "split", u)

            def stick_consts():
                pool.wait_ge(x_out, at("x_out", 0))
                pool.wait_ge(pool_done, now(pool_done))
                pool.memset(tri[:], -1.0).then_inc(pool_done, 1)
                step(pool_done)
                pool.wait_ge(pool_done, now(pool_done))
                pool.affine_select(out=tri[:], in_=tri[:], compare_op=ALU.is_ge, fill=0.0, base=0,
                                   pattern=[[-1, P]], channel_multiplier=1).then_inc(pool_done, 1)
                step(pool_done)
                pool.wait_ge(pool_done, now(pool_done))
                pool.memset(nones[:], -1.0).then_inc(pool_done, 1)
                step(pool_done)
                pool.wait_ge(pool_done, now(pool_done))
                pool.memset(masks[:], 0.0).then_inc(pool_done, 1)
                step(pool_done)
                pool.wait_ge(pool_done, now(pool_done))
                pool.affine_select(out=masks[:], in_=masks[:], compare_op=ALU.is_gt, fill=MASKED, base=0,
                                   pattern=[[1, P]], channel_multiplier=-1).then_inc(pool_done, 1)
                step(pool_done)
                pool.wait_ge(pool_done, now(pool_done))
                pool.tensor_copy(mask_r[:], masks[:]).then_inc(pool_done, 1)
                step(pool_done)
                pool.wait_ge(pool_done, now(pool_done))
                pool.tensor_copy(ident_r[:], ident[:]).then_inc(pool_done, 1)
                step(pool_done, "stick_consts")

            def stick_pool():
                for g in range(HEADS * len(STICK)):
                    h, i, hf, kb, qs = cut(g)
                    if kb > 0:
                        q0 = qs + P if kb >= NQ * hf else qs
                        pool.wait_ge(dve_done, at("stick_sp", g))
                        if g >= 2:
                            pool.wait_ge(pe_done, at("stick_b", g - 2))
                        if q0 > qs:
                            pool.wait_ge(pool_done, now(pool_done))
                            pool.tensor_copy(s_p[:, g % 3, qs:q0], s_sp[:, g % 3, qs:q0]).then_inc(pool_done, 1)
                            step(pool_done, "stick_p", g)
                        if q0 < HALF:
                            pool.wait_ge(pool_done, at("stick_p", g - 1))
                            pool.tensor_tensor(s_p[:, g % 3, q0:], s_p[:, (g - 1) % 3, q0:],
                                               s_sp[:, g % 3, q0:], ALU.add).then_inc(pool_done, 1)
                            step(pool_done, "stick_p", g)

            def second_pool():
                far = -MASKED * 512
                for hf in range(2):
                    w = bias[:, hf, :].rearrange("p (b k) -> p b k", b=NQ)
                    pool.wait_ge(x_out, at("x_out", 1))
                    pool.wait_ge(pool_done, now(pool_done))
                    pool.iota(w, pattern=[[0, NQ], [-1, 2 * P]], base=P, channel_multiplier=1,
                              allow_small_or_imprecise_dtypes=True).then_inc(pool_done, 1)
                    step(pool_done)
                    pool.wait_ge(pool_done, now(pool_done))
                    pool.affine_select(out=w, in_=w, compare_op=ALU.is_ge, fill=far, base=P,
                                       pattern=[[0, NQ], [-1, 2 * P]], channel_multiplier=1).then_inc(pool_done, 1)
                    step(pool_done)
                    pool.wait_ge(pool_done, now(pool_done))
                    pool.affine_select(out=w, in_=w, compare_op=ALU.is_gt, fill=far, base=0,
                                       pattern=[[0, NQ], [1, 2 * P]], channel_multiplier=-1).then_inc(pool_done, 1)
                    step(pool_done)
                pool.wait_ge(pool_done, now(pool_done))
                pool.memset(bias[:, 0, 0:P], far).then_inc(pool_done, 1)
                step(pool_done)

                def slope(n, hf):
                    if n:
                        pool.wait_ge(dve_done, at("sec_p", 2 * n - 2 + hf, 0))
                    pool.wait_ge(pool_done, now(pool_done))
                    pool.tensor_scalar(bias[:, hf, :], bias[:, hf, :], 0.5, None, ALU.mult).then_inc(pool_done, 1)
                    step(pool_done, "bias_s", n, hf)

                slope(0, 0)
                slope(0, 1)
                for kind, x in SECOND:
                    if kind == "norm" and x < SWA_STEPS:
                        if x < SWA_STEPS - 2:
                            slope(x // 2 + 1, x % 2)
                        if x == SWA_STEPS - 2:
                            row = bias[:, 0, :]
                            pool.wait_ge(dve_done, at("sec_p", x, 0))
                            pool.wait_ge(pool_done, now(pool_done))
                            pool.iota(row, pattern=[[-1, T]], base=T - P, channel_multiplier=1,
                                      allow_small_or_imprecise_dtypes=True).then_inc(pool_done, 1)
                            step(pool_done)
                            pool.wait_ge(pool_done, now(pool_done))
                            pool.affine_select(out=row, in_=row, compare_op=ALU.is_ge, fill=far,
                                               base=T - P, pattern=[[-1, T]], channel_multiplier=1).then_inc(pool_done, 1)
                            step(pool_done, "bias_d")
                    elif kind == "norm":
                        c = RI + x % 4 * 4
                        pool.wait_ge(dve_done, at("sec_r", x))
                        if x >= SWA_STEPS + 4:
                            pool.wait_ge(pe_done, at("sec_T", last_piece(x - 4)))
                        else:
                            pool.wait_ge(dve_done, at("sec_p", SWA_STEPS - 1, 0))
                        pool.tensor_scalar(diff_diag[:, x % 4, :], ident[:], small[:, c:c + 1], None, ALU.mult).then_inc(pool_done, 1)
                        step(pool_done, "sec_gd", x)
                pool.wait_ge(pe_done, at("sec_T", last_piece(STEPS - 2)))

            for u in range(len(UNITS)):
                if u == U_BOUT:
                    stick_consts()
                if u == U_BOUT + 1:
                    stick_pool()
                if u == U_BRANCH:
                    second_pool()
                split(u)

        @block.tensor
        def _(pe):
            def product(ps, hi_w, lo_w, rhs, chunks, k0, name, ready=None, hf=0):
                for k in range(chunks):
                    if ready is not None:
                        pe.wait_ge(dve_done, at("h_" + ready, k, hf))
                    for n, (w, part) in enumerate(((hi_w, 0), (lo_w, 0), (hi_w, 1))):
                        ins = pe.matmul(ps, w[:, k0 + k, :], rhs(part, k0 + k), start=(k == 0 and n == 0),
                                        stop=(k == chunks - 1 and n == 2))
                ins.then_inc(pe_done, 1)
                step(pe_done, *(name or ()))

            def unit(u, op_in, ready=None, turned=None):
                s = u % 2
                pe.wait_ge(pool_done, at("split", u))
                if u >= 2:
                    pe.wait_ge(reader(u - 2), at("free", u - 2))
                for hf in range(2):
                    rhs = lambda part, k: op_in[:, part, k, hf * HALF:(hf + 1) * HALF]
                    product(PS[:, 2 * s + hf, :], w_hi[:, s], w_lo[:, s], rhs, UNITS[u][3], 0, ("unit", u, hf), ready, hf)
                    if turned is not None and hf == 0:
                        turn_v(pe, turned)

            def pair(u, op_in, ready, turned=None):
                pe.wait_ge(pool_done, at("split", u))
                pe.wait_ge(pool_done, at("split", u + 1))
                if u >= 2:
                    pe.wait_ge(reader(u - 2), at("free", u - 2))
                if u >= 2:
                    pe.wait_ge(reader(u - 1), at("free", u - 1))
                for hf in range(2):
                    for k in range(KC):
                        pe.wait_ge(dve_done, at("h_" + ready, k, hf))
                        for s in (u % 2, 1 - u % 2):
                            for n, (w, part) in enumerate(((w_hi, 0), (w_lo, 0), (w_hi, 1))):
                                ins = pe.matmul(PS[:, 2 * s + hf, :], w[:, s, k, :],
                                                op_in[:, part, k, hf * HALF:(hf + 1) * HALF],
                                                start=(k == 0 and n == 0), stop=(k == KC - 1 and n == 2))
                            if k == KC - 1:
                                ins.then_inc(pe_done, 1)
                                step(pe_done, "unit", u + (s != u % 2), hf)
                    if turned is not None and hf == 0:
                        turn_v(pe, turned)

            def norm_sum(n, hf):
                pe.wait_ge(dve_done, at("sq_add", n, KC - 1, hf))
                pe.wait_ge(pool_done, at("consts"))
                if n in MISC_FREE:
                    pe.wait_ge(act_done, at("rstd", MISC_FREE[n], 1))
                bank, squares = (6, M[3]) if n == "n1" else (4, M[1])
                pe.matmul(PS[:, bank + hf, :], ones[:], squares[:, hf * HALF:(hf + 1) * HALF], start=True, stop=True).then_inc(pe_done, 1)
                step(pe_done, "norm_sum", n, hf)

            def mod_sum(g):
                if g < FIRST_MODS:
                    pe.wait_ge(dve_done, at("first_step", g, KC - 1))
                else:
                    pe.wait_ge(dve_done, at("mod_step", (g + 1) * MOD_PIECES - 1))
                if g:
                    pe.wait_ge(dve_done, at("mod_out", g - 1))
                for j in range(KC):
                    ins = pe.matmul(PS[:, 6, j:j + 1], mod_acc[:, j * P:(j + 1) * P], ones[:, 0:1], start=True, stop=True)
                ins.then_inc(pe_done, 1)
                step(pe_done, "mod_sum", g)

            pe.wait_ge(pool_done, at("consts"))
            pe.wait_ge(vec_in[0], at("vec_in", 0))
            pe.transpose(PS[:, 7, 0:P], vec_rows[:, 0, :], ident[:]).then_inc(pe_done, 1)
            step(pe_done, "vec_T")
            for j in range(KC):
                for hf in range(2):
                    n = 2 * j + hf
                    if n >= 4:
                        pe.wait_ge(act_done, at("x_set", n - 4))
                    for b in range(4):
                        pe.wait_ge(x_in[(4 * hf + b)], at("x_in", 4 * hf + b))
                    for b in range(4):
                        ins = pe.transpose(PS[:, n % 4, b * P:(b + 1) * P],
                                           x_rows[:, 4 * hf + b, j * P:(j + 1) * P], ident[:])
                    ins.then_inc(pe_done, 1)
                    step(pe_done, "x_T", n)
            norm_sum("a", 0)
            norm_sum("a", 1)
            mod_sum(0)
            pe.wait_ge(vec_in[1], at("vec_in", 1))
            pe.wait_ge(dve_done, at("cols"))
            for t in (1, 2):
                ins = pe.transpose(PS[:, 7, t * P:(t + 1) * P], vec_rows[:, t, :], ident[:])
            ins.then_inc(pe_done, 1)
            step(pe_done, "vec_T2")
            mod_sum(1)
            pe.wait_ge(act_done, at("x_set", 15))
            for j in range(KC):
                if j == 0:
                    pair(U_AIN, opA, "a")
                for q in range(0 if j else 2, 4):
                    unit(U_AIN + 4 * j + q, opA)
                    if q == 0:
                        mod_sum(FIRST_MODS + j - 1)
            for n in range(KC):
                unit(U_AOUT + n, opB, None if n else "y")
                if n % 4 == 0:
                    mod_sum(FIRST_MODS + KC - 1 + n // 4)
            norm_sum("kv", 0)
            norm_sum("kv", 1)
            mod_sum(FIRST_MODS + KC + 1)
            pair(U_KV, opA, "kv")
            for n in range(2, 2 * KC):
                unit(U_KV + n, opA, turned=U_KV + n - 1 if n > KC else None)
                if n in (4, 8):
                    mod_sum(FIRST_MODS + KC + 1 + n // 4)
            pair(U_QZ, opA, "b", turned=U_KV + 2 * KC - 1)
            for n in range(2, 2 * KC):
                unit(U_QZ + n, opA)
            stick_pe(pe)
            for n in range(KC):
                unit(U_BOUT + n, opA, None if n else "att")
            for hf in range(2):
                norm_sum("fin1", hf)
                norm_sum("n1", hf)
            pair(U_IN2, opA, "n1")
            for n in range(2, 34):
                unit(U_IN2 + n, opA, turned=U_IN2 + n - 1 if 13 < n <= 18 else None)
            second_pe(pe)
            for n in range(KC):
                u = U_BRANCH + n
                s = u % 2
                pe.wait_ge(pool_done, at("split", u))
                if u >= 2:
                    pe.wait_ge(reader(u - 2), at("free", u - 2))
                pe.wait_ge(dve_done, at("sec_out", 2 * DIFF_HEADS - 1))
                for hf in range(2):
                    rhs = lambda part, k: opA[:, part, k, hf * HALF:(hf + 1) * HALF]
                    product(PS[:, 2 * s + hf, :], w_hi[:, s], w_lo[:, s], rhs, 4, 0, ("unit_a", u, hf))
                    product(PS[:, 4 + 2 * s + hf, :], w_hi[:, s], w_lo[:, s], rhs, 4, 4, ("unit", u, hf))
            for n in range(KC):
                unit(U_OUT2 + n, opB, None if n else "merged")
            norm_sum("n2", 0)
            norm_sum("n2", 1)
            u = U_FFN
            for first, many in FGROUPS:
                if u == U_FFN:
                    pair(u, opA, "n2")
                    u += 2
                for f in range(2 if first == 0 else 0, 2 * many):
                    unit(u, opA)
                    u += 1
                for n in range(KC):
                    unit(u, opB, None if n else f"ff{first}")
                    u += 1
            norm_sum("fin2", 0)
            norm_sum("fin2", 1)
            for tb in range(NT):
                pe.wait_ge(dve_done, at("x_fin2", KC - 1, tb // NQ))
                if tb >= 2:
                    pe.wait_ge(act_done, at("row_out", tb - 2))
                pe.wait_ge(reader(len(UNITS) - 1), at("free", len(UNITS) - 1))
                pe.wait_ge(reader(len(UNITS) - 2), at("free", len(UNITS) - 2))
                for j in range(KC):
                    ins = pe.transpose(PS[:, 2 * (tb % 2) + j // 4, (j % 4) * P:(j % 4 + 1) * P],
                                       X[:, j, tb * P:(tb + 1) * P], ident[:])
                ins.then_inc(pe_done, 1)
                step(pe_done, "row_T", tb)

        @block.scalar
        def _(act):
            def act_norm(n, hf):
                t = slice(hf * HALF, (hf + 1) * HALF)
                if n == "n1":
                    act.wait_ge(dve_done, at("mean_n1", hf))
                    act.wait_ge(act_done, now(act_done))
                    act.activation(M[3][:, t], M[3][:, t], ACT.Ln, bias=small[:, EPS_COL:EPS_COL + 1],
                                   scale=1.0 / D).then_inc(act_done, 1)
                    step(act_done)
                    act.wait_ge(act_done, now(act_done))
                    act.activation(M[3][:, t], M[3][:, t], ACT.Exp, scale=-0.5).then_inc(act_done, 1)
                    step(act_done, "rstd2", hf)
                else:
                    act.wait_ge(pe_done, at("norm_sum", n, hf))
                    act.wait_ge(act_done, now(act_done))
                    act.activation(M[1][:, t], PS[:, 4 + hf, :], ACT.Ln, bias=small[:, EPS_COL:EPS_COL + 1],
                                   scale=1.0 / D).then_inc(act_done, 1)
                    step(act_done)
                    act.wait_ge(act_done, now(act_done))
                    act.activation(M[1][:, t], M[1][:, t], ACT.Exp, scale=-0.5).then_inc(act_done, 1)
                    step(act_done, "rstd", n, hf)

            def act_v(u, x):
                s = u % 2
                act.wait_ge(pe_done, at("unit", u, 1))
                if not (u in FIRST_V):
                    act.wait_ge(pe_done, at("v_T", u - 1))
                if u < U_IN2:
                    act.wait_ge(dve_done, at("mod_step", 14 * MOD_PIECES - 1))
                else:
                    act.wait_ge(dve_done, at("sq_add", "n1", KC - 1, 1))
                act.wait_ge(act_done, now(act_done))
                act.activation(vt[:], banks(2 * s), ACT.Copy).then_inc(act_done, 1)
                step(act_done, "vt", u)
                names[("free", u)] = names[("vt", u)]

            def act_v_hi(u, x, kind):
                s = u % 2
                src = PS[:, 4:6, :].rearrange("p b (k e d) -> p (b k) e d", k=4, e=2)
                if kind == "stick" or kind == "swa":
                    for e in range(2):
                        place = 0 if kind == "swa" else e
                        dst = vstage[:, s, e, :].rearrange("p (k s d) -> p k s d", k=NT, s=2)[:, :, place, :]
                        act.wait_ge(pe_done, at("v_T", u))
                        if x >= 2:
                            act.wait_ge(v_stored[(u - 2) % 2], at("v_stored", u - 2))
                        act.wait_ge(act_done, now(act_done))
                        act.activation(dst, src[:, :, e, :], ACT.Copy).then_inc(act_done, 1)
                        step(act_done, "v_hi", u)
                else:
                    act.wait_ge(pe_done, at("v_T", u))
                    if x >= 2:
                        act.wait_ge(v_stored[(u - 2) % 2], at("v_stored", u - 2))
                    act.wait_ge(act_done, now(act_done))
                    act.activation(vstage[:, s, 0, :], banks(4), ACT.Copy).then_inc(act_done, 1)
                    step(act_done, "v_hi", u)

            def store_v(u, x, dst):
                act.wait_ge(dve_done, at("v_split", u))
                act.dma_start(dst, vstage[:, u % 2, :, :].bitcast(F32)).then_inc(v_stored[u % 2], 16)
                step(v_stored[u % 2], "v_stored", u, by=16)

            def act_parts(n, shift):
                for hf in range(2):
                    for j in range(KC):
                        x = hf * KC + j
                        s = x % 2
                        if x == 4 and n != "b":
                            if n == "n1":
                                act_norm("fin1", 1)
                            act_norm(n, 1)
                        if x == 3 and n == "b":
                            act_v(U_QZ - 1, KC - 1)
                        if x == 11 and n == "b":
                            act_v_hi(U_QZ - 1, KC - 1, "stick")
                        if x == 12 and n == "b":
                            store_v(U_QZ - 1, KC - 1, v_dram[KC - 1])
                        act.wait_ge(dve_done, at("xn", n, x))
                        act.wait_ge(act_done, now(act_done))
                        act.activation(hn[:, s, :], xn[:, s, :], ACT.Identity, bias=mod[:, shift, j:j + 1],
                                       scale=small[:, GS + j:GS + j + 1]).then_inc(act_done, 1)
                        step(act_done, "hn", n, x)
                        act.wait_ge(act_done, now(act_done))
                        act.activation(opA[:, 0, j, hf * HALF:(hf + 1) * HALF], hn[:, s, :], ACT.Copy).then_inc(act_done, 1)
                        step(act_done, "hi", n, x)
                u = {m: v for v, m in AFTER_PAIR.items()}[n]
                act.wait_ge(w_in[u % 2], at("w_in", u))
                act.wait_ge(pe_done, at("unit", u - 2, 1))
                act.wait_ge(act_done, now(act_done))
                act.activation(w_hi[:, u % 2], w_raw[:, u % 2], ACT.Copy).then_inc(act_done, 1)
                step(act_done, "tile_hi", u)

            def square(n, j, hf):
                slot = M[0] if j % 2 == 0 else M[2]
                t = slice(hf * HALF, (hf + 1) * HALF)
                if n != "a":
                    act.wait_ge(dve_done, at("x_new", n, j, hf))
                if j >= 2:
                    act.wait_ge(dve_done, at("sq_add", n, j - 2, hf))
                act.wait_ge(act_done, now(act_done))
                act.activation(slot[:, t], X[:, j, t], ACT.Square).then_inc(act_done, 1)
                step(act_done, "sq", n, j, hf)
                if n == "fin1":
                    c = C["final_norm_g"] + j
                    if j:
                        act.wait_ge(dve_done, at("sq_add", "n1", j - 1, hf))
                    act.wait_ge(act_done, now(act_done))
                    act.activation(M[4][:, t], X[:, j, t], ACT.Square, scale=cols[:, c:c + 1]).then_inc(act_done, 1)
                    step(act_done, "sq", "n1", j, hf)

            act.wait_ge(dve_done, at("cols"))
            act.wait_ge(act_done, now(act_done))
            act.activation(small[:, SILU_C:SILU_C + 16], cols[:, 0:16], ACT.Silu).then_inc(act_done, 1)
            step(act_done, "silu_c")
            for j in range(KC):
                for hf in range(2):
                    n = 2 * j + hf
                    act.wait_ge(pe_done, at("x_T", n))
                    act.wait_ge(act_done, now(act_done))
                    act.activation(X[:, j, hf * HALF:(hf + 1) * HALF], PS[:, n % 4, :], ACT.Copy).then_inc(act_done, 1)
                    step(act_done, "x_set", n)
                    square("a", j, hf)
            act.preload_act_table_set("natural_log_exp_and_others")
            act_norm("a", 0)
            act_parts("a", A_SHIFT)
            act.wait_ge(dve_done, at("lam_sum"))
            act.wait_ge(act_done, now(act_done))
            act.activation(small[:, LAM + 2:LAM + 4], small[:, LAM:LAM + 2], ACT.Exp).then_inc(act_done, 1)
            step(act_done, "lam_exp")
            for j in range(KC):
                u = U_AIN + 4 * j
                for hf in range(2):
                    act.wait_ge(pe_done, at("unit", u, 1))
                    if j:
                        act.wait_ge(dve_done, at("yz", j - 1, hf))
                    act.wait_ge(act_done, at("hi", "a", 15))
                    act.wait_ge(dve_done, at("lo", "a", 15))
                    act.wait_ge(act_done, now(act_done))
                    act.activation(cs[:, hf, :], PS[:, 2 * (u % 2) + hf, :], ACT.Copy).then_inc(act_done, 1)
                    step(act_done, "cs", j, hf)
                names[("free", u)] = names[("cs", j, 1)]
                for hf in range(2):
                    act.wait_ge(pe_done, at("unit", u + 3, 1))
                    act.wait_ge(dve_done, at("cu", j, hf))
                    act.wait_ge(act_done, now(act_done))
                    act.activation(cs[:, hf, :], PS[:, 2 * ((u + 3) % 2) + hf, :], ACT.Silu).then_inc(act_done, 1)
                    step(act_done, "sz", j, hf)
                names[("free", u + 3)] = names[("sz", j, 1)]
                for hf in range(2):
                    act.wait_ge(dve_done, at("yz", j, hf))
                    act.wait_ge(act_done, now(act_done))
                    act.activation(opB[:, 0, j, hf * HALF:(hf + 1) * HALF], yt[:, hf, :], ACT.Copy).then_inc(act_done, 1)
                    step(act_done, "yh", j, hf)
            for n in range(KC):
                square("kv", n, 0)
                square("kv", n, 1)
            act.preload_act_table_set("natural_log_exp_and_others")
            act_norm("kv", 0)
            act_parts("kv", KV_SHIFT)

            def act_hl(u, x, scale, dram, row0, name):
                s = u % 2
                act.wait_ge(pe_done, at("unit", u, 1))
                if x >= 2:
                    act.wait_ge(stored[(u - 2) % 2], at("stored", u - 2))
                else:
                    if U_QZ <= u < U_BOUT:
                        act.wait_ge(stored[(U_KV + KC - 2 + x) % 2], at("stored", U_KV + KC - 2 + x))
                act.wait_ge(act_done, now(act_done))
                act.activation(stage[:, x % 2, 0, :], banks(2 * s), ACT.Copy, scale=scale).then_inc(act_done, 1)
                step(act_done, "hl_hi", u)

            def store_hl(u, x, dram, row0):
                act.wait_ge(dve_done, at("hl_lo", u))
                act.wait_ge(act_done, at("hl_hi", u))
                act.dma_start(dram[:, row0:row0 + P, :].rearrange("c p t -> p c t"), stage[:, x % 2, :, :].bitcast(F32)).then_inc(stored[u % 2], 16)
                step(stored[u % 2], "stored", u, by=16)

            for n in range(KC):
                act_hl(U_KV + n, n, 1.0, k_dram, n * P, "k")
                if n:
                    store_hl(U_KV + n - 1, n - 1, k_dram, (n - 1) * P)
            store_hl(U_KV + KC - 1, KC - 1, k_dram, (KC - 1) * P)
            for n in range(KC - 1):
                act_v(U_KV + KC + n, n)
                act_v_hi(U_KV + KC + n, n, "stick")
                store_v(U_KV + KC + n, n, v_dram[n])
            act_parts("b", B_SHIFT)
            for n in range(KC):
                act_hl(U_QZ + n, n, QSCALE, q_dram, n * P, "q")
                if n:
                    store_hl(U_QZ + n - 1, n - 1, q_dram, (n - 1) * P)
            store_hl(U_QZ + KC - 1, KC - 1, q_dram, (KC - 1) * P)
            for n in range(KC):
                u = U_QZ + KC + n
                s = u % 2
                act.wait_ge(pe_done, at("unit", u, 1))
                act.wait_ge(act_done, now(act_done))
                act.activation(sz[:, n, :], banks(2 * s), ACT.Silu).then_inc(act_done, 1)
                step(act_done, "free", u)
            stick_act(act)
            for n in range(KC):
                square("fin1", n, 0)
                square("fin1", n, 1)
            act.preload_act_table_set("natural_log_exp_and_others")
            act_norm("fin1", 0)
            act_norm("n1", 0)
            act_parts("n1", SHIFT1)
            dst = [(q2_dram, n * P) for n in range(8)] + [(k2_dram, n * P) for n in range(5)]
            for n in range(13):
                act_hl(U_IN2 + n, n, -QSCALE if n < 8 else 1.0, None, None, None)
                if n:
                    store_hl(U_IN2 + n - 1, n - 1, *dst[n - 1])
            store_hl(U_IN2 + 12, 12, *dst[12])
            for n in range(5):
                u = U_IN2 + 13 + n
                act_v(u, n)
                act_v_hi(u, n, "diff" if n else "swa")
                store_v(u, n, va_dram if n == 0 else vd_dram[n - 1])
            for n in range(16):
                u = U_IN2 + 18 + n
                s = u % 2
                act.wait_ge(pe_done, at("unit", u, 1))
                act.wait_ge(stored[(U_IN2 + 12) % 2], at("stored", U_IN2 + 12))
                act.wait_ge(stored[(U_IN2 + 11) % 2], at("stored", U_IN2 + 11))
                act.wait_ge(v_stored[(U_IN2 + 17) % 2], at("v_stored", U_IN2 + 17))
                act.wait_ge(v_stored[(U_IN2 + 16) % 2], at("v_stored", U_IN2 + 16))
                act.wait_ge(act_done, now(act_done))
                act.activation(gates[:, n, :], banks(2 * s), ACT.Sigmoid).then_inc(act_done, 1)
                step(act_done, "free", u)
            second_act(act)
            for n in range(KC):
                for hf in range(2):
                    act.wait_ge(dve_done, at("mz", n, hf))
                    act.wait_ge(act_done, now(act_done))
                    act.activation(opB[:, 0, n, hf * HALF:(hf + 1) * HALF], d_o[:, hf, :], ACT.Copy).then_inc(act_done, 1)
                    step(act_done, "mh", n, hf)
            for n in range(KC):
                square("n2", n, 0)
                square("n2", n, 1)
            act.preload_act_table_set("natural_log_exp_and_others")
            act_norm("n2", 0)
            act_parts("n2", SHIFT2)
            u = U_FFN
            for first, many in FGROUPS:
                for f in range(first, first + many):
                    for hf in range(2):
                        act.wait_ge(pe_done, at("unit", u, 1))
                        if f:
                            act.wait_ge(dve_done, at("fconv", f - 1, 1))
                        else:
                            act.wait_ge(dve_done, at("lo", "n2", 15))
                        act.wait_ge(act_done, now(act_done))
                        act.activation(M[0][:, hf * HALF:(hf + 1) * HALF], PS[:, 2 * (u % 2) + hf, :],
                                       ACT.Copy).then_inc(act_done, 1)
                        step(act_done, "fa", f, hf)
                    names[("free", u)] = names[("fa", f, 1)]
                    for hf in range(2):
                        act.wait_ge(dve_done, at("fconv", f, hf))
                        act.wait_ge(act_done, now(act_done))
                        act.activation(yt[:, hf, :], yt[:, hf, :], ACT.Gelu).then_inc(act_done, 1)
                        step(act_done, "fg", f, hf)
                    for hf in range(2):
                        act.wait_ge(dve_done, at("fz", f, hf))
                        if first:
                            act.wait_ge(pe_done, at("unit", U_FFN + 2 * first + KC * FGROUPS.index((first, many)) - 1, 1))
                        act.wait_ge(act_done, now(act_done))
                        act.activation(opB[:, 0, f - first, hf * HALF:(hf + 1) * HALF], yt[:, hf, :],
                                       ACT.Copy).then_inc(act_done, 1)
                        step(act_done, "fh", f, hf)
                    u += 2
                u += KC
            for n in range(KC):
                square("fin2", n, 0)
                square("fin2", n, 1)
            act.preload_act_table_set("natural_log_exp_and_others")
            act_norm("fin2", 0)
            act_norm("fin2", 1)
            for tb in range(NT):
                act.wait_ge(pe_done, at("row_T", tb))
                if tb >= 4:
                    act.wait_ge(row_gone[(tb - 4) % 4], at("row_gone", tb - 4))
                act.activation(M[ROW_PLACES[tb % 4]][:], banks(2 * (tb % 2)), ACT.Copy).then_inc(act_done, 1)
                step(act_done, "row_out", tb)

        @block.vector
        def _(dve):
            def mod_steps(pieces):
                for n in pieces:
                    g = n // MOD_PIECES
                    kc, h = divmod(n % MOD_PIECES, 2)
                    acc = mod_acc[:, h * HALF:(h + 1) * HALF]
                    src = SILU_C + 8 * MODS[g][2] + kc
                    c = small[:, src:src + 1]
                    dve.wait_ge(mod_in[n % 2], at("mod_in", n))
                    if n % MOD_PIECES == 0:
                        dve.wait_ge(pe_done, at("mod_sum", g - 1))
                    if kc == 0:
                        dve.wait_ge(dve_done, now(dve_done))
                        dve.tensor_scalar(acc, mod_raw[:, n % 2, :], c, None, ALU.mult).then_inc(dve_done, 1)
                        step(dve_done, "mod_step", n)
                    else:
                        dve.wait_ge(dve_done, now(dve_done))
                        dve.scalar_tensor_tensor(out=acc, in0=mod_raw[:, n % 2, :], scalar=c, in1=acc,
                                                 op0=ALU.mult, op1=ALU.add).then_inc(dve_done, 1)
                        step(dve_done, "mod_step", n)

            def mod_unit(u):
                if u >= 5 and u % 4 == 1 and u <= MOD_UNITS + 1:
                    mod_out(FIRST_MODS + u // 4 - 1)
                if u < MOD_UNITS:
                    n = FIRST_MODS * MOD_PIECES + u * MOD_STEPS
                    mod_steps(range(n, n + MOD_STEPS))

            def mod_out(g):
                name, part, _ = MODS[g]
                b = C[MOD_BIAS[name]] + part * KC
                dve.wait_ge(pe_done, at("mod_sum", g))
                dve.wait_ge(dve_done, now(dve_done))
                dve.tensor_tensor(mod[:, g, :], PS[:, 6, 0:KC], cols[:, b:b + KC], ALU.add).then_inc(dve_done, 1)
                step(dve_done, "mod_out", g)

            def gains(gname, scale):
                g = cols[:, C[gname]:C[gname] + KC]
                dve.wait_ge(dve_done, now(dve_done))
                dve.scalar_tensor_tensor(out=small[:, GS:GS + KC], in0=mod[:, scale, :], scalar=1.0, in1=g,
                                         op0=ALU.add, op1=ALU.mult).then_inc(dve_done, 1)
                step(dve_done)

            def sq_add(n, j, hf):
                t = slice(hf * HALF, (hf + 1) * HALF)
                slot = M[4] if n == "n1" else M[0] if j % 2 == 0 else M[2]
                total = M[3] if n == "n1" else M[1]
                if j == 0:
                    dve.wait_ge(act_done, at("sq", n, j, hf))
                    dve.wait_ge(dve_done, now(dve_done))
                    dve.tensor_copy(total[:, t], slot[:, t]).then_inc(dve_done, 1)
                    step(dve_done, "sq_add", n, j, hf)
                else:
                    dve.wait_ge(act_done, at("sq", n, j, hf))
                    dve.wait_ge(dve_done, now(dve_done))
                    dve.tensor_tensor(total[:, t], total[:, t], slot[:, t], ALU.add).then_inc(dve_done, 1)
                    step(dve_done, "sq_add", n, j, hf)

            def mean_n1(hf):
                t = slice(hf * HALF, (hf + 1) * HALF)
                dve.wait_ge(act_done, at("rstd", "fin1", hf))
                dve.wait_ge(pe_done, at("norm_sum", "n1", hf))
                dve.wait_ge(dve_done, now(dve_done))
                dve.tensor_tensor(M[3][:, t], M[1][:, t], M[1][:, t], ALU.mult).then_inc(dve_done, 1)
                step(dve_done)
                dve.wait_ge(dve_done, now(dve_done))
                dve.tensor_tensor(M[3][:, t], M[3][:, t], PS[:, 6 + hf, :], ALU.mult).then_inc(dve_done, 1)
                step(dve_done, "mean_n1", hf)

            def rstd_n1(hf):
                t = slice(hf * HALF, (hf + 1) * HALF)
                dve.wait_ge(act_done, at("rstd2", hf))
                dve.wait_ge(dve_done, now(dve_done))
                dve.tensor_tensor(M[3][:, t], M[3][:, t], M[1][:, t], ALU.mult).then_inc(dve_done, 1)
                step(dve_done)

            def parts(n, gname, scale, u_last):
                gains(gname, scale)
                if n == "n1":
                    c = C["final_norm_g"]
                    dve.wait_ge(dve_done, now(dve_done))
                    dve.tensor_tensor(small[:, GS:GS + KC], small[:, GS:GS + KC], cols[:, c:c + KC], ALU.mult).then_inc(dve_done, 1)
                    step(dve_done)
                    mean_n1(0)
                    rstd_n1(0)
                r = M[3] if n == "n1" else M[1]
                for x in range(2 * KC + 1):
                    if x < 2 * KC:
                        hf, j = divmod(x, KC)
                        t = slice(hf * HALF, (hf + 1) * HALF)
                        if x == 5 and n == "n1":
                            mean_n1(1)
                        if x == KC and n == "n1":
                            rstd_n1(1)
                        if x == 12 and n == "b":
                            v_lo(U_QZ - 1, KC - 1, "stick")
                        if not (n == "n1" or j):
                            dve.wait_ge(act_done, at("rstd", "kv" if n == "b" else n, hf))
                        if u_last is not None and j == 0:
                            dve.wait_ge(pe_done, at("unit", u_last, hf))
                        dve.wait_ge(dve_done, now(dve_done))
                        dve.tensor_tensor(xn[:, x % 2, :], X[:, j, t], r[:, t], ALU.mult).then_inc(dve_done, 1)
                        step(dve_done, "xn", n, x)
                    if x:
                        y = x - 1
                        hf, j = divmod(y, KC)
                        t = slice(hf * HALF, (hf + 1) * HALF)
                        dve.wait_ge(act_done, at("hi", n, y))
                        dve.wait_ge(dve_done, now(dve_done))
                        dve.tensor_tensor(opA[:, 1, j, t], hn[:, y % 2, :], opA[:, 0, j, t].bitcast(F32),
                                          ALU.subtract).then_inc(dve_done, 1)
                        step(dve_done, "lo", n, y)
                        names[("h_" + n, j, hf)] = names[("lo", n, y)]

            dve.wait_ge(dve_done, now(dve_done))
            dve.memset(vec_rows[:, 1:3, :], 0.0).then_inc(dve_done, 1)
            step(dve_done, "vec_zero")
            dve.wait_ge(pe_done, at("vec_T"))
            dve.wait_ge(dve_done, now(dve_done))
            dve.tensor_copy(cols[:, 0:P], PS[:, 7, 0:P]).then_inc(dve_done, 1)
            step(dve_done, "cols")

            def first_steps(g, ks):
                for kc in ks:
                    src = SILU_C + 8 * MODS[g][2] + kc
                    c = small[:, src:src + 1]
                    if kc == 0:
                        dve.wait_ge(first_mod_in[g][kc], at("first_mod_in", g, kc))
                        dve.wait_ge(act_done, at("silu_c"))
                        if g:
                            dve.wait_ge(pe_done, at("mod_sum", g - 1))
                        dve.wait_ge(dve_done, now(dve_done))
                        dve.tensor_scalar(mod_acc[:], first_mods[g][:, kc, :], c, None, ALU.mult).then_inc(dve_done, 1)
                        step(dve_done, "first_step", g, kc)
                    else:
                        dve.wait_ge(first_mod_in[g][kc], at("first_mod_in", g, kc))
                        dve.wait_ge(dve_done, now(dve_done))
                        dve.scalar_tensor_tensor(out=mod_acc[:], in0=first_mods[g][:, kc, :], scalar=c,
                                                 in1=mod_acc[:], op0=ALU.mult, op1=ALU.add).then_inc(dve_done, 1)
                        step(dve_done, "first_step", g, kc)

            first_steps(0, range(2))
            for j in range(KC):
                sq_add("a", j, 0)
                sq_add("a", j, 1)
                if j >= 2:
                    first_steps(0, range(j, j + 1))
            mod_out(0)
            dve.wait_ge(pe_done, at("vec_T2"))
            dve.wait_ge(dve_done, now(dve_done))
            dve.tensor_copy(cols[:, P:3 * P], PS[:, 7, P:3 * P]).then_inc(dve_done, 1)
            step(dve_done)
            for i in range(2):
                dve.wait_ge(vec_in[1], at("vec_in", 1))
                dve.wait_ge(dve_done, now(dve_done))
                dve.tensor_tensor(lam_rows[:, 512 + 64 * i:576 + 64 * i], lam_rows[:, 128 * i:128 * i + 64],
                                  lam_rows[:, 128 * i + 64:128 * i + 128], ALU.mult).then_inc(dve_done, 1)
                step(dve_done)
            dve.wait_ge(dve_done, now(dve_done))
            dve.reduce_sum(small[:, LAM:LAM + 2], lam_rows[:, 512:640].rearrange("p (i d) -> p i d", i=2), AX_X).then_inc(dve_done, 1)
            step(dve_done, "lam_sum")
            first_steps(1, range(KC))
            mod_out(1)
            parts("a", "a_norm_g", A_SCALE, None)
            dve.wait_ge(act_done, at("lam_exp"))
            dve.wait_ge(dve_done, now(dve_done))
            dve.scalar_tensor_tensor(out=small[:, LAMS:LAMS + 1], in0=small[:, LAM + 3:LAM + 4],
                                     scalar=-LAM_INIT, in1=small[:, LAM + 2:LAM + 3], op0=ALU.add,
                                     op1=ALU.subtract).then_inc(dve_done, 1)
            step(dve_done)
            dve.wait_ge(dve_done, now(dve_done))
            dve.tensor_scalar(small[:, NSINK:NSINK + 8], small[:, SINK:SINK + 8], -1.0, None, ALU.mult).then_inc(dve_done, 1)
            step(dve_done)
            dve.wait_ge(dve_done, now(dve_done))
            dve.tensor_scalar(small[:, SUBG:SUBG + 1], cols[:, C["diff_subln_g_2"]:C["diff_subln_g_2"] + 1],
                              1.0 - LAM_INIT, None, ALU.mult).then_inc(dve_done, 1)
            step(dve_done)
            cw = C["a_conv_w"]

            def conv(src, w, j, kc, hf, bias_col, name):
                t0 = hf * HALF
                b = None if bias_col is None else cols[:, bias_col:bias_col + 1]
                o = yt[:, hf, :]
                w_of = lambda tap: cols[:, w + tap * kc + j:w + tap * kc + j + 1]
                if b is None:
                    dve.wait_ge(dve_done, now(dve_done))
                    dve.tensor_scalar(o, src[:, t0:t0 + HALF], w_of(2), None, ALU.mult).then_inc(dve_done, 1)
                    step(dve_done)
                else:
                    dve.wait_ge(dve_done, now(dve_done))
                    dve.tensor_scalar(o, src[:, t0:t0 + HALF], w_of(2), b, ALU.mult, ALU.add).then_inc(dve_done, 1)
                    step(dve_done)
                for tap, back in ((1, 1), (0, 2)):
                    lo = max(0, back - t0)
                    dve.wait_ge(dve_done, now(dve_done))
                    dve.scalar_tensor_tensor(out=o[:, lo:], in0=src[:, t0 + lo - back:t0 + HALF - back],
                                             scalar=w_of(tap), in1=o[:, lo:], op0=ALU.mult, op1=ALU.add).then_inc(dve_done, 1)
                    step(dve_done, *(name or ()))

            for j in range(KC):
                u = U_AIN + 4 * j
                mod_unit(u)
                mod_unit(u + 1)
                for hf in range(2):
                    t = slice(hf * HALF, (hf + 1) * HALF)
                    dve.wait_ge(pe_done, at("unit", u + 1, 1))
                    dve.wait_ge(act_done, at("cs", j, hf))
                    dve.wait_ge(dve_done, now(dve_done))
                    dve.tensor_tensor(M[0][:, t], cs[:, hf, :], PS[:, 2 * ((u + 1) % 2) + hf, :], ALU.mult).then_inc(dve_done, 1)
                    step(dve_done, "cu", j, hf)
                names[("free", u + 1)] = names[("cu", j, 1)]
                for hf in range(2):
                    if j:
                        dve.wait_ge(act_done, at("yh", j - 1, hf))
                    conv(M[0], cw, j, KC, hf, None, None)
                mod_unit(u + 2)
                for hf in range(2):
                    dve.wait_ge(pe_done, at("unit", u + 2, 1))
                    dve.wait_ge(dve_done, now(dve_done))
                    dve.tensor_tensor(yt[:, hf, :], yt[:, hf, :], PS[:, 2 * ((u + 2) % 2) + hf, :], ALU.mult).then_inc(dve_done, 1)
                    step(dve_done)
                did_free = now(dve_done)
                names[("free", u + 2)] = did_free
                mod_unit(u + 3)
                for hf in range(2):
                    dve.wait_ge(act_done, at("sz", j, hf))
                    dve.wait_ge(dve_done, now(dve_done))
                    dve.tensor_tensor(yt[:, hf, :], yt[:, hf, :], cs[:, hf, :], ALU.mult).then_inc(dve_done, 1)
                    step(dve_done, "yz", j, hf)
                for hf in range(2):
                    t = slice(hf * HALF, (hf + 1) * HALF)
                    dve.wait_ge(act_done, at("yh", j, hf))
                    dve.wait_ge(dve_done, now(dve_done))
                    dve.tensor_tensor(opB[:, 1, j, t], yt[:, hf, :], opB[:, 0, j, t].bitcast(F32),
                                      ALU.subtract).then_inc(dve_done, 1)
                    step(dve_done, "y", j, hf)
                    names[("h_y", j, hf)] = names[("y", j, hf)]

            def residual(n, u, gate, j, hf, back=None):
                t = slice(hf * HALF, (hf + 1) * HALF)
                dve.wait_ge(pe_done, at("unit", u, hf))
                if back is not None:
                    dve.wait_ge(x_back[j], at("x_back", back, j))
                dve.wait_ge(dve_done, now(dve_done))
                dve.scalar_tensor_tensor(out=X[:, j, t], in0=PS[:, 2 * (u % 2) + hf, :],
                                         scalar=mod[:, gate, j:j + 1], in1=X[:, j, t], op0=ALU.mult,
                                         op1=ALU.add).then_inc(dve_done, 1)
                step(dve_done, "x_new", n, j, hf)
                if hf:
                    names[("free", u)] = names[("x_new", n, j, 1)]

            def residuals(n, u0, gate, back=None, sums=True):
                norms = (("fin1", "n1") if n == "fin1" else (n,)) if sums else ()
                for j in range(KC):
                    mod_unit(u0 + j)
                    residual(n, u0 + j, gate, j, 0, back)
                    for m in norms:
                        if j:
                            sq_add(m, j - 1, 0)
                            sq_add(m, j - 1, 1)
                        if j == KC - 1:
                            sq_add(m, j, 0)
                    residual(n, u0 + j, gate, j, 1, back)
                for m in norms:
                    sq_add(m, KC - 1, 1)

            residuals("kv", U_AOUT, A_GATE)
            parts("kv", "kv_norm_g", KV_SCALE, U_AOUT - 1)

            def hl_lo(u, x, scale):
                s = u % 2
                dve.wait_ge(act_done, at("hl_hi", u))
                dve.wait_ge(dve_done, now(dve_done))
                dve.scalar_tensor_tensor(out=stage[:, x % 2, 1, :], in0=banks(2 * s),
                                         scalar=scale, in1=stage[:, x % 2, 0, :].bitcast(F32), op0=ALU.mult,
                                         op1=ALU.subtract).then_inc(dve_done, 1)
                step(dve_done, "hl_lo", u)
                names[("free", u)] = names[("hl_lo", u)]

            def v_lo(u, x, kind):
                s = u % 2
                src = PS[:, 4:6, :].rearrange("p b (k e d) -> p (b k) e d", k=4, e=2)
                if kind in ("stick", "swa"):
                    for e in range(2):
                        place = 0 if kind == "swa" else e
                        v = vstage[:, s, e, :].rearrange("p (k s d) -> p k s d", k=NT, s=2)
                        dve.wait_ge(act_done, at("v_hi", u))
                        dve.wait_ge(dve_done, now(dve_done))
                        dve.tensor_tensor(v[:, :, 1 - place, :], src[:, :, e, :], v[:, :, place, :].bitcast(F32),
                                          ALU.subtract).then_inc(dve_done, 1)
                        step(dve_done, "v_split", u)
                else:
                    dve.wait_ge(act_done, at("v_hi", u))
                    dve.wait_ge(dve_done, now(dve_done))
                    dve.tensor_tensor(vstage[:, s, 1, :], banks(4),
                                      vstage[:, s, 0, :].bitcast(F32), ALU.subtract).then_inc(dve_done, 1)
                    step(dve_done, "v_split", u)

            for n in range(KC):
                mod_unit(U_KV + n)
                hl_lo(U_KV + n, n, 1.0)
            mod_unit(U_KV + KC)
            for n in range(KC - 1):
                if n == 1:
                    mod_unit(U_KV + KC + 1)
                v_lo(U_KV + KC + n, n, "stick")
            parts("b", "b_norm_g", B_SCALE, U_QZ - 1)
            names[("x_free", 0)] = now(dve_done)
            for n in range(KC):
                hl_lo(U_QZ + n, n, QSCALE)
            stick_dve(dve)
            residuals("fin1", U_BOUT, B_GATE, 0)

            def scale_x(n, gname, j, hf):
                t = slice(hf * HALF, (hf + 1) * HALF)
                c = C[gname] + j
                dve.wait_ge(act_done, at("rstd", n, hf))
                dve.wait_ge(dve_done, now(dve_done))
                dve.scalar_tensor_tensor(out=X[:, j, t], in0=X[:, j, t], scalar=cols[:, c:c + 1],
                                         in1=M[1][:, t], op0=ALU.mult, op1=ALU.mult).then_inc(dve_done, 1)
                step(dve_done, "x_" + n, j, hf)

            parts("n1", "norm1_g_2", SCALE1, U_IN2 - 1)
            for n in range(13):
                hl_lo(U_IN2 + n, n, -QSCALE if n < 8 else 1.0)
                if n < KC:
                    scale_x("fin1", "final_norm_g", n, 0)
                    scale_x("fin1", "final_norm_g", n, 1)
                    names[("x_free", 1)] = now(dve_done)
            for n in range(5):
                v_lo(U_IN2 + 13 + n, n, "diff" if n else "swa")
            second_dve(dve)
            for n in range(KC):
                u = U_BRANCH + n
                s = u % 2
                for hf in range(2):
                    t = slice(hf * HALF, (hf + 1) * HALF)
                    dve.wait_ge(pe_done, at("unit", u, 1))
                    if n:
                        dve.wait_ge(act_done, at("mh", n - 1, hf))
                    dve.wait_ge(dve_done, now(dve_done))
                    dve.tensor_tensor(d_o[:, hf, :], gates[:, n, t], PS[:, 2 * s + hf, :], ALU.mult).then_inc(dve_done, 1)
                    step(dve_done)
                    dve.wait_ge(pe_done, at("sec_pv", len(PIECES) - 2))
                    dve.wait_ge(dve_done, now(dve_done))
                    dve.tensor_tensor(M[4 - 1][:, t], gates[:, KC + n, t], PS[:, 4 + 2 * s + hf, :], ALU.mult).then_inc(dve_done, 1)
                    step(dve_done)
                names[("free", u)] = now(dve_done)
                for hf in range(2):
                    t = slice(hf * HALF, (hf + 1) * HALF)
                    dve.wait_ge(dve_done, now(dve_done))
                    dve.tensor_tensor(d_o[:, hf, :], d_o[:, hf, :], M[3][:, t], ALU.add).then_inc(dve_done, 1)
                    step(dve_done, "mz", n, hf)
                for hf in range(2):
                    t = slice(hf * HALF, (hf + 1) * HALF)
                    dve.wait_ge(act_done, at("mh", n, hf))
                    dve.wait_ge(dve_done, now(dve_done))
                    dve.tensor_tensor(opB[:, 1, n, t], d_o[:, hf, :], opB[:, 0, n, t].bitcast(F32),
                                      ALU.subtract).then_inc(dve_done, 1)
                    step(dve_done, "merged", n, hf)
                    names[("h_merged", n, hf)] = names[("merged", n, hf)]
            residuals("n2", U_OUT2, GATE1, 1)
            parts("n2", "norm2_g_2", SCALE2, U_IN2 + 33)
            u = U_FFN
            for gi, (first, many) in enumerate(FGROUPS):
                for f in range(first, first + many):
                    for hf in range(2):
                        dve.wait_ge(act_done, at("fa", f, 1))
                        if f:
                            dve.wait_ge(act_done, at("fh", f - 1, hf))
                        conv(M[0], C["conv_w_2"], f, FC, hf, C["conv_b_2"] + f, ("fconv", f, hf))
                    for hf in range(2):
                        dve.wait_ge(act_done, at("fg", f, hf))
                        dve.wait_ge(pe_done, at("unit", u + 1, 1))
                        dve.wait_ge(dve_done, now(dve_done))
                        dve.tensor_tensor(yt[:, hf, :], yt[:, hf, :], PS[:, 2 * ((u + 1) % 2) + hf, :], ALU.mult).then_inc(dve_done, 1)
                        step(dve_done, "fz", f, hf)
                    names[("free", u + 1)] = names[("fz", f, 1)]
                    for hf in range(2):
                        t = slice(hf * HALF, (hf + 1) * HALF)
                        dve.wait_ge(act_done, at("fh", f, hf))
                        dve.wait_ge(dve_done, now(dve_done))
                        dve.tensor_tensor(opB[:, 1, f - first, t], yt[:, hf, :],
                                          opB[:, 0, f - first, t].bitcast(F32), ALU.subtract).then_inc(dve_done, 1)
                        step(dve_done, "ff", f, hf)
                        names[(f"h_ff{first}", f - first, hf)] = names[("ff", f, hf)]
                    u += 2
                end = gi == len(FGROUPS) - 1
                residuals("fin2" if end else ("g", gi), u, GATE2, None, sums=end)
                u += KC
            for hf in range(2):
                for j in range(KC):
                    scale_x("fin2", "final_g_2", j, hf)

    return names


def kernel(**inputs):
    import concourse.bacc as bacc
    from concourse.bass_utils import run_bass_kernel_spmd

    arrays = {f"in_{k}": np.ascontiguousarray(v) for k, v in inputs.items()}
    known = {}
    for _ in range(2):
        nc = bacc.Bacc("TRN2", target_bir_lowering=False, num_devices=1)
        args = {k[3:]: nc.dram_tensor(k, list(v.shape), F32, kind="ExternalInput").ap() for k, v in arrays.items()}
        out = nc.dram_tensor("out_0", [1, T, D], F32, kind="ExternalOutput").ap()
        known = program(nc, args, out, known)
    r = run_bass_kernel_spmd(nc, [arrays], core_ids=[0])
    return r.results[0]["out_0"]
```
